# Optimizing a Trainium2 kernel written in Bass

```python
import jax
import jax.numpy as jnp
from jax import lax
import numpy as np

D_MODEL = 1024
BATCH = 1
SEQ = 1024
DEPTH = 2
DEC_BATCH = 1
DEC_SEQ = 32
PAST_LEN = 512

CHUNK = 64
HEAD_DIM = 64
HQ_A = 8
HKV_A = 2
G_A = HQ_A // HKV_A
WINDOW_A = 128
NPREV_A = WINDOW_A // CHUNK
H_B = 4
DH_B = 128
CONV_W = 4
H_C = 16
NPREV_C = 8
MAX_REL_C = 256
D_FF = ((8 * D_MODEL + 3 * 256 - 1) // (3 * 256)) * 256
EPS = 1e-6
NEG = -1e30
N_AB = (DEPTH + 1) // 2
N_C = DEPTH // 2
W_A = HQ_A * HEAD_DIM
KV_A = HKV_A * HEAD_DIM
W_B = H_B * DH_B
W_C = H_C * HEAD_DIM
SPLIT_AB = [W_A, W_A + KV_A, W_A + 2 * KV_A, W_A + 2 * KV_A + 2 * W_B, W_A + 2 * KV_A + 3 * W_B,
            W_A + 2 * KV_A + 3 * W_B + H_B, W_A + 2 * KV_A + 3 * W_B + 2 * H_B]
P_AB = W_A + 2 * KV_A + 3 * W_B + 2 * H_B + W_B

kernel_name = 'hybrid_streaming_encoder_step'

def rmsnorm(x, g):
    xf = x.astype(jnp.float32)
    y = xf * lax.rsqrt(jnp.mean(xf * xf, axis=-1, keepdims=True) + EPS)
    return (y * g.astype(jnp.float32)).astype(x.dtype)

def alibi_slopes():
    h = jnp.arange(1, HQ_A + 1, dtype=jnp.float32)
    return jnp.exp2(-8.0 * h / HQ_A).reshape(HKV_A, G_A)

def alibi_bias(slopes, q_pos, k_pos):
    dist = jnp.abs(q_pos[:, None] - k_pos[None, :]).astype(jnp.float32)
    return -slopes[:, :, None, None] * dist

def relpos_bias(table, q_pos, k_pos):
    rel = jnp.clip(q_pos[:, None] - k_pos[None, :], -MAX_REL_C, MAX_REL_C) + MAX_REL_C
    return table.astype(jnp.float32)[:, rel][:, None]

def attend(q, k, v, bias, valid, sinks):
    B, Lq, Hkv, G, d = q.shape
    s = jnp.einsum('bqhgd,bkhd->bhgqk', q, k).astype(jnp.float32) * (d ** -0.5) + bias
    if valid is not None:
        s = jnp.where(valid, s, NEG)
    if sinks is None:
        p = jax.nn.softmax(s, axis=-1)
    else:
        sk = sinks.astype(jnp.float32)[None, :, :, None]
        m = jnp.maximum(s.max(axis=-1), sk)
        p = jnp.exp(s - m[..., None])
        p = p / (p.sum(axis=-1, keepdims=True) + jnp.exp(sk - m)[..., None])
    o = jnp.einsum('bhgqk,bkhd->bqhgd', p.astype(v.dtype), v)
    return o.reshape(B, Lq, Hkv * G * d)

def band_attention_prompt(q, k, v, n_prev, bias_fn, sinks):
    B, S = q.shape[:2]
    nc = S // CHUNK
    pad = n_prev * CHUNK
    band = pad + CHUNK
    kp = jnp.pad(k, ((0, 0), (pad, 0), (0, 0), (0, 0)))
    vp = jnp.pad(v, ((0, 0), (pad, 0), (0, 0), (0, 0)))
    qc = jnp.moveaxis(q.reshape((B, nc, CHUNK) + q.shape[2:]), 1, 0)

    def one_chunk(args):
        c, q_c = args
        start = c * CHUNK
        k_b = lax.dynamic_slice_in_dim(kp, start, band, axis=1)
        v_b = lax.dynamic_slice_in_dim(vp, start, band, axis=1)
        q_pos = start + jnp.arange(CHUNK)
        k_pos = start - pad + jnp.arange(band)
        valid = (k_pos >= 0)[None, :]
        return attend(q_c, k_b, v_b, bias_fn(q_pos, k_pos), valid, sinks)

    out = lax.map(one_chunk, (jnp.arange(nc), qc))
    return jnp.moveaxis(out, 0, 1).reshape(B, S, -1)

def causal_conv(u, buf, w, b):
    T = u.shape[1]
    up = jnp.concatenate([buf.astype(u.dtype), u], axis=1)
    y = up[:, 0:T] * w[0]
    for j in range(1, CONV_W):
        y = y + up[:, j:j + T] * w[j]
    return jax.nn.silu(y + b), up[:, -(CONV_W - 1):]

def mlstm_chunk(state, q, k, v, logi, logf):
    C, n, m = state
    L = q.shape[2]
    b = jnp.cumsum(logf, axis=-1)
    causal = jnp.tril(jnp.ones((L, L), dtype=bool))
    logD = jnp.where(causal, b[..., :, None] - b[..., None, :] + logi[..., None, :], -jnp.inf)
    inter = b + m[..., None]
    m_t = jnp.maximum(inter, logD.max(axis=-1))
    a = jnp.exp(inter - m_t)
    w = jnp.einsum('bhtd,bhsd->bhts', q, k) * jnp.exp(logD - m_t[..., None])
    num = a[..., None] * jnp.einsum('bhvk,bhtk->bhtv', C, q) + jnp.einsum('bhts,bhsv->bhtv', w, v)
    den = a * jnp.einsum('bhk,bhtk->bht', n, q) + w.sum(axis=-1)
    h = num / jnp.maximum(jnp.abs(den), jnp.exp(-m_t))[..., None]
    bL = b[..., -1]
    logw_end = bL[..., None] - b + logi
    m_new = jnp.maximum(bL + m, logw_end.max(axis=-1))
    a_end = jnp.exp(bL + m - m_new)
    w_end = jnp.exp(logw_end - m_new[..., None])
    C_new = a_end[..., None, None] * C + jnp.einsum('bhs,bhsv,bhsk->bhvk', w_end, v, k)
    n_new = a_end[..., None] * n + jnp.einsum('bhs,bhsk->bhk', w_end, k)
    return (C_new, n_new, m_new), h

def mixer_ab(h, j, W, cache):
    B, T, _ = h.shape
    f32 = jnp.float32
    qa, ka, va, qkb, vb, ig, fg, og = jnp.split(h @ W['w_in_ab'][j], SPLIT_AB, axis=-1)
    qa = qa.reshape(B, T, HKV_A, G_A, HEAD_DIM)
    ka = ka.reshape(B, T, HKV_A, HEAD_DIM)
    va = va.reshape(B, T, HKV_A, HEAD_DIM)
    slopes = alibi_slopes()
    sinks = W['sink_a'][j].reshape(HKV_A, G_A)
    bias_fn = lambda qp, kp: alibi_bias(slopes, qp, kp)
    if cache is None:
        out_a = band_attention_prompt(qa, ka, va, NPREV_A, bias_fn, sinks)
        new_k, new_v = ka[:, -WINDOW_A:], va[:, -WINDOW_A:]
        conv_buf = jnp.zeros((B, CONV_W - 1, 2 * W_B), h.dtype)
        state = (jnp.zeros((B, H_B, DH_B, DH_B), f32), jnp.zeros((B, H_B, DH_B), f32), jnp.zeros((B, H_B), f32))
    else:
        ck, cv, s_c, s_n, s_m, conv_buf = cache
        lc = ck.shape[1]
        k_all = jnp.concatenate([ck.astype(ka.dtype), ka], axis=1)
        v_all = jnp.concatenate([cv.astype(va.dtype), va], axis=1)
        q_pos = PAST_LEN + jnp.arange(T)
        k_pos = PAST_LEN - lc + jnp.arange(lc + T)
        out_a = attend(qa, k_all, v_all, bias_fn(q_pos, k_pos), None, sinks)
        new_k, new_v = ka, va
        state = (s_c.astype(f32), s_n.astype(f32), s_m.astype(f32))
    qk_c, conv_new = causal_conv(qkb, conv_buf, W['conv_w_b'][j], W['conv_b_b'][j])
    heads = lambda a: a.reshape(B, T, H_B, DH_B).transpose(0, 2, 1, 3).astype(f32)
    qb = heads(qk_c[..., :W_B])
    kb = heads(qk_c[..., W_B:]) * (DH_B ** -0.5)
    vh = heads(vb)
    bg = W['b_gates_b'][j].astype(f32)
    logi = (ig.astype(f32) + bg[:H_B]).transpose(0, 2, 1)
    logf = jax.nn.log_sigmoid(fg.astype(f32) + bg[H_B:]).transpose(0, 2, 1)
    if cache is None:
        nc = T // CHUNK
        to_chunks = lambda a: jnp.moveaxis(a.reshape(a.shape[:2] + (nc, CHUNK) + a.shape[3:]), 2, 0)
        xs = tuple(to_chunks(a) for a in (qb, kb, vh, logi, logf))
        state, hs = lax.scan(lambda st, x_c: mlstm_chunk(st, *x_c), state, xs)
        hb = jnp.moveaxis(hs, 0, 2).reshape(B, H_B, T, DH_B)
    else:
        state, hb = mlstm_chunk(state, qb, kb, vh, logi, logf)
    hb = hb.transpose(0, 2, 1, 3)
    hb = hb * lax.rsqrt(jnp.mean(hb * hb, axis=-1, keepdims=True) + EPS) * W['hnorm_b'][j].astype(f32).reshape(H_B, DH_B)
    hb = jax.nn.sigmoid(og.astype(f32)) * hb.reshape(B, T, W_B)
    out = jnp.concatenate([out_a, hb.astype(h.dtype)], axis=-1) @ W['w_out_ab'][j]
    return out, (new_k, new_v) + state + (conv_new,)

def mixer_c(h, j, W, cache):
    B, T, _ = h.shape
    q, k, v = jnp.split(h @ W['w_in_c'][j], 3, axis=-1)
    q = q.reshape(B, T, H_C, 1, HEAD_DIM)
    k = k.reshape(B, T, H_C, HEAD_DIM)
    v = v.reshape(B, T, H_C, HEAD_DIM)
    table = W['relbias_c'][j]
    bias_fn = lambda qp, kp: relpos_bias(table, qp, kp)
    if cache is None:
        out = band_attention_prompt(q, k, v, NPREV_C, bias_fn, None)
        new_k, new_v = k[:, -NPREV_C * CHUNK:], v[:, -NPREV_C * CHUNK:]
    else:
        ck, cv = cache
        lc = ck.shape[1]
        k_all = jnp.concatenate([ck.astype(k.dtype), k], axis=1)
        v_all = jnp.concatenate([cv.astype(v.dtype), v], axis=1)
        q_pos = PAST_LEN + jnp.arange(T)
        k_pos = PAST_LEN - lc + jnp.arange(lc + T)
        out = attend(q, k_all, v_all, bias_fn(q_pos, k_pos), None, None)
        new_k, new_v = k, v
    return out @ W['w_out_c'][j], (new_k, new_v)

def swiglu(h, i, W):
    return (jax.nn.silu(h @ W['w_ffn_gate'][i]) * (h @ W['w_ffn_up'][i])) @ W['w_ffn_down'][i]

def trunk(x, c, caches, W):
    ab_states, c_states = [], []
    for i in range(DEPTH):
        mod = jax.nn.silu(c) @ W['w_ada'][i] + W['b_ada'][i]
        sh1, sc1, gt1, sh2, sc2, gt2 = [m[:, None, :] for m in jnp.split(mod, 6, axis=-1)]
        g = W['norm_g'][i]
        h = rmsnorm(x, g[0]) * (1 + sc1) + sh1
        j = i // 2
        if i % 2 == 0:
            cache = None if caches is None else tuple(a[j] for a in caches[:6])
            y, st = mixer_ab(h, j, W, cache)
            ab_states.append(st)
        else:
            cache = None if caches is None else tuple(a[j] for a in caches[6:])
            y, st = mixer_c(h, j, W, cache)
            c_states.append(st)
        x = x + gt1 * rmsnorm(y, g[1])
        h = rmsnorm(x, g[2]) * (1 + sc2) + sh2
        x = x + gt2 * rmsnorm(swiglu(h, i, W), g[3])
    stack = lambda sts: tuple(jnp.stack(s) for s in zip(*sts))
    return x, stack(ab_states) + stack(c_states)

def setup_inputs(seed: int = 0) -> dict:
    key = jax.random.key(seed)
    keys = iter(jax.random.split(key, 40))

    def nrm(shape, scale):
        return jax.random.normal(next(keys), shape, jnp.float32) * scale

    d = D_MODEL
    la = min(WINDOW_A, PAST_LEN)
    lc = min(NPREV_C * CHUNK, PAST_LEN)
    return {
        'x_prompt': nrm((BATCH, SEQ, d), 1.0),
        'x_sample': nrm((DEC_BATCH, DEC_SEQ, d), 1.0),
        'cache_a_k': nrm((N_AB, DEC_BATCH, la, HKV_A, HEAD_DIM), 1.0),
        'cache_a_v': nrm((N_AB, DEC_BATCH, la, HKV_A, HEAD_DIM), 1.0),
        'state_b_c': nrm((N_AB, DEC_BATCH, H_B, DH_B, DH_B), 0.3),
        'state_b_n': nrm((N_AB, DEC_BATCH, H_B, DH_B), 0.3),
        'state_b_m': nrm((N_AB, DEC_BATCH, H_B), 0.5),
        'state_b_conv': nrm((N_AB, DEC_BATCH, CONV_W - 1, 2 * W_B), 1.0),
        'cache_c_k': nrm((N_C, DEC_BATCH, lc, H_C, HEAD_DIM), 1.0),
        'cache_c_v': nrm((N_C, DEC_BATCH, lc, H_C, HEAD_DIM), 1.0),
        'c_prompt': nrm((BATCH, d), 1.0),
        'c_sample': nrm((DEC_BATCH, d), 1.0),
        'w_in_ab': nrm((N_AB, d, P_AB), d ** -0.5),
        'sink_a': nrm((N_AB, HQ_A), 0.5),
        'conv_w_b': nrm((N_AB, CONV_W, 2 * W_B), CONV_W ** -0.5),
        'conv_b_b': nrm((N_AB, 2 * W_B), 0.02),
        'b_gates_b': jnp.concatenate([nrm((N_AB, H_B), 0.1), 3.0 + nrm((N_AB, H_B), 0.5)], axis=-1),
        'hnorm_b': 1.0 + nrm((N_AB, W_B), 0.1),
        'w_out_ab': nrm((N_AB, W_A + W_B, d), (W_A + W_B) ** -0.5),
        'w_in_c': nrm((N_C, d, 3 * W_C), d ** -0.5),
        'relbias_c': nrm((N_C, H_C, 2 * MAX_REL_C + 1), 0.5),
        'w_out_c': nrm((N_C, W_C, d), W_C ** -0.5),
        'w_ada': nrm((DEPTH, d, 6 * d), 0.5 * d ** -0.5),
        'b_ada': nrm((DEPTH, 6 * d), 0.02),
        'norm_g': 1.0 + nrm((DEPTH, 4, d), 0.1),
        'w_ffn_gate': nrm((DEPTH, d, D_FF), d ** -0.5),
        'w_ffn_up': nrm((DEPTH, d, D_FF), d ** -0.5),
        'w_ffn_down': nrm((DEPTH, D_FF, d), D_FF ** -0.5),
    }

def reference(x_prompt, x_sample, cache_a_k, cache_a_v, state_b_c, state_b_n, state_b_m, state_b_conv,
              cache_c_k, cache_c_v, c_prompt, c_sample, w_in_ab, sink_a, conv_w_b, conv_b_b, b_gates_b,
              hnorm_b, w_out_ab, w_in_c, relbias_c, w_out_c, w_ada, b_ada, norm_g, w_ffn_gate, w_ffn_up,
              w_ffn_down):
    W = dict(w_in_ab=w_in_ab, sink_a=sink_a, conv_w_b=conv_w_b, conv_b_b=conv_b_b, b_gates_b=b_gates_b,
             hnorm_b=hnorm_b, w_out_ab=w_out_ab, w_in_c=w_in_c, relbias_c=relbias_c, w_out_c=w_out_c,
             w_ada=w_ada, b_ada=b_ada, norm_g=norm_g, w_ffn_gate=w_ffn_gate, w_ffn_up=w_ffn_up,
             w_ffn_down=w_ffn_down)
    y_prompt, sp = trunk(x_prompt, c_prompt, None, W)
    caches = (cache_a_k, cache_a_v, state_b_c, state_b_n, state_b_m, state_b_conv, cache_c_k, cache_c_v)
    y_sample, ss = trunk(x_sample, c_sample, caches, W)
    pa_k, pa_v, pb_c, pb_n, pb_m, pb_conv, pc_k, pc_v = sp
    sa_k, sa_v, sb_c, sb_n, sb_m, sb_conv, sc_k, sc_v = ss
    return (y_prompt, y_sample, pa_k, pa_v, pb_c, pb_n, pb_m, pb_conv, pc_k, pc_v,
            sa_k, sa_v, sb_c, sb_n, sb_m, sb_conv, sc_k, sc_v)


_drawn_inputs = setup_inputs


def setup_inputs(seed=0):
    import zlib

    import numpy as np

    out = dict(_drawn_inputs(seed))
    spreads = {}
    factors = {'sink_a': 8.0}
    for name, (base, spread) in spreads.items():
        noise = np.random.default_rng([zlib.crc32(name.encode()), seed]).standard_normal(out[name].shape)
        drawn = base * np.exp(spread * noise) if base else spread * noise
        out[name] = jnp.asarray(drawn.astype(out[name].dtype))
    for name, factor in factors.items():
        out[name] = (out[name] * factor).astype(out[name].dtype)
    return out
```

```python
import concourse.bass as bass
from concourse import mybir
from contextlib import ExitStack
import numpy as np

F32 = mybir.dt.float32
F32R = mybir.dt.float32r
ALU = mybir.AluOpType
ACT = mybir.ActivationFunctionType

D = 1024
TP, TS = 1024, 32
T = TP + TS
KD = D // 128
NTT = 3
TW = T // NTT
NBLK = TP // 128
HQ_A, HKV_A, HD = 8, 2, 64
H_B, DH_B = 4, 128
H_C = 16
W_A = HQ_A * HD
W_B = H_B * DH_B
COL_KA, COL_VA = W_A, W_A + 128
COL_QKB = W_A + 256
COL_VB = COL_QKB + 2 * W_B
COL_IG = COL_VB + W_B
COL_FG = COL_IG + H_B
COL_OG = COL_FG + H_B
D_FF = 2816
FF_GROUPS = [5, 5, 4, 4, 4]
PREV_C = 512
MAX_REL = 256
EPS = 1e-6
BIG = 1e30
QSCALE = -(HD ** -0.5)
KSCALE = DH_B ** -0.5
REV = 768
CONV_W = 4
DMA_RING = 2048
UW = 3 + TP + 3 + TS
CW = UW - 3

BW = {"A": 256, "C": 640}
CREDIT = 3


def tile_plan():
    plan, g, a, d = {}, 0, 0, 0

    def add(name, n, by):
        nonlocal g, a, d
        plan[name] = (g, n, a, d)
        g += n
        a += 3 * n if by == "act" else 3 * (n // 2) if by == "both" else 0
        d += 3 * n if by == "dve" else 3 * (n // 2) if by == "both" else 0

    for layer in range(2):
        if layer == 0:
            add("kv", 2, "act")
            add("qa", 4, "act")
            add("gates", 1, "act")
            add("heads", 4 * H_B, "act")
        else:
            add("qkv", 3 * KD, "act")
        add(f"out{layer}", KD, "act")
        for n, ff in enumerate(FF_GROUPS):
            add(f"gu{layer}{n}", 2 * ff, "both")
            add(f"down{layer}{n}", KD, "dve")
    return plan, g


def build(nc, ins, outs):
    I, O = ins, outs
    plan, TILES = tile_plan()
    ctx = ExitStack()
    with ctx:
        def at(name, shape, offset, dt=F32):
            return nc.alloc_sbuf_tensor_at(name, shape, dt, offset=offset)

        HB_ = KD * T * 4
        B0 = (nc.sbuf_base + 31) // 32 * 32
        h_hi = at("h_hi", [128, KD, T], B0, F32R)
        h_lo = at("h_lo", [128, KD, T], B0 + HB_, F32R)
        y_mix = at("y_mix", [128, KD, T], B0)
        R1 = B0 + 2 * HB_
        FFM = max(FF_GROUPS)
        ff_hi = at("ff_hi", [128, FFM, T], R1, F32R)
        ff_lo = at("ff_lo", [128, FFM, T], R1 + FFM * T * 4, F32R)
        norm_buf = at("norm_buf", [128, NTT, KD, TW], R1)
        o_hi = at("o_hi", [128, KD, T], R1, F32R)
        o_lo = at("o_lo", [128, KD, T], R1 + HB_, F32R)
        YF = R1 + 6 * T * 4 * 2
        y_ffn = at("y_ffn", [128, KD, T], YF)
        x = at("x", [128, KD, T], YF + HB_)
        XE = YF + 2 * HB_
        w_raw = at("w_raw", [128, 2, KD, 128], XE)
        w_hi = at("w_hi", [128, 2, KD, 128], XE + 8192, F32R)
        w_lo = at("w_lo", [128, 2, KD, 128], XE + 16384, F32R)
        SM = XE + 24576
        top = [SM]

        def small(name, shape, dt=F32):
            n = 4 * int(np.prod(shape[1:]))
            t = at(name, shape, top[0], dt)
            top[0] += (n + 31) // 32 * 32
            assert top[0] <= 229368, (name, top[0])
            return t

        ident = small("ident", [128, 128])
        ones = small("ones", [128, 128])
        prm = small("prm", [128, 128])
        prm2 = small("prm2", [128, 120])
        silu_c = small("silu_c", [128, KD, 2])
        mod = small("mod", [128, 12, KD, 2])
        pre_scale = small("pre_scale", [128, 4, KD, 2])
        post_gate = small("post_gate", [128, 4, KD, 2])
        mins = small("mins", [128, 6])
        sums = small("sums", [128, 6])
        rsum = small("rsum", [128, 6])
        neg_sink = small("neg_sink", [128, HQ_A])
        sink2 = small("sink2", [128, 2])
        sink_e = small("sink_e", [128, 6])
        F0 = top[0]
        sil = at("sil", [128, T], F0)
        ffs = at("ffs", [128, T], F0 + 4 * T)
        rstd = at("rstd", [128, NTT, TW], F0 + 8 * T)
        conv_t = at("conv_t", [128, CW], F0)
        assert F0 + 12 * T <= 229368, F0
        ada_row = at("ada_row", [2, 4, 256], F0)

        MX = R1 + 2 * HB_
        mx = [MX]

        def scratch(name, shape, dt=F32):
            n = 4 * int(np.prod(shape[1:]))
            t = at(name, shape, mx[0], dt)
            mx[0] += (n + 31) // 32 * 32
            assert mx[0] <= XE, (name, mx[0] - XE)
            return t

        neg_bias = scratch("neg_bias", [128, 2, 640])
        probs_a = at("probs_a", [128, 3, 256], mx[0])
        probs = scratch("probs", [128, 2, 640])
        probs_t = scratch("probs_t", [128, 2, 5, 128])
        o_tok = scratch("o_tok", [128, NBLK + 1, 128])
        v_tok = scratch("v_tok", [128, NBLK + 2, 128])
        k_out = scratch("k_out", [128, 5, 128])
        mark = mx[0]
        q_c = [scratch("q_c0", [128, T]), at("q_c1", [128, T], F0)]
        k_c = [scratch("k_c0", [128, T]), at("k_c1", [128, T], F0 + 4 * T)]
        v_c = [scratch("v_c0", [128, T]), at("v_c1", [128, T], F0 + 8 * T)]
        cache_kt = scratch("cache_kt", [128, 512])
        cache_k = [scratch(f"cache_k{p}", [128, 4, 128]) for p in range(2)]
        cache_v = [scratch(f"cache_v{p}", [128, 4, 128]) for p in range(2)]
        mx[0] = mark
        q_a = scratch("q_a", [128, T])
        k_a = scratch("k_a", [128, T])
        v_a = scratch("v_a", [128, T])
        cache_ak = scratch("cache_ak", [128, 128])
        cache_akt = scratch("cache_akt", [128, 128])
        mx[0] = MX
        u_in = [scratch("u_q", [128, UW]), scratch("u_k", [128, UW])]
        qk_b = [scratch("q_b", [128, T]), scratch("k_b", [128, T])]
        v_b = scratch("v_b", [128, T])
        og_b = scratch("og_b", [128, T])
        SELW = 2 * T + NBLK + 1
        brd = scratch("brd", [4, SELW])
        nm_h = at("nm_h", [4, T], R1 + HB_ + 7 * T * 4)
        a_h = at("a_h", [4, T], R1 + 7 * T * 4)
        h_tok = scratch("h_tok", [128, NBLK + 1, 128])
        qa_b = at("qa_b", [128, T], F0 + 8 * T)
        ot_f = conv_t
        FB = F0 + 4256
        wts = at("wts", [128, 2, 128], FB)
        decay = at("decay", [128, 2, 128], FB + 1024)
        k_w = at("k_w", [128, 2, 128], FB + 2048)
        v_x = at("v_x", [128, 2, 132], FB + 3072)
        assert FB + 3072 + 1056 <= F0 + 8 * T
        G0 = MX
        row = {n: at("row_" + n, [4, T], G0 + 4 * T * i) for i, n in enumerate(
            ["logi", "fg", "logf", "m", "g", "b"])}
        row["carry"] = at("row_carry", [4, T], G0 + 2 * 4256 + 4 * 4224 + 8512)
        row["t"] = at("row_t", [4, T], F0)
        row["enegm"] = at("row_enegm", [4, T], F0 + 4 * T)
        row["wend"] = at("row_wend", [4, T], F0 + 8 * T)
        XT = R1
        x_in = at("x_in", [128, NBLK + 1, D], XT)
        prm_in = at("prm_in", [128, 128], XT + (NBLK + 1) * D * 4)
        prm2_in = at("prm2_in", [128, 128], XT + (NBLK + 1) * D * 4 + 512)
        ADB = KD * 256 * 4
        ada_s = [at(f"ada_s{u}", [128, KD, 256], YF + ADB * u) for u in range(4)]
        ada_m = [at(f"ada_m{u}", [128, KD, 256], (YF, R1 + HB_ // 2)[u // 2] + ADB * (u % 2)) for u in range(4)]
        y_out = [at(f"y_out{p}", [128, D], R1 + 4096 * p) for p in range(2)]

        MS = XE - 10240
        mS = [MS]

        def state(name, shape):
            n = 4 * int(np.prod(shape[1:]))
            t = at(name, shape, mS[0])
            mS[0] += (n + 31) // 32 * 32
            assert mS[0] <= XE
            return t

        mem = [state("mem_prompt", [128, 132]), state("mem_sample", [128, 132])]
        mem_in = state("mem_in", [128, H_B, 128])
        mem_out = state("mem_out", [128, 2, 132])
        cols = state("cols", [128, NBLK + 1, 3, H_B])
        cols_h = state("cols_h", [128, NBLK + 1, 3])
        conv_h = state("conv_h", [128, 5, 2])
        hnorm_h = state("hnorm_h", [128, 1])
        onehot = state("onehot", [4, 1])
        ae_h = state("ae_h", [4, NBLK + 1])
        rden = state("rden", [128, 2])
        junk = state("junk", [128, 128])
        aend_h = state("aend_h", [128, NBLK + 1])
        ssq = state("ssq", [128, NBLK + 1])
        rs9 = state("rs9", [128, NBLK + 1])
        den = state("den", [128, 2])
        m_in = state("m_in", [4, 1])
        gate_b = state("gate_b", [36, 1])
        m_prev = state("m_prev", [4, NBLK + 1])
        nm_end = state("nm_end", [4, NBLK + 1])
        cmask = state("cmask", [128, 128])
        table = at("table", [16, 2 * MAX_REL + 1], XT + (NBLK + 1) * D * 4 + 1024)
        rtable = at("rtable", [16, REV], XT + (NBLK + 1) * D * 4 + 4096)
        assert mx[0] <= MS, (mx[0], MS)

        psum = ctx.enter_context(nc.psum_tensor("psum", [128, 8, 512], F32))
        def bank(b, w=512, rows=128):
            return psum[0:rows, b, 0:w]

        tps = psum[:, 5:7, :].rearrange("p b (s c) -> p (b s) c", c=128)
        oacc = psum[:, 7, :]

        x_spill = nc.dram_tensor("x_spill", [128, KD * T], F32, kind="Internal")
        rev_dram = nc.dram_tensor("rev_dram", [16, REV], F32, kind="Internal")

        bias_dram = nc.dram_tensor("bias_dram", [H_C, 128, 640], F32, kind="Internal")

        def sem(name):
            return ctx.enter_context(nc.semaphore(name))

        par_in, par2_in, misc_in, x_in_sem = sem("par_in"), sem("par2_in"), sem("misc_in"), sem("x_in_sem")
        const_done, rows_t, rows_got = sem("const_done"), sem("rows_t"), sem("rows_got")
        c_ready, ada_done, ada_got, derived = sem("c_ready"), sem("ada_done"), sem("ada_got"), sem("derived")
        ada_copied, ada_t = sem("ada_copied"), sem("ada_t")
        ada_loaded = [sem(f"ada_loaded{i}") for i in range(4)]
        xt_done, xt_act, xt_dve = sem("xt_done"), sem("xt_act"), sem("xt_dve")
        w_loaded = [sem("w_loaded0"), sem("w_loaded1")]
        hi_done, lo_done = sem("hi_done"), sem("lo_done")
        proj_done, evac_act, evac_dve = sem("proj_done"), sem("evac_act"), sem("evac_dve")
        ffhi_done, fflo_done = sem("ffhi_done"), sem("fflo_done")
        sq_done, ss_done, ms_done, rt_done = sem("sq_done"), sem("ss_done"), sem("ms_done"), sem("rt_done")
        x_new, xn_done, hh_done, hl_done = sem("x_new"), sem("xn_done"), sem("hh_done"), sem("hl_done")
        spilled, x_loaded = sem("spilled"), sem("x_loaded")
        scores, scores_read, p_done = sem("scores"), sem("scores_read"), sem("p_done")
        t_done, t_read, o_done, o_read = sem("t_done"), sem("t_read"), sem("o_done"), sem("o_read")
        oh_done, ol_done = sem("oh_done"), sem("ol_done")
        bias_raw, bias_ok = [sem("bias_raw0"), sem("bias_raw1")], [sem("bias_ok0"), sem("bias_ok1")]
        ck_in, cv_in = [sem("ck_in0"), sem("ck_in1")], [sem("cv_in0"), sem("cv_in1")]
        kv_stored, stored, sink_ok, rev_ok, rev_st = sem("kv_stored"), sem("stored"), sem("sink_ok"), sem("rev_ok"), sem("rev_st")
        rev_built, sink_neg, toeplitz = sem("rev_built"), sem("sink_neg"), sem("toeplitz")
        gate_raw, gate_e, gate_rows = sem("gate_raw"), sem("gate_e"), sem("gate_rows")
        gate_dve, cols_t, cols_ok = sem("gate_dve"), sem("cols_t"), sem("cols_ok")
        conv_in, conv_done, conv_stored, head_set = sem("conv_in"), sem("conv_done"), sem("conv_stored"), sem("head_set")
        abc_done, qa_done = sem("abc_done"), sem("qa_done")
        st_done, arg_done, kv_done = sem("st_done"), sem("arg_done"), sem("kv_done")
        decay_done, kvx_done, w_done = sem("decay_done"), sem("kvx_done"), sem("w_done")
        num_done, den_done, num_read = sem("num_done"), sem("den_done"), sem("num_read")
        upd_done, mem_done = sem("upd_done"), sem("mem_done")
        ms9, rt9, hn_done, hT_done, og_done, oh9, ol9 = (sem(n) for n in (
            "ms9", "rt9", "hn_done", "hT_done", "og_done", "oh9", "ol9"))
        memT_done, memT_read, n_copied, state_st = sem("memT_done"), sem("memT_read"), sem("n_copied"), sem("state_st")
        mstate_ok, conv_free, state_free = sem("mstate_ok"), sem("conv_free"), sem("state_free")
        yt_done, yt_read, y_st = sem("yt_done"), sem("yt_read"), [sem("y_st0"), sem("y_st1")]

        ctx.enter_context(nc.allow_non_contiguous_dma(reason="three frames of conv state, one column of n"))
        block = ctx.enter_context(nc.Block())

        def apart(eng):
            eng.sem_inc(waited[eng], 1)

        waited = {nc.tensor: sem("waited_pe"), nc.vector: sem("waited_dve"), nc.gpsimd: sem("waited_pool")}

        def one(n):
            return n + 1

        def tt_cols(tt):
            return slice(tt * TW, (tt + 1) * TW)

        def groups(tt):
            if tt < NTT - 1:
                return [(0, TW, 0)]
            return [(0, TW - TS, 0), (TW - TS, TW, 1)]

        def qrows(p):
            return 128 if p < NBLK else TS

        def score_width(kind, p):
            if p == NBLK:
                return BW[kind] - 128 + TS, 0
            w = min(BW[kind], 128 * (p + 1))
            return w, BW[kind] - w

        def key_blocks(kind, p):
            if p == NBLK:
                return [(("cache", i), 128) for i in range(BW[kind] // 128 - 1)] + [(NBLK, TS)]
            n = score_width(kind, p)[0] // 128
            return [(b, 128) for b in range(p - n + 1, p + 1)]

        KINDS = {
            "A": dict(n0=0, r0=4, o0=0, pre=0, lag=2, score_bufs=3, fills=21, probs=probs_a),
            "C": dict(n0=72, r0=4 + 72, o0=8, pre=4, lag=1, score_bufs=2, fills=18, probs=probs),
        }

        def score_bank(kind, n):
            return 1 + n % 3 if kind == "A" else 1 + 2 * (n % 2)

        @block.sync
        def _(sp):
            def rows_in(dst, r, src):
                n = src.shape[0]
                sp.dma_start(dst[r:r + n, :], src).then_inc(par_in if dst is prm_in else par2_in, 16)
                return r + n

            v128 = lambda a, pat: a.rearrange(pat, c=128)
            r = rows_in(prm_in, 0, v128(I["c_prompt"], "b (k c) -> (b k) c"))
            r = rows_in(prm_in, r, v128(I["c_sample"], "b (k c) -> (b k) c"))
            r = rows_in(prm_in, r, v128(I["norm_g"], "l n (k c) -> (l n k) c"))
            r = rows_in(prm_in, r, v128(I["conv_w_b"], "l j (k c) -> (l j k) c"))
            r = rows_in(prm_in, r, v128(I["conv_b_b"], "l (k c) -> (l k) c"))
            r = rows_in(prm_in, r, v128(I["hnorm_b"], "l (k c) -> (l k) c"))
            r = rows_in(prm_in, r, I["state_b_n"].rearrange("l b h c -> (l b h) c"))
            assert r == 128
            r = rows_in(prm2_in, 0, v128(I["b_ada"], "l (k c) -> (l k) c"))
            r = rows_in(prm2_in, r, v128(I["state_b_conv"], "l b j (k c) -> (l b j k) c"))
            assert r == 120
            sp.dma_start(ident[:, :], I["ident"]).then_inc(misc_in, 16)
            sp.dma_start(table[:, :], I["relbias_c"][0]).then_inc(rev_ok, 16)
            ada = I["w_ada"].rearrange("l (k p) n -> l p k n", p=128)
            xp = I["x_prompt"].rearrange("o (b p) d -> p (o b) d", p=128)
            for half in range(2):
                sp.dma_start(x_in[:, 4 * half:4 * half + 4, :], xp[:, 4 * half:4 * half + 4, :]).then_inc(x_in_sem, 16)
            sp.dma_start(x_in[0:TS, NBLK, :], I["x_sample"][0]).then_inc(x_in_sem, 16)
            def load(g, parts):
                if not (isinstance(g, int) and g < 2):
                    sp.wait_ge(lo_done, g - 1)
                for dst, src in parts:
                    sp.dma_start(dst, src).then_inc(w_loaded[parts_slot[0]], 16)

            parts_slot = [0]

            def plain(w, slot, cols, kt):
                parts_slot[0] = slot
                cut = {8: (0, 3, 6, 8), 5: (0, 2, 4, 5), 4: (0, 1, 2, 4)}[kt]
                return [(w_raw[:, slot, a:b, :], w[:, a:b, cols]) for a, b in zip(cut, cut[1:])]

            view = lambda a: a.rearrange("(k p) n -> p k n", p=128)
            w_ab = view(I["w_in_ab"][0])
            for i, c in enumerate((COL_KA, COL_VA)):
                load(i, plain(w_ab, i, slice(c, c + 128), KD))
            def ada_load(ring, layer, q, n):
                for u in range(4):
                    sp.wait_ge(ada_done, q * 4 + (n + u + 1))
                    if ring is ada_m and n + u == 10 and q == 0:
                        sp.wait_ge(hl_done, 3)
                    c = bass.ds(q * 1024 + ((n + u) * 256 - layer * 6 * D), 256)
                    sp.dma_start(ring[u][:, :, :], ada[layer][:, :, c]).then_inc(ada_loaded[u], 16)

            with sp.Fori(0, 2) as q:
                ada_load(ada_s, 0, q, 0)
            sp.wait_ge(rev_built, 2)
            sp.dma_start(rev_dram.ap(), rtable[:, :]).then_inc(rev_st, 16)
            sp.wait_ge(rev_st, 16)
            sp.dma_start(bias_dram.ap(), bass.AP(rev_dram, 127, [[REV, H_C], [-1, 128], [1, 640]])).then_inc(toeplitz, 16)
            def q_tile(t):
                g = plan["qa"][0] + t
                slot = g % 2
                parts_slot[0] = slot
                c0, c1 = slice(t * HD, t * HD + HD), slice(t * HD + 256, t * HD + 256 + HD)
                load(g, [(w_raw[:, slot, :, 0:HD], w_ab[:, :, c0]),
                         (w_raw[:, slot, 0:4, HD:128], w_ab[:, 0:4, c1]),
                         (w_raw[:, slot, 4:8, HD:128], w_ab[:, 4:8, c1])])

            def gates_tile():
                g = plan["gates"][0]
                parts_slot[0] = g % 2
                load(g, [(w_raw[:, g % 2, :, 0:4], w_ab[:, :, COL_IG:COL_IG + 4]),
                         (w_raw[:, g % 2, :, 32:36], w_ab[:, :, COL_FG:COL_FG + 4]),
                         (w_raw[:, g % 2, :, 64:68], w_ab[:, :, COL_FG:COL_FG + 4])])

            def head_tile(h, i):
                g0 = plan["heads"][0]
                c = (COL_QKB, COL_QKB + W_B, COL_VB, COL_OG, COL_QKB + 128)[i]
                load(h * 4 + (g0 + i), plain(w_ab, (g0 + i) % 2, bass.ds(h * 128 + c, 128) if not isinstance(h, int)
                                             else slice(h * 128 + c, h * 128 + c + 128), KD))

            q_tile(0)
            q_tile(1)
            ada_load(ada_m, 0, 0, 8)
            q_tile(2)
            ada_load(ada_m, 0, 0, 12)
            q_tile(3)
            with sp.Fori(1, 3) as q:
                ada_load(ada_m, 0, q, 12)
            ada_load(ada_m, 1, 3, 12)
            gates_tile()
            with sp.Fori(4, 6) as q:
                ada_load(ada_m, 1, q, 12)
            head_tile(0, 0)
            with sp.Fori(6, 9) as q:
                ada_load(ada_m, 1, q, 12)
            with sp.Fori(0, H_B - 1) as hd:
                for i in range(1, 5):
                    head_tile(hd, i)
            for i in range(1, 4):
                head_tile(H_B - 1, i)

            def out_tiles(layer):
                g0 = plan[f"out{layer}"][0]
                w = view(I["w_out_c"][0]) if layer else None
                with sp.Fori(0, KD // 2) as j:
                    for par in range(2):
                        slot = (g0 + par) % 2
                        c = bass.ds(j * 256 + par * 128, 128)
                        if layer:
                            parts = plain(w, slot, c, KD)
                        else:
                            parts_slot[0] = slot
                            wo = I["w_out_ab"][0]
                            lo_h = wo[0:256, :].rearrange("(k p) n -> p k n", p=HD)
                            hi_h = wo[256:512, :].rearrange("(k p) n -> p k n", p=HD)
                            rest = wo[512:1024, :].rearrange("(k p) n -> p k n", p=128)
                            parts = [(w_raw[0:HD, slot, 0:4, :], lo_h[:, :, c]),
                                     (w_raw[HD:128, slot, 0:4, :], hi_h[:, :, c]),
                                     (w_raw[:, slot, 4:8, :], rest[:, :, c])]
                        load(j * 2 + (g0 + par), parts)

            def ffn_tiles(layer):
                wg, wu = view(I["w_ffn_gate"][layer]), view(I["w_ffn_up"][layer])
                f0 = 0
                for n, ff in enumerate(FF_GROUPS):
                    g0 = plan[f"gu{layer}{n}"][0]
                    with sp.Fori(0, ff) as f:
                        c = bass.ds(f * 128 + f0 * 128, 128)
                        load(f * 2 + g0, plain(wg, g0 % 2, c, KD))
                        load(f * 2 + (g0 + 1), plain(wu, (g0 + 1) % 2, c, KD))
                    wd = view(I["w_ffn_down"][layer][f0 * 128:(f0 + ff) * 128, :])
                    g0 = plan[f"down{layer}{n}"][0]
                    with sp.Fori(0, KD // 2) as j:
                        for par in range(2):
                            load(j * 2 + (g0 + par), plain(wd, (g0 + par) % 2, bass.ds(j * 256 + par * 128, 128), ff))
                    f0 += ff

            out_tiles(0)
            ffn_tiles(0)
            w_c = view(I["w_in_c"][0])
            g0 = plan["qkv"][0]
            with sp.Fori(0, KD // 2) as j:
                for i in range(6):
                    c = bass.ds(j * 256 + (i // 3) * 128 + (i % 3) * D, 128)
                    load(j * 6 + (g0 + i), plain(w_c, (g0 + i) % 2, c, KD))
            out_tiles(1)
            ffn_tiles(1)
            for b in range(NBLK + 1):
                sp.wait_ge(yt_read, b + 1)
                n = qrows(b)
                dst = O["y_prompt"][0, b * 128:(b + 1) * 128, :] if b < NBLK else O["y_sample"][0]
                sp.dma_start(dst, y_out[b % 2][0:n, :]).then_inc(y_st[b % 2], 16)
            sp.wait_ge(y_st[0], 16 * (NBLK // 2 + 1))
            sp.wait_ge(y_st[1], 16 * (NBLK // 2))

        @block.gpsimd
        def _(pool):
            nc.gpsimd.memset(ones[:, :], 1.0).then_inc(const_done, 1)
            pool.sem_inc(conv_free, 1)
            pool.sem_inc(state_free, 1)
            pool.dma_start(neg_sink[:, :], I["sink_a"][0].partition_broadcast(128)).then_inc(sink_ok, 16)
            pool.wait_ge(hl_done, 3)
            pool.dma_start(x_spill.ap(), x[:, :, :].rearrange("p k t -> p (k t)")).then_inc(spilled, 16)
            pool.wait_ge(spilled, 16)
            pool.dma_start(cache_ak[:, :], I["cache_a_k"][0, 0].rearrange("t h d -> t (h d)")).then_inc(ck_in[0], 16)
            pool.dma_start(v_tok[:, NBLK + 1, :], I["cache_a_v"][0, 0].rearrange("t h d -> t (h d)")).then_inc(cv_in[0], 16)
            pool.wait_ge(t_read, 4)
            a_k = lambda a: a[0, 0].rearrange("t h d -> t (h d)")
            pool.dma_start(a_k(O["pa_k"]), k_out[:, 0, :]).then_inc(kv_stored, 16)
            pool.dma_start(a_k(O["sa_k"]), k_out[0:TS, 1, :]).then_inc(kv_stored, 16)
            pool.dma_start(a_k(O["pa_v"]), v_tok[:, NBLK - 1, :]).then_inc(kv_stored, 16)
            pool.dma_start(a_k(O["sa_v"]), v_tok[0:TS, NBLK, :]).then_inc(kv_stored, 16)
            with pool.Fori(0, 4) as t:
                for e in range(2):
                    pool.wait_ge(scores_read, t * 18 + CREDIT)
                    apart(pool)
                    pool.dma_start(neg_bias[:, e, 0:256].unsqueeze(1), I["alibi"].rearrange("h p c -> p h c")[:, bass.ds(t + e * 4, 1), :]
                                   ).then_inc(bias_raw[e], 16)
            pool.wait_ge(ol_done, one(8))
            pool.wait_ge(kv_stored, 64)
            pool.dma_start(m_in[:, :], I["state_b_m"][0].rearrange("b h -> h b")).then_inc(mstate_ok, 16)
            pool.dma_start(gate_b[0:4, :], I["b_gates_b"][0:1, 0:4].rearrange("b h -> h b")).then_inc(mstate_ok, 16)
            pool.dma_start(gate_b[32:36, :], I["b_gates_b"][0:1, 4:8].rearrange("b h -> h b")).then_inc(mstate_ok, 16)
            pool.dma_start(cmask[:, :], I["causal"]).then_inc(mstate_ok, 16)
            pool.dma_start(mem_in[:, :, :], I["state_b_c"][0, 0].rearrange("h v k -> v h k")).then_inc(mstate_ok, 16)
            pool.wait_ge(gate_rows, 2)
            pool.dma_start(O["pb_m"][0].rearrange("b h -> h b"), row["m"][:, TP - 1:TP]).then_inc(stored, 16)
            pool.dma_start(O["sb_m"][0].rearrange("b h -> h b"), row["m"][:, T - 1:T]).then_inc(stored, 16)
            with pool.Fori(0, H_B) as h:
                for i in range(2):
                    pool.wait_ge(evac_act, h * 12 + (CREDIT + plan["heads"][2] + 3 * (i + 1)))
                    apart(pool)
                    for name, c in (("pb_conv", TP), ("sb_conv", UW - 3)):
                        dst = O[name][0, 0].rearrange("j f -> f j")
                        pool.dma_start(dst[bass.ds(h * 128 + i * W_B, 128), :], u_in[i][:, c:c + 3]).then_inc(conv_stored, 16)
                pool.wait_ge(conv_stored, h * 64 + 64)
                pool.sem_inc(conv_free, 1)
                pool.wait_ge(memT_read, one(h + 1))
                apart(pool)
                for i, (nc_, nn) in enumerate((("pb_c", "pb_n"), ("sb_c", "sb_n"))):
                    dst = O[nc_][0, 0].rearrange("h v k -> v h k")
                    pool.dma_start(dst[:, bass.ds(h, 1), :], mem_out[:, i, 0:128]).then_inc(state_st, 16)
                    dst = O[nn][0, 0].rearrange("h k -> k h")
                    pool.dma_start(dst[:, bass.ds(h, 1)], mem_out[:, i, 128:129]).then_inc(state_st, 16)
                pool.wait_ge(state_st, h * 64 + 64)
                pool.sem_inc(state_free, 1)

            def reload_x(layer):
                pool.wait_ge(proj_done, 3 * plan[f"out{layer}"][0] + 1)
                pool.dma_start(x[:, :, :].rearrange("p k t -> p (k t)"), x_spill.ap()).then_inc(x_loaded, 16)

            reload_x(0)
            pool.wait_ge(hl_done, 9)
            pool.dma_start(x_spill.ap(), x[:, :, :].rearrange("p k t -> p (k t)")).then_inc(spilled, 16)
            pool.wait_ge(spilled, 32)

            def bias_c(hp, e, first=False):
                if not first:
                    pool.wait_ge(scores_read, hp * 18 + (CREDIT + 72 - 18 + 9 * (e + 1)))
                    apart(pool)
                pool.dma_start(neg_bias[:, e, :].unsqueeze(1), bias_dram.ap().rearrange("h p c -> p h c")[:, bass.ds(hp * 2 + e, 1), :]).then_inc(bias_raw[e], 16)
                pool.wait_ge(bias_raw[e], hp * 16 + (64 + 16))
                apart(pool)
                nc.gpsimd.memset(neg_bias[0:64, e, 576:640], BIG)
                nc.gpsimd.memset(neg_bias[64:128, e, 0:64], BIG).then_inc(bias_ok[e], 1)

            def caches_c(hp, par):
                for name, dst, s in (("cache_c_k", cache_k, ck_in), ("cache_c_v", cache_v, cv_in)):
                    src = I[name][0, 0].rearrange("(b p) h d -> p b (h d)", p=128)
                    pool.dma_start(dst[par][:, :, :], src[:, :, bass.ds(hp * 128, 128)]).then_inc(s[par], 16)

            def stores_c(hp):
                pool.wait_ge(t_read, hp * 22 + (76 + 4))
                apart(pool)
                for pn, sn, src in (("pc_k", "sc_k", k_out), ("pc_v", "sc_v", v_tok[:, 4:9, :])):
                    dst = O[pn][0, 0].rearrange("(b p) h d -> p b (h d)", p=128)
                    pool.dma_start(dst[:, :, bass.ds(hp * 128, 128)], src[:, 0:4, :]).then_inc(kv_stored, 16)
                    dst = O[sn][0, 0].rearrange("p h d -> p (h d)")
                    pool.dma_start(dst[:, bass.ds(hp * 128, 128)], src[0:TS, 4, :]).then_inc(kv_stored, 16)

            def pair_c(hp, par, last):
                if not last:
                    pool.wait_ge(ol_done, one(hp * 2 + 8))
                    apart(pool)
                    caches_c(hp + 1, 1 - par)
                stores_c(hp)
                if not last:
                    for e in range(2):
                        bias_c(hp + 1, e)

            pool.wait_ge(toeplitz, 16)
            caches_c(0, 0)
            for e in range(2):
                bias_c(0, e, first=True)
            with pool.Fori(0, 3) as j:
                for par in range(2):
                    pair_c(j * 2 + par, par, False)
            pair_c(6, 0, False)
            pair_c(7, 1, True)
            pool.wait_ge(kv_stored, 64 + 64 * 8)
            reload_x(1)

        @block.tensor
        def _(pe):
            tr = nc.tensor.transpose

            def project(g, slot, tt, hi, lo, kt, b, free, half=None):
                if half != 1:
                    pe.wait_ge(free[0], free[1])
                    pe.wait_ge(lo_done, g + 1)
                out = psum[:, b, 0:TW]
                c = tt_cols(tt)
                for k in {None: range(kt), 0: range(kt // 2), 1: range(kt // 2, kt)}[half]:
                    nc.tensor.matmul(out, w_hi[:, slot, k], hi[:, k, c], start=(k == 0), stop=False)
                    nc.tensor.matmul(out, w_hi[:, slot, k], lo[:, k, c], start=False, stop=False)
                    last = nc.tensor.matmul(out, w_lo[:, slot, k], hi[:, k, c], start=False, stop=(k == kt - 1))
                if half != 0:
                    last.then_inc(proj_done, 1)

            def act_tile(name, i, slot, src, par=None):
                g0, _, a0, _ = plan[name]
                for tt in range(NTT):
                    project(i + g0, slot, tt, src[0], src[1], KD, tt, (evac_act, i * 3 + (a0 + tt + 1)))

            pe.sem_inc(hT_done, 1)
            pe.sem_inc(ada_done, 4)
            pe.wait_ge(misc_in, 16)
            pe.wait_ge(par_in, 112)
            tr(bank(0, 128), prm_in[:, :], ident[:, :]).then_inc(rows_t, 1)
            pe.wait_ge(par2_in, 32)
            tr(bank(1, 120), prm2_in[0:120, :], ident[0:120, 0:120]).then_inc(rows_t, 1)
            pe.wait_ge(rows_got, 2)
            pe.wait_ge(x_in_sem, 48)
            for k in range(KD):
                for part in range(3):
                    n = 3 * k + part
                    if n >= 3:
                        pe.wait_ge(xt_act, k) if part == 0 else pe.wait_ge(xt_dve, 2 * (k - 1) + part)
                    for b in range(4 * part, min(4 * part + 4, NBLK + 1)):
                        m = qrows(b)
                        last = tr(psum[:, part, 128 * (b % 4):128 * (b % 4) + m],
                                  x_in[0:m, b, 128 * k:128 * k + 128], ident[0:m, 0:m])
                    last.then_inc(xt_done, 1)
            def sum_squares(n):
                for tt in range(NTT):
                    pe.wait_ge(sq_done, 3 * n + tt + 1)
                    for k in range(KD):
                        last = nc.tensor.matmul(bank(tt, TW), ones[:, :], norm_buf[:, tt, k], start=(k == 0), stop=(k == KD - 1))
                    last.then_inc(ss_done, 1)

            pe.wait_ge(const_done, 1)
            sum_squares(0)

            def ada_products(ring, m, half, bank_, copied, loads):
                u = m % 4
                if half == 0:
                    pe.wait_ge(ada_copied, copied)
                    pe.wait_ge(ada_loaded[u], loads)
                for k in range(half * KD // 2, (half + 1) * KD // 2):
                    last = nc.tensor.matmul(psum[0:2, bank_, 0:256], silu_c[:, k], ring[u][:, k, :],
                                            start=(k == 0), stop=(k == KD - 1))
                if half == 1:
                    last.then_inc(ada_done, 1)

            def ada_transposes(q, bank_):
                pe.wait_ge(ada_copied, q * 4 + (4 + 2))
                pe.wait_ge(ada_got, one(q))
                apart(pe)
                for v in range(8):
                    last = tr(psum[:, bank_, 2 * v:2 * v + 2], ada_row[:, v // 2, 128 * (v % 2):128 * (v % 2) + 128], ident[0:2, 0:2])
                last.then_inc(ada_t, 1)

            pe.wait_ge(c_ready, 1)
            with pe.Fori(0, 2) as q:
                for v in range(8):
                    ada_products(ada_s, v // 2, v % 2, 3 + v // 2 % 2, q * 4 + (v // 2 + 1), q * 16 + 16)
                ada_transposes(q, 5)

            h = (h_hi, h_lo)
            def att_round(kind, it, r, items, after_out=False):
                c = KINDS[kind]
                for out_slot, src, m, n in items:
                    last = tr(tps[0:n, out_slot, 0:m], src, ident[0:m, 0:m])
                last.then_inc(t_done, 1)

            def attention(kind, it, q, k, kct, vt, vc, par, fill, pre):
                c = KINDS[kind]
                N = lambda n: it * 18 + (c["n0"] + n)
                R = lambda n: it * (18 + c["pre"]) + (c["r0"] + c["pre"] + n)
                lag, sb = c["lag"], c["score_bufs"]
                pre()
                for i in range(19 + lag):
                    if i < 18:
                        n, e, p = i, i // 9, i % 9
                        m, (w, _) = qrows(p), score_width(kind, p)
                        rows = slice(64 * e, 64 * e + 64)
                        pe.wait_ge(scores_read, N(n) + (CREDIT + 1 - sb))
                        apart(pe)
                        lhs = q[rows, 128 * p:128 * p + m]
                        col = 0
                        for blk, kn in cut_scores(kind, p):
                            last = nc.tensor.matmul(psum[0:m, score_bank(kind, n) + col // 512, col % 512:col % 512 + kn],
                                                    lhs, keys(blk, kn, rows, k, kct), start=True, stop=True)
                            col += kn
                        last.then_inc(scores, 1)
                    if fill and i < c["fills"]:
                        fill(i)
                    if lag <= i < 18 + lag:
                        n = i - lag
                        e, p = n // 9, n % 9
                        m = qrows(p)
                        pe.wait_ge(p_done, N(n) + 1)
                        pe.wait_ge(t_read, R(n))
                        apart(pe)
                        for s, (_, kn) in enumerate(key_blocks(kind, p)):
                            last = tr(tps[0:kn, s, 0:m], c["probs"][0:m, n % sb, 128 * s:128 * s + kn], ident[0:m, 0:m])
                        last.then_inc(t_done, 1)
                    if i > lag:
                        n = i - lag - 1
                        e, p = n // 9, n % 9
                        m = qrows(p)
                        pe.wait_ge(t_read, R(n) + 1)
                        pe.wait_ge(o_read, one(N(n)))
                        apart(pe)
                        kb = key_blocks(kind, p)
                        for s, (blk, kn) in enumerate(kb):
                            v = vc[0:kn, blk[1], 64 * e:64 * e + 64] if isinstance(blk, tuple) else vt[0:kn, blk, 64 * e:64 * e + 64]
                            last = nc.tensor.matmul(oacc[0:m, 0:64], probs_t[0:kn, n % 2, s, 0:m], v,
                                                    start=(s == 0), stop=(s == len(kb) - 1))
                        last.then_inc(o_done, 1)
                pe.wait_ge(o_read, one(N(18)))
                for r, blocks in enumerate((range(0, 5), range(5, 9))):
                    pe.wait_ge(t_read, R(18))
                    if r == 1:
                        pe.wait_ge(ol_done, one(it * 2 + (c["o0"] + 1)))
                    for s, b in enumerate(blocks):
                        m = qrows(b)
                        last = tr(tps[:, s, 0:m], o_tok[0:m, b, :], ident[0:m, 0:m])
                    last.then_inc(t_done, 1)

            def cut_scores(kind, p):
                if p == NBLK:
                    return [(("cache", 0), BW[kind] - 128), (TP, TS)]
                w = score_width(kind, p)[0]
                k0 = 128 * (p + 1) - w
                return [(k0, min(w, 512))] + ([(k0 + 512, w - 512)] if w > 512 else [])

            def keys(blk, kn, rows, k, kct):
                return kct[rows, 0:kn] if isinstance(blk, tuple) else k[rows, blk:blk + kn]

            def ada_fill(j, par, i):
                v = 20 * par + i
                if v in (8, 16, 24, 32) or v == 40:
                    ada_transposes(j * 5 + (2 + v // 8 - 1), 4)
                if i < 20:
                    m = v // 2
                    ada_products(ada_m, m, v % 2, 0, j * 20 + (8 + m + 2), j * 80 + 16 * (2 + m // 4 + 1))

            pe.wait_ge(hl_done, 3)
            for i in range(2):
                act_tile("kv", i, i, h)
            pe.wait_ge(ck_in[0], 16)
            att_round("A", 0, 0, [(0, cache_ak[:, :], 128, 128)])
            pe.wait_ge(evac_act, CREDIT + 6)
            pe.wait_ge(t_read, 1)
            att_round("A", 0, 1, [(s, v_a[:, 128 * b:128 * b + 128], 128, 128) for s, b in enumerate(range(5))])
            pe.wait_ge(t_read, 2)
            att_round("A", 0, 2, [(s, v_a[:, 128 * b:128 * b + qrows(b)], 128, qrows(b)) for s, b in enumerate(range(5, 9))])
            pe.wait_ge(t_read, 3)
            att_round("A", 0, 3, [(s, k_a[:, 128 * b:128 * b + qrows(b)], 128, qrows(b)) for s, b in enumerate((7, 8))])
            pe.wait_ge(cv_in[0], 16)
            with pe.Fori(0, 2) as j:
                for par in range(2):
                    t = j * 2 + par
                    act_tile("qa", t, (plan["qa"][0] + par) % 2, h)
                    pe.wait_ge(evac_act, t * 3 + (CREDIT + plan["qa"][2] + 3))
                    pe.wait_ge(ol_done, one(t * 2))
                    attention("A", t, q_a, k_a, cache_akt, v_tok, v_tok[:, NBLK + 1:NBLK + 2, :], par,
                              lambda i: ada_fill(j, par, i), lambda: None)
            pe.wait_ge(ol_done, one(8))
            act_tile("gates", 0, plan["gates"][0] % 2, h)
            pe.wait_ge(gate_rows, 2)
            for b in range(NBLK + 1):
                m = qrows(b)
                for i, name in enumerate(("g", "wend", "enegm")):
                    last = tr(psum[0:m, 5, 12 * b + 4 * i:12 * b + 4 * i + 4], row[name][:, 128 * b:128 * b + m], ident[0:4, 0:4])
            last.then_inc(cols_t, 1)
            pe.wait_ge(mstate_ok, 80)
            for i in range(H_B):
                last = tr(psum[:, 6, 128 * i:128 * i + 128], mem_in[:, i, :], ident[:, :])
            last.then_inc(cols_t, 1)
            pe.wait_ge(cols_ok, 2)
            with pe.Fori(0, H_B) as hd:
                g0 = plan["heads"][0]
                for i in range(4):
                    act_tile("heads", hd * 4 + i, (g0 + i) % 2, h)
                pe.wait_ge(head_set, hd + 1)
                pe.wait_ge(evac_act, hd * 12 + (CREDIT + plan["heads"][2] + 12))
                pe.wait_ge(og_done, one(hd))
                for tt in range(NTT):
                    nc.tensor.matmul(bank(tt, TW), ones[0:4, :], a_h[:, tt_cols(tt)], start=True, stop=True
                                     ).then_inc(abc_done, 1)
                nc.tensor.matmul(bank(3, NBLK + 1), ones[0:4, :], ae_h[:, :], start=True, stop=True
                                 ).then_inc(abc_done, 1)
                pe.wait_ge(conv_in, one(hd * 2 + 2))
                pe.wait_ge(qa_done, hd * 4 + 4)
                pe.wait_ge(ol9, one(hd))
                pe.wait_ge(memT_read, one(hd))

                def front(c):
                    m = qrows(c)
                    cs = slice(128 * c, 128 * c + m)
                    pe.wait_ge(w_done, one(hd * 9 + c))
                    nc.tensor.matmul(psum[0:m, 4, 0:m], qk_b[1][:, cs], qk_b[0][:, cs], start=True, stop=True).then_inc(st_done, 1)
                    pe.wait_ge(decay_done, one(hd * 9 + c))
                    apart(pe)
                    nc.tensor.matmul(psum[0:m, 5, 0:m], ones[0:4, 0:m], nm_h[:, cs], start=True, stop=False)
                    nc.tensor.matmul(psum[0:m, 5, 0:m], ident[0:m, 0:m], cmask[0:m, 0:m], start=False, stop=True).then_inc(arg_done, 1)
                    pe.wait_ge(kvx_done, one(hd * 9 + c))
                    tr(psum[0:m, 6, 0:128], qk_b[1][:, cs], ident[:, :])
                    tr(psum[0:m, 6, 128:256], v_b[:, cs], ident[:, :]).then_inc(kv_done, 1)

                def back(c):
                    m = qrows(c)
                    cs = slice(128 * c, 128 * c + m)
                    mm = mem[c // NBLK]
                    pe.wait_ge(mem_done, hd * 11 + (c + 2))
                    pe.wait_ge(num_read, one(hd * 9 + c))
                    pe.wait_ge(w_done, one(hd * 9 + (c + 1)))
                    pe.wait_ge(kvx_done, one(hd * 9 + (c + 1)))
                    nc.tensor.matmul(psum[0:m, 7, 0:129], qa_b[:, cs], mm[:, 0:129], start=True, stop=False)
                    nc.tensor.matmul(psum[0:m, 7, 0:129], wts[0:m, c % 2, 0:m], v_x[0:m, c % 2, 0:129], start=False, stop=True
                                     ).then_inc(num_done, 1)
                    nc.tensor.matmul(psum[:, 3, 0:129], k_w[0:m, c % 2, :], v_x[0:m, c % 2, 0:129], start=True, stop=True
                                     ).then_inc(upd_done, 1)

                front(0)
                for c in range(NBLK + 1):
                    if c < NBLK:
                        front(c + 1)
                    back(c)
                pe.wait_ge(mem_done, hd * 11 + 11)
                pe.wait_ge(kvx_done, one(hd * 9 + 9))
                for i in range(2):
                    last = tr(psum[:, 6, 128 * i:128 * i + 128], mem[i][:, 0:128], ident[:, :])
                last.then_inc(memT_done, 1)
                pe.wait_ge(hn_done, hd + 1)
                for r, blocks in enumerate((range(0, 4), range(4, 8), range(8, 9))):
                    b_ = (4, 5, 3)[r]
                    for s, b in enumerate(blocks):
                        m = qrows(b)
                        last = tr(psum[:, b_, 128 * s:128 * s + m], h_tok[0:m, b, :], ident[0:m, 0:m])
                    last.then_inc(hT_done, 1)

            def out_tiles(layer):
                with pe.Fori(0, KD // 2) as j:
                    for par in range(2):
                        act_tile(f"out{layer}", j * 2 + par, (plan[f"out{layer}"][0] + par) % 2, (o_hi, o_lo))

            def ffn(layer):
                for n, ff in enumerate(FF_GROUPS):
                    g0, _, a0, d0 = plan[f"gu{layer}{n}"]
                    with pe.Fori(0, ff) as f:
                        for tt in range(NTT):
                            project(f * 2 + g0, g0 % 2, tt, h_hi, h_lo, KD, tt, (evac_dve, f * 3 + (d0 + CREDIT - 2 + tt)))
                        for tt in range(NTT):
                            project(f * 2 + (g0 + 1), (g0 + 1) % 2, tt, h_hi, h_lo, KD, tt, (evac_act, f * 3 + (a0 + CREDIT + 1 + tt)))
                    nff = 3 * (sum(FF_GROUPS) * layer + sum(FF_GROUPS[:n + 1]))
                    pe.wait_ge(fflo_done, nff)
                    g0, _, _, d0 = plan[f"down{layer}{n}"]
                    with pe.Fori(0, KD // 2) as j:
                        for par in range(2):
                            for tt in range(NTT):
                                project(j * 2 + (g0 + par), (g0 + par) % 2, tt, ff_hi, ff_lo, ff, tt,
                                        (evac_dve, j * 6 + (3 * par + d0 + tt + CREDIT - 2)))

            pe.wait_ge(ol9, one(H_B))
            out_tiles(0)
            sum_squares(1)
            sum_squares(2)
            pe.wait_ge(hl_done, 6)
            ffn(0)
            sum_squares(3)
            sum_squares(4)
            pe.wait_ge(hl_done, 9)
            g0, _, a0, _ = plan["qkv"]

            def qkv_step(hp, par, f, b, ahead, half=None):
                i, tt = f // 3, f % 3
                slot = (g0 + 3 * par + i) % 2
                project(hp * 3 + (g0 + i), slot, tt, h_hi, h_lo, KD, b, (evac_act, hp * 9 + (a0 + f + CREDIT - ahead)), half)

            for f in range(9):
                qkv_step(0, 0, f, f % 3, 2)

            def pair(hp, par, last):
                c = KINDS["C"]
                pe.wait_ge(evac_act, hp * 9 + (a0 + 9 + CREDIT))
                R = lambda n: hp * 22 + (c["r0"] + n)

                def pre():
                    pe.wait_ge(ol_done, one(hp * 2 + c["o0"]))
                    pe.wait_ge(ck_in[par], ck_count(hp, par))
                    att_round("C", hp, 0, [(s, cache_k[par][:, s, :], 128, 128) for s in range(4)])
                    pe.wait_ge(t_read, R(1))
                    att_round("C", hp, 1, [(s, v_c[par][:, 128 * b:128 * b + 128], 128, 128) for s, b in enumerate(range(5))])
                    pe.wait_ge(t_read, R(2))
                    att_round("C", hp, 2, [(s, v_c[par][:, 128 * b:128 * b + qrows(b)], 128, qrows(b)) for s, b in enumerate(range(5, 9))])
                    pe.wait_ge(t_read, R(3))
                    att_round("C", hp, 3, [(s, k_c[par][:, 128 * b:128 * b + qrows(b)], 128, qrows(b)) for s, b in enumerate(range(4, 9))])
                    pe.wait_ge(cv_in[par], ck_count(hp, par))
                    pe.wait_ge(t_read, R(4))

                fill = None if last else (lambda i: qkv_step(hp + 1, 1 - par, i // 2, 0, 0, i % 2))
                attention("C", hp, q_c[par], k_c[par], cache_kt, v_tok, cache_v[par], par, fill, pre)

            def ck_count(hp, par):
                return (hp - par) * 8 + (16 + (16 if par == 0 else 0))

            with pe.Fori(0, 3) as j:
                for par in range(2):
                    pair(j * 2 + par, par, False)
            pair(6, 0, False)
            pair(7, 1, True)
            pe.wait_ge(ol_done, one(24))
            out_tiles(1)
            sum_squares(5)
            sum_squares(6)
            pe.wait_ge(hl_done, 12)
            ffn(1)
            sum_squares(7)
            pe.wait_ge(x_new, 12)
            for b in range(NBLK + 1):
                m = qrows(b)
                if b >= 2:
                    pe.wait_ge(yt_read, b - 1)
                for k in range(KD):
                    last = tr(psum[0:m, 4 * (b % 2) + k // 4, 128 * (k % 4):128 * (k % 4) + 128], x[:, k, 128 * b:128 * b + m], ident[:, :])
                last.then_inc(yt_done, 1)

        @block.scalar
        def _(act):
            A = nc.scalar.activation
            for s in (decay_done, kvx_done, num_read, memT_read, conv_in):
                act.sem_inc(s, 1)
            act.sem_inc(evac_act, CREDIT)

            def split_hi(g, slot):
                if not (isinstance(g, int) and g < 2):
                    act.wait_ge(proj_done, g * 3 - 3)
                act.wait_ge(w_loaded[slot], loads(g, slot))
                A(w_hi[:, slot], w_raw[:, slot], ACT.Copy).then_inc(hi_done, 1)

            def loads(g, slot):
                return (g - slot) * 24 + 48

            def split_next(g, slot):
                if isinstance(g, int) and g + 2 >= TILES:
                    return
                split_hi(g + 2, slot)

            act.wait_ge(rows_t, 1)
            A(prm[:, :], bank(0, 128), ACT.Copy).then_inc(rows_got, 1)
            act.drain()
            A(silu_c[:, :, :].rearrange("p k r -> p r k"), prm[:, 0:16].rearrange("p (r k) -> p r k", r=2), ACT.Silu).then_inc(c_ready, 1)
            act.wait_ge(rows_t, 2)
            A(prm2[:, :], bank(1, 120), ACT.Copy).then_inc(rows_got, 1)
            for k in range(KD):
                act.wait_ge(xt_done, 3 * k + 1)
                A(x[:, k, 0:512], bank(0), ACT.Copy).then_inc(xt_act, 1)
            def square(n, src, ready):
                for tt in range(NTT):
                    act.wait_ge(ready[0], ready[1] + (tt if ready[2] else 0))
                    A(norm_buf[:, tt], src[:, :, tt_cols(tt)], ACT.Square).then_inc(sq_done, 1)

            def root(n):
                for tt in range(NTT):
                    act.wait_ge(ms_done, 3 * n + tt + 1)
                    A(rstd[:, tt], rstd[:, tt], ACT.Sqrt).then_inc(rt_done, 1)

            def h_out(n, s):
                for tt in range(NTT):
                    act.wait_ge(xn_done, 3 * n + tt + 1)
                    for k in range(KD):
                        for a, b, r in groups(tt):
                            A(norm_buf[:, tt, k, a:b], norm_buf[:, tt, k, a:b], ACT.Identity,
                              scale=pre_scale[:, s, k, r:r + 1], bias=mod[:, 3 * s, k, r:r + 1])
                    act.drain()
                    A(h_hi[:, :, tt_cols(tt)], norm_buf[:, tt], ACT.Copy).then_inc(hh_done, 1)

            for g in range(2):
                split_hi(g, g)
            act.wait_ge(xt_dve, 16)
            square(0, x, (xt_act, 8, False))
            root(0)
            act.wait_ge(derived, 1)
            h_out(0, 0)

            def copies(name, i, slot, dst, func=ACT.Copy, scale=1.0, wait=None, g=None):
                g0, _, a0, _ = plan[name]
                for tt in range(NTT):
                    act.wait_ge(proj_done, i * 3 + (3 * g0 + tt + 1))
                    A(dst(tt), bank(tt, TW), func, scale=scale).then_inc(evac_act, 1)
                split_next(i + g0, slot)

            def attention(kind, it, sinks, fill, pre):
                c = KINDS[kind]
                N = lambda n: it * 18 + (c["n0"] + n)
                TD = lambda n: it * (20 + c["pre"]) + ((0 if kind == "A" else 4 + 80) + (4 if kind == "A" else 0) + c["pre"] + n)
                lag, sb, probs = c["lag"], c["score_bufs"], c["probs"]
                pre()
                def exps(n):
                    p = n % 9
                    m, (w, _) = qrows(p), score_width(kind, p)
                    act.wait_ge(scores_read, N(n) + (CREDIT + 1))
                    if sinks:
                        e = n // 9
                        A(sink_e[0:m, n % 6:n % 6 + 1], sink2[0:m, e:e + 1], ACT.Exp, scale=-1.0, bias=mins[0:m, n % 6:n % 6 + 1])
                    A(probs[0:m, n % sb, 0:w], probs[0:m, n % sb, 0:w], ACT.Exp, scale=-1.0,
                      bias=mins[0:m, n % 6:n % 6 + 1], accum_out=sums[0:m, n % 6:n % 6 + 1]).then_inc(p_done, 1)

                def copy(n):
                    p = n % 9
                    m, kb = qrows(p), key_blocks(kind, p)
                    act.wait_ge(t_done, TD(n) + 1)
                    full = sum(kn == 128 for _, kn in kb)
                    if full == len(kb):
                        A(probs_t[:, n % 2, 0:full, 0:m], tps[:, 0:full, 0:m], ACT.Copy).then_inc(t_read, 1)
                    else:
                        A(probs_t[:, n % 2, 0:full, 0:m], tps[:, 0:full, 0:m], ACT.Copy)
                        A(probs_t[0:TS, n % 2, full, 0:m], tps[0:TS, full, 0:m], ACT.Copy).then_inc(t_read, 1)

                for i in range(18 + lag):
                    if lag == 1 and i < 18:
                        exps(i)
                    if i >= lag:
                        copy(i - lag)
                    if lag > 1 and i < 18:
                        exps(i)
                    if fill and i % 2 == 1 and i < 18:
                        fill((i - 1) // 2)
                for r in range(2):
                    act.wait_ge(t_done, TD(18 + r) + 1)
                    nb, c0 = (5, 0) if r == 0 else (4, 640)
                    dst = o_hi[:, bass.ds(it, 1) if not isinstance(it, int) else slice(it, it + 1), :]
                    w = 640 if r == 0 else T - 640
                    A(dst[:, :, c0:c0 + w], psum_cols(w), ACT.Copy).then_inc(oh_done, 1)

            def psum_cols(w):
                return psum[:, 5:7, :].rearrange("p b c -> p (b c)")[:, 0:w].unsqueeze(1)

            act.wait_ge(spilled, 16)
            act.wait_ge(rev_st, 16)

            def num_out(hd, c):
                m = qrows(c)
                act.wait_ge(den_done, hd * 9 + (c + 1))
                A(h_tok[0:m, c, :], psum[0:m, 7, 0:128], ACT.Copy, scale=rden[0:m, c % 2:c % 2 + 1])
                A(junk[0:m, :], psum[0:m, 7, 0:128], ACT.Square, scale=rden[0:m, c % 2:c % 2 + 1],
                  accum_out=ssq[0:m, c:c + 1]).then_inc(num_read, 1)

            copies("kv", 0, 0, lambda tt: k_a[:, tt_cols(tt)])
            copies("kv", 1, 1, lambda tt: v_a[:, tt_cols(tt)])
            act.wait_ge(t_done, 1)
            A(cache_akt[:, :], tps[:, 0, :], ACT.Copy).then_inc(t_read, 1)
            act.wait_ge(t_done, 2)
            A(v_tok[:, 0:5, :], tps[:, 0:5, :], ACT.Copy).then_inc(t_read, 1)
            act.wait_ge(t_done, 3)
            A(v_tok[:, 5:8, :], tps[:, 0:3, :], ACT.Copy)
            A(v_tok[0:TS, 8, :], tps[0:TS, 3, :], ACT.Copy).then_inc(t_read, 1)
            act.wait_ge(t_done, 4)
            A(k_out[:, 0, :], tps[:, 0, :], ACT.Copy)
            A(k_out[0:TS, 1, :], tps[0:TS, 1, :], ACT.Copy).then_inc(t_read, 1)
            act.wait_ge(sink_neg, 1)
            with act.Fori(0, 2) as j:
                for par in range(2):
                    t = j * 2 + par
                    copies("qa", t, (plan["qa"][0] + par) % 2, lambda tt: q_a[:, tt_cols(tt)], scale=QSCALE)
                    attention("A", t, True, None, lambda: None)
            act.wait_ge(mstate_ok, 80)
            g0, _, a0, _ = plan["gates"]
            for tt in range(NTT):
                act.wait_ge(proj_done, 3 * g0 + tt + 1)
                A(row["logi"][:, tt_cols(tt)], psum[0:4, tt, 0:TW], ACT.Identity, bias=gate_b[0:4, :])
                A(row["fg"][:, tt_cols(tt)], psum[32:36, tt, 0:TW], ACT.Identity, bias=gate_b[32:36, :]).then_inc(evac_act, 1)
            split_next(g0, g0 % 2)
            act.drain()
            A(row["t"][:, :], row["fg"][:, :], ACT.Abs)
            act.drain()
            A(row["t"][:, :], row["t"][:, :], ACT.Exp, scale=-1.0)
            act.drain()
            A(row["t"][:, :], row["t"][:, :], ACT.Ln, bias=1.0).then_inc(gate_e, 1)
            act.wait_ge(gate_rows, 1)
            A(brd[:, T:2 * T], brd[:, T:2 * T], ACT.Exp)
            A(brd[:, 2 * T:SELW], brd[:, 2 * T:SELW], ACT.Exp)
            A(row["enegm"][:, :], row["m"][:, :], ACT.Exp, scale=-1.0)
            A(row["wend"][:, :], row["wend"][:, :], ACT.Exp).then_inc(gate_rows, 1)
            act.wait_ge(stored, 32)
            act.wait_ge(cols_ok, 2)
            with act.Fori(0, H_B) as hd:
                g0, _, a0, _ = plan["heads"]
                for i in range(4):
                    slot = (g0 + i) % 2
                    for tt in range(NTT):
                        act.wait_ge(proj_done, hd * 12 + (3 * g0 + 3 * i + tt + 1))
                        if i < 2:
                            if tt == 0:
                                act.wait_ge(conv_free, hd + 1)
                                act.wait_ge(conv_done, one(hd * 2))
                            a = tt * TW
                            n = TW if tt < 2 else TW - TS
                            if tt < 2:
                                A(u_in[i][:, 3 + a:3 + a + n], psum[:, tt, 0:n], ACT.Copy).then_inc(evac_act, 1)
                            else:
                                A(u_in[i][:, 3 + a:3 + a + n], psum[:, tt, 0:n], ACT.Copy)
                                A(u_in[i][:, UW - TS:UW], psum[:, tt, n:TW], ACT.Copy).then_inc(evac_act, 1)
                        elif i == 2:
                            A(v_b[:, tt_cols(tt)], bank(tt, TW), ACT.Copy).then_inc(evac_act, 1)
                        else:
                            A(og_b[:, tt_cols(tt)], bank(tt, TW), ACT.Sigmoid).then_inc(evac_act, 1)
                    if i in (1, 2):
                        n = i - 1
                        act.wait_ge(conv_done, one(hd * 2 + (n + 1)))
                        A(qk_b[n][:, 0:TP], conv_t[:, 0:TP], ACT.Silu, bias=conv_h[:, 4, n:n + 1])
                        A(qk_b[n][:, TP:T], conv_t[:, TP + 3:CW], ACT.Silu, bias=conv_h[:, 4, n:n + 1]).then_inc(conv_in, 1)
                    split_next(hd * 4 + (g0 + i), slot)
                for c in range(NBLK + 1):
                    m = qrows(c)
                    act.wait_ge(arg_done, hd * 9 + (c + 1))
                    A(decay[0:m, c % 2, 0:m], psum[0:m, 5, 0:m], ACT.Exp, bias=cols_h[0:m, c, 0:1]).then_inc(decay_done, 1)
                    act.wait_ge(kv_done, hd * 9 + (c + 1))
                    A(k_w[0:m, c % 2, :], psum[0:m, 6, 0:128], ACT.Copy, scale=cols_h[0:m, c, 1:2])
                    A(v_x[0:m, c % 2, 0:128], psum[0:m, 6, 128:256], ACT.Copy).then_inc(kvx_done, 1)
                    if c >= 1:
                        num_out(hd, c - 1)
                num_out(hd, NBLK)
                act.wait_ge(ms9, hd + 1)
                A(rs9[:, :], rs9[:, :], ACT.Sqrt).then_inc(rt9, 1)
                act.wait_ge(memT_done, hd + 1)
                act.wait_ge(n_copied, hd + 1)
                A(mem_out[:, :, 0:128], psum[:, 6, 0:256].rearrange("p (i k) -> p i k", i=2), ACT.Copy).then_inc(memT_read, 1)
                act.wait_ge(og_done, one(hd + 1))
                A(o_hi[:, bass.ds(hd + 4, 1), :], ot_f[:, 0:T].unsqueeze(1), ACT.Copy).then_inc(oh9, 1)

            def out_tiles(layer):
                with act.Fori(0, KD // 2) as j:
                    for par in range(2):
                        i = j * 2 + par
                        copies(f"out{layer}", i, (plan[f"out{layer}"][0] + par) % 2,
                               lambda tt: y_mix[:, bass.ds(i, 1), tt_cols(tt)].rearrange("p o c -> p (o c)"))

            def ffn(layer):
                for n, ff in enumerate(FF_GROUPS):
                    g0, _, a0, d0 = plan[f"gu{layer}{n}"]
                    nff = 3 * (sum(FF_GROUPS) * layer + sum(FF_GROUPS[:n]))
                    with act.Fori(0, ff) as f:
                        for tt in range(NTT):
                            act.wait_ge(proj_done, f * 6 + (3 * g0 + tt + 1))
                            act.wait_ge(evac_dve, f * 3 + (d0 + CREDIT))
                            A(sil[:, tt_cols(tt)], bank(tt, TW), ACT.Silu).then_inc(evac_act, 1)
                        split_hi(f * 2 + (g0 + 2), g0 % 2)
                        for tt in range(NTT):
                            act.wait_ge(evac_dve, f * 3 + (d0 + CREDIT + tt + 1))
                            A(ff_hi[:, bass.ds(f, 1), tt_cols(tt)].rearrange("p o c -> p (o c)"), ffs[:, tt_cols(tt)], ACT.Copy
                              ).then_inc(ffhi_done, 1)
                        split_hi(f * 2 + (g0 + 3), (g0 + 1) % 2)
                    g0 = plan[f"down{layer}{n}"][0]
                    final = layer == 1 and n == len(FF_GROUPS) - 1
                    with act.Fori(0, KD // 2 - final) as j:
                        for par in range(2):
                            split_hi(j * 2 + (g0 + par + 2), (g0 + par) % 2)

            def residual(n, src, ready, s):
                square(n, src, ready)
                root(n)
                if s is None:
                    return
                act.wait_ge(derived, 2)
                square(n + 1, x, (x_new, 3 * (n // 2) + 1, True))
                root(n + 1)
                h_out((n + 1) // 2, s)

            out_tiles(0)
            residual(1, y_mix, (evac_act, CREDIT + plan["out0"][2] + 24, False), 1)
            ffn(0)
            last0 = plan["down04"]
            residual(3, y_ffn, (evac_dve, CREDIT + last0[3] + 24, False), 2)
            act.wait_ge(spilled, 32)
            g0, _, a0, _ = plan["qkv"]

            def qkv_step(hp, par, f, b):
                i, tt = f // 3, f % 3
                act.wait_ge(proj_done, hp * 9 + (3 * g0 + f + 1))
                A((q_c, k_c, v_c)[i][par][:, tt_cols(tt)], bank(b, TW), ACT.Copy, scale=QSCALE if i == 0 else 1.0).then_inc(evac_act, 1)
                if tt == NTT - 1:
                    split_hi(hp * 3 + (g0 + i + 2), (g0 + 3 * par + i) % 2)

            for f in range(9):
                qkv_step(0, 0, f, f % 3)

            def pair(hp, par, last):
                TD = lambda n: hp * 24 + (84 + n)

                def pre():
                    act.wait_ge(t_done, TD(1))
                    A(cache_kt[:, :], tps[:, 0:4, :].rearrange("p s c -> p (s c)"), ACT.Copy).then_inc(t_read, 1)
                    act.wait_ge(t_done, TD(2))
                    act.wait_ge(kv_stored, hp * 64 + 64)
                    A(v_tok[:, 0:5, :], tps[:, 0:5, :], ACT.Copy).then_inc(t_read, 1)
                    act.wait_ge(t_done, TD(3))
                    A(v_tok[:, 5:8, :], tps[:, 0:3, :], ACT.Copy)
                    A(v_tok[0:TS, 8, :], tps[0:TS, 3, :], ACT.Copy).then_inc(t_read, 1)
                    act.wait_ge(t_done, TD(4))
                    A(k_out[:, 0:4, :], tps[:, 0:4, :], ACT.Copy)
                    A(k_out[0:TS, 4, :], tps[0:TS, 4, :], ACT.Copy).then_inc(t_read, 1)

                fill = None if last else (lambda f: qkv_step(hp + 1, 1 - par, f, 0))
                attention("C", hp, False, fill, pre)

            with act.Fori(0, 3) as j:
                for par in range(2):
                    pair(j * 2 + par, par, False)
            pair(6, 0, False)
            pair(7, 1, True)
            out_tiles(1)
            residual(5, y_mix, (evac_act, CREDIT + plan["out1"][2] + 24, False), 3)
            ffn(1)
            residual(7, y_ffn, (evac_dve, CREDIT + plan["down14"][3] + 24, False), None)
            for b in range(NBLK + 1):
                m = qrows(b)
                act.wait_ge(yt_done, b + 1)
                if b >= 2:
                    act.wait_ge(y_st[b % 2], 16 * (b // 2))
                A(y_out[b % 2][0:m, :], psum[0:m, 4 * (b % 2):4 * (b % 2) + 2, :].rearrange("p b c -> p (b c)"), ACT.Copy).then_inc(yt_read, 1)

        @block.vector
        def _(dve):
            V = nc.vector
            for s in (ada_got, ol_done, w_done, og_done, ol9, conv_done, o_read):
                dve.sem_inc(s, 1)
            dve.sem_inc(ada_copied, 2)
            dve.sem_inc(evac_dve, CREDIT)
            dve.sem_inc(scores_read, CREDIT)

            def split_lo(g, slot):
                dve.wait_ge(hi_done, g + 1)
                V.tensor_tensor(w_lo[:, slot], w_raw[:, slot], w_hi[:, slot].bitcast(F32), ALU.subtract).then_inc(lo_done, 1)

            def split_next(g, slot):
                if isinstance(g, int) and g + 2 >= TILES:
                    return
                split_lo(g + 2, slot)

            dve.wait_ge(sink_ok, 16)
            V.tensor_scalar(neg_sink[:, :], neg_sink[:, :], -1.0, None, ALU.mult).then_inc(sink_neg, 1)
            dve.wait_ge(rev_ok, 16)
            pad = BW["C"] - 1 - MAX_REL
            V.tensor_scalar(rtable[:, 0:pad], table[:, 2 * MAX_REL:2 * MAX_REL + 1].to_broadcast([16, pad]), -1.0, None,
                            ALU.mult).then_inc(rev_built, 1)
            V.tensor_scalar(rtable[:, pad:REV], table[:, 2 * MAX_REL:2 * MAX_REL - (REV - pad):-1], -1.0, None,
                            ALU.mult).then_inc(rev_built, 1)
            for k in range(KD):
                for part in (1, 2):
                    dve.wait_ge(xt_done, 3 * k + part + 1)
                    n = 512 if part == 1 else TS
                    V.tensor_copy(x[:, k, 512 * part:512 * part + n], bank(part, n)).then_inc(xt_dve, 1)
            for g in range(2):
                split_lo(g, g)

            def ada_copy(q, m, b_):
                dve.wait_ge(ada_done, q * 4 + (4 + m + 1))
                V.tensor_copy(ada_row[:, m % 4, :], psum[0:2, b_, 0:256]).then_inc(ada_copied, 1)

            def ada_group(q, b_):
                dve.wait_ge(ada_t, q + 1)
                V.tensor_tensor(mod[:, bass.ds(q, 1)].rearrange("p o k r -> p (o k) r"),
                                psum[:, b_, 0:16].rearrange("p (k r) -> p k r", r=2),
                                prm2[:, bass.ds(q * 8, 8)].unsqueeze(2).to_broadcast([128, KD, 2]),
                                ALU.add).then_inc(ada_got, 1)

            def derive(s):
                gb = lambda n: prm[:, 16 + 8 * n:24 + 8 * n].unsqueeze(2).to_broadcast([128, KD, 2])
                return (lambda: V.scalar_tensor_tensor(pre_scale[:, s], mod[:, 3 * s + 1], 1.0, gb(2 * s), ALU.add, ALU.mult),
                        lambda: V.tensor_tensor(post_gate[:, s], mod[:, 3 * s + 2], gb(2 * s + 1), ALU.mult))

            def mean_square(n):
                for tt in range(NTT):
                    dve.wait_ge(ss_done, 3 * n + tt + 1)
                    V.tensor_scalar(rstd[:, tt], bank(tt, TW), 1.0 / D, EPS, ALU.mult, ALU.add).then_inc(ms_done, 1)

            def rms(n, tt, src):
                dve.wait_ge(rt_done, 3 * n + tt + 1)
                V.reciprocal(rstd[:, tt], rstd[:, tt])
                dve.drain()
                return V.tensor_tensor(norm_buf[:, tt], src[:, :, tt_cols(tt)],
                                       rstd[:, tt].unsqueeze(1).to_broadcast([128, KD, TW]), ALU.mult)

            def norm_h(n, i, meanwhile=None):
                mean_square(n)
                for tt in range(NTT):
                    rms(n, tt, x).then_inc(xn_done, 1)
                if meanwhile:
                    meanwhile()
                for tt in range(NTT):
                    dve.wait_ge(hh_done, 3 * i + tt + 1)
                    V.tensor_tensor(h_lo[:, :, tt_cols(tt)], norm_buf[:, tt], h_hi[:, :, tt_cols(tt)].bitcast(F32),
                                    ALU.subtract).then_inc(hl_done, 1)

            def first_modulation():
                with dve.Fori(0, 2) as q:
                    for u in range(4):
                        ada_copy(q, u, 3 + u % 2)
                    ada_group(q, 5)
                dve.drain()
                derive(0)[0]().then_inc(derived, 1)

            norm_h(0, 0, first_modulation)

            def residual(n, src, more):
                mean_square(n)
                for tt in range(NTT):
                    rms(n, tt, src)
                    dve.drain()
                    for k in range(KD):
                        for a, b, r in groups(tt):
                            c = slice(tt * TW + a, tt * TW + b)
                            last = V.scalar_tensor_tensor(x[:, k, c], norm_buf[:, tt, k, a:b], post_gate[:, n // 2, k, r:r + 1],
                                                          x[:, k, c], ALU.mult, ALU.add)
                    last.then_inc(x_new, 1)
                if more:
                    norm_h(n + 1, (n + 1) // 2)

            def attention(kind, it, sinks, fill):
                c = KINDS[kind]
                N = lambda n: it * 18 + (c["n0"] + n)
                lag, sb, probs = c["lag"], c["score_bufs"], c["probs"]
                for i in range(20 + lag):
                    if i >= lag + 2:
                        n = i - lag - 2
                        e, p = n // 9, n % 9
                        m = qrows(p)
                        s6 = slice(n % 6, n % 6 + 1)
                        dve.wait_ge(o_done, N(n) + 1)
                        src = sums
                        if sinks:
                            V.tensor_tensor(rsum[0:m, s6], sums[0:m, s6], sink_e[0:m, s6], ALU.add)
                            dve.drain()
                            src = rsum
                        V.reciprocal(rsum[0:m, s6], src[0:m, s6])
                        dve.drain()
                        V.tensor_scalar(o_tok[0:m, p, 64 * e:64 * e + 64], oacc[0:m, 0:64], rsum[0:m, s6], None,
                                        ALU.mult).then_inc(o_read, 1)
                    if i < 18:
                        n, e, p = i, i // 9, i % 9
                        m, (w, c0) = qrows(p), score_width(kind, p)
                        if p == 0:
                            if kind == "A":
                                dve.wait_ge(bias_raw[e], it * 16 + 16)
                            else:
                                dve.wait_ge(bias_ok[e], it + 1)
                        dve.wait_ge(scores, N(n) + 1)
                        b_ = score_bank(kind, n)
                        sc = psum[0:m, b_:b_ + 2, :].rearrange("p b c -> p (b c)")[:, 0:w]
                        mn = mins[0:m, n % 6:n % 6 + 1]
                        apart(dve)
                        op = V.tensor_tensor_reduce(out=probs[0:m, n % sb, 0:w], in0=sc, in1=neg_bias[0:m, e, c0:c0 + w],
                                                    scale=1.0, scalar=3.0e38, op0=ALU.add, op1=ALU.min, accum_out=mn)
                        if sinks:
                            dve.drain()
                            op = V.tensor_tensor(mn, mn, sink2[0:m, e:e + 1], ALU.min)
                        op.then_inc(scores_read, 1)
                    if fill:
                        fill(i)
                for r in range(2):
                    dve.wait_ge(oh_done, it * 2 + (c["o0"] + r + 1))
                    c0, w = (0, 640) if r == 0 else (640, T - 640)
                    sel = bass.ds(it, 1) if not isinstance(it, int) else slice(it, it + 1)
                    src = psum[:, 5:7, :].rearrange("p b c -> p (b c)")[:, 0:w].unsqueeze(1)
                    V.tensor_tensor(o_lo[:, sel, c0:c0 + w], src, o_hi[:, sel, c0:c0 + w].bitcast(F32), ALU.subtract
                                    ).then_inc(ol_done, 1)

            for i in range(2):
                split_next(i, i)
            dve.wait_ge(spilled, 16)
            with dve.Fori(0, 2) as j:
                for par in range(2):
                    t = j * 2 + par
                    V.tensor_copy(sink2[:, :].unsqueeze(2), neg_sink[:, :].rearrange("p (e t) -> p e t", e=2)[:, :, bass.ds(t, 1)])
                    split_lo(t + (plan["qa"][0] + 2), (plan["qa"][0] + par) % 2)
                    dve.drain()

                    def fill(i):
                        v = 20 * par + i
                        if i < 20 and v % 2 == 1:
                            ada_copy(j * 5, 8 + v // 2, 0)
                        if i <= 20 and v in (8, 16, 24, 32) or v == 40:
                            ada_group(j * 5 + (2 + v // 8 - 1), 4)

                    attention("A", t, True, fill)
            dve.drain()
            for s in range(4):
                if s:
                    derive(s)[0]()
                last = derive(s)[1]()
            last.then_inc(derived, 1)
            split_next(plan["gates"][0], plan["gates"][0] % 2)
            V.memset(row["carry"][:, :], 1.0)
            dve.drain()
            V.memset(row["carry"][:, 0:T:128], 0.0)
            dve.wait_ge(gate_e, 1)
            V.scalar_tensor_tensor(row["logf"][:, :], row["fg"][:, :], 0.0, row["t"][:, :], ALU.min, ALU.subtract)
            dve.drain()
            V.tensor_tensor_scan(row["b"][:, :], row["carry"][:, :], row["logf"][:, :], 0.0, ALU.mult, ALU.add)
            V.tensor_tensor_scan(row["m"][:, 0:TP], row["logf"][:, 0:TP], row["logi"][:, 0:TP], 0.0, ALU.add, ALU.max)
            V.tensor_tensor_scan(row["m"][:, TP:T], row["logf"][:, TP:T], row["logi"][:, TP:T], m_in[:, :], ALU.add, ALU.max)
            V.memset(m_prev[:, 0:1], 0.0)
            dve.drain()
            V.tensor_copy(m_prev[:, 1:NBLK], row["m"][:, 127:TP - 1:128])
            V.tensor_copy(m_prev[:, NBLK:NBLK + 1], m_in[:, :])
            V.tensor_tensor(row["g"][:, :], row["logi"][:, :], row["b"][:, :], ALU.subtract)
            V.tensor_tensor(brd[:, 0:T], row["b"][:, :], row["m"][:, :], ALU.subtract)
            dve.drain()
            V.tensor_copy(nm_end[:, 0:NBLK], brd[:, 127:TP:128])
            V.tensor_copy(nm_end[:, NBLK:NBLK + 1], brd[:, T - 1:T])
            dve.drain()
            V.tensor_tensor(brd[:, 2 * T:SELW], m_prev[:, :], nm_end[:, :], ALU.add)
            for dst, src, per in ((brd[:, T:2 * T], brd[:, 0:T], m_prev), (row["wend"][:, :], row["g"][:, :], nm_end)):
                V.tensor_tensor(dst[:, 0:TP].rearrange("p (b c) -> p b c", c=128), src[:, 0:TP].rearrange("p (b c) -> p b c", c=128),
                                per[:, 0:NBLK].unsqueeze(2).to_broadcast([4, NBLK, 128]), ALU.add)
                last = V.tensor_scalar(dst[:, TP:T], src[:, TP:T], per[:, NBLK:NBLK + 1], None, ALU.add)
            last.then_inc(gate_rows, 1)
            V.memset(cols[:, :, :, :], 0.0)
            dve.drain()
            dve.wait_ge(cols_t, 1)
            for b0, b1, m in ((0, NBLK, 128), (NBLK, NBLK + 1, TS)):
                src = psum[0:m, 5, 12 * b0:12 * b1].rearrange("p (b i h) -> p b i h", i=3, h=H_B)
                for i in range(3):
                    last = V.tensor_scalar(cols[0:m, b0:b1, i, :], src[:, :, i, :], KSCALE if i == 1 else 1.0, None, ALU.mult)
            last.then_inc(cols_ok, 1)
            dve.wait_ge(cols_t, 2)
            V.tensor_copy(mem_in[:, :, :].rearrange("p h k -> p (h k)"), bank(6)).then_inc(cols_ok, 1)
            dve.wait_ge(stored, 32)
            dve.wait_ge(gate_rows, 2)
            V.memset(h_tok[:, :, :], 0.0)
            V.memset(ssq[:, :], 0.0)
            V.memset(v_x[:, :, 128:129], 1.0)
            for i in range(2):
                V.memset(u_in[i][:, 0:3], 0.0)
            dve.drain()
            with dve.Fori(0, H_B) as hd:
                g0, _, a0, _ = plan["heads"]
                hs = bass.ds(hd, 1)
                dve.wait_ge(hT_done, one(hd * 3))
                dve.wait_ge(state_free, hd + 1)
                V.tensor_copy(onehot[:, :], ident[0:4, hs])
                cw = prm[:, 80:120].rearrange("p (j i h) -> p j i h", i=2, h=H_B)
                V.tensor_copy(conv_h[:, :, :].unsqueeze(3), cw[:, :, :, hs])
                V.tensor_copy(hnorm_h[:, :], prm[:, bass.ds(hd + 120, 1)])
                V.tensor_copy(cols_h[:, :, :].unsqueeze(3), cols[:, :, :, hs])
                cs_in = prm2[:, 96:120].rearrange("p (j i h) -> p i j h", i=2, h=H_B)
                for i in range(2):
                    V.tensor_copy(u_in[i][:, TP + 3:TP + 6].unsqueeze(2), cs_in[:, i, :, hs])
                V.memset(mem[0][:, 0:129], 0.0).then_inc(mem_done, 1)
                V.tensor_copy(mem[1][:, 0:128].unsqueeze(1), mem_in[:, hs, :])
                V.tensor_copy(mem[1][:, 128:129], prm[:, bass.ds(hd + 124, 1)]).then_inc(mem_done, 1)
                dve.drain()
                V.tensor_scalar(nm_h[:, :], brd[:, 0:T], onehot[:, :], None, ALU.mult)
                V.tensor_scalar(a_h[:, :], brd[:, T:2 * T], onehot[:, :], None, ALU.mult)
                V.tensor_scalar(ae_h[:, :], brd[:, 2 * T:SELW], onehot[:, :], None, ALU.mult).then_inc(head_set, 1)
                for i in range(4):
                    if i < 2:
                        dve.wait_ge(evac_act, hd * 12 + (CREDIT + a0 + 3 * (i + 1)))
                        dve.wait_ge(conv_in, one(hd * 2 + i))
                        V.tensor_scalar(conv_t[:, :], u_in[i][:, 0:CW], conv_h[:, 0, i:i + 1], None, ALU.mult)
                        for jj in range(1, CONV_W):
                            dve.drain()
                            last = V.scalar_tensor_tensor(conv_t[:, :], u_in[i][:, jj:jj + CW], conv_h[:, jj, i:i + 1], conv_t[:, :],
                                                          ALU.mult, ALU.add)
                        last.then_inc(conv_done, 1)
                    split_lo(hd * 4 + (g0 + i + 2), (g0 + i) % 2)
                dve.wait_ge(conv_in, one(hd * 2 + 1))
                for tt in range(NTT):
                    dve.wait_ge(abc_done, hd * 4 + (tt + 1))
                    V.tensor_tensor(qa_b[:, tt_cols(tt)], qk_b[0][:, tt_cols(tt)], bank(tt, TW), ALU.mult).then_inc(qa_done, 1)
                dve.wait_ge(abc_done, hd * 4 + 4)
                V.tensor_copy(aend_h[:, :], bank(3, NBLK + 1)).then_inc(qa_done, 1)
                dve.drain()

                def weights(c):
                    m = qrows(c)
                    dve.wait_ge(st_done, hd * 9 + (c + 1))
                    dve.wait_ge(decay_done, one(hd * 9 + (c + 1)))
                    V.scalar_tensor_tensor(wts[0:m, c % 2, 0:m], psum[0:m, 4, 0:m], KSCALE, decay[0:m, c % 2, 0:m],
                                           ALU.mult, ALU.mult).then_inc(w_done, 1)

                def finish(c):
                    m = qrows(c)
                    dve.wait_ge(num_done, hd * 9 + (c + 1))
                    d_ = den[0:m, c % 2:c % 2 + 1]
                    V.tensor_scalar(d_, psum[0:m, 7, 128:129], cols_h[0:m, c, 2:3], None, ALU.max)
                    dve.drain()
                    V.scalar_tensor_tensor(d_, psum[0:m, 7, 128:129], -1.0, d_, ALU.mult, ALU.max)
                    dve.drain()
                    V.reciprocal(rden[0:m, c % 2:c % 2 + 1], d_).then_inc(den_done, 1)
                    mm = mem[c // NBLK]
                    dve.wait_ge(upd_done, hd * 9 + (c + 1))
                    V.scalar_tensor_tensor(mm[:, 0:129], mm[:, 0:129], aend_h[:, c:c + 1], psum[:, 3, 0:129],
                                           ALU.mult, ALU.add).then_inc(mem_done, 1)

                weights(0)
                for c in range(NBLK + 1):
                    if c < NBLK:
                        weights(c + 1)
                    finish(c)
                dve.drain()
                for i in range(2):
                    last = V.tensor_copy(mem_out[:, i, 128:129], mem[i][:, 128:129])
                last.then_inc(n_copied, 1)
                dve.wait_ge(num_read, one(hd * 9 + 9))
                V.tensor_scalar(rs9[:, :], ssq[:, :], 1.0 / DH_B, EPS, ALU.mult, ALU.add).then_inc(ms9, 1)
                dve.wait_ge(rt9, hd + 1)
                V.reciprocal(rs9[:, :], rs9[:, :])
                dve.drain()
                V.tensor_tensor(h_tok[:, :, :], h_tok[:, :, :], rs9[:, :].unsqueeze(2).to_broadcast([128, NBLK + 1, 128]),
                                ALU.mult).then_inc(hn_done, 1)
                for r, (c0, w, b_) in enumerate(((0, 512, 4), (512, 512, 5), (TP, TS, 3))):
                    dve.wait_ge(hT_done, one(hd * 3 + (r + 1)))
                    last = V.scalar_tensor_tensor(ot_f[:, c0:c0 + w], psum[:, b_, 0:w], hnorm_h[:, :], og_b[:, c0:c0 + w],
                                                  ALU.mult, ALU.mult)
                last.then_inc(og_done, 1)
                dve.wait_ge(oh9, hd + 1)
                V.tensor_tensor(o_lo[:, bass.ds(hd + 4, 1), :], ot_f[:, 0:T].unsqueeze(1), o_hi[:, bass.ds(hd + 4, 1), :].bitcast(F32),
                                ALU.subtract).then_inc(ol9, 1)

            def out_tiles(layer):
                with dve.Fori(0, KD // 2) as j:
                    for par in range(2):
                        split_lo(j * 2 + (plan[f"out{layer}"][0] + par + 2), (plan[f"out{layer}"][0] + par) % 2)

            def ffn(layer):
                for n, ff in enumerate(FF_GROUPS):
                    g0, _, a0, d0 = plan[f"gu{layer}{n}"]
                    nff = 3 * (sum(FF_GROUPS) * layer + sum(FF_GROUPS[:n]))
                    with dve.Fori(0, ff) as f:
                        split_lo(f * 2 + (g0 + 2), g0 % 2)
                        for tt in range(NTT):
                            dve.wait_ge(proj_done, f * 6 + (3 * g0 + 3 + tt + 1))
                            dve.wait_ge(evac_act, f * 3 + (a0 + CREDIT + tt + 1))
                            V.tensor_tensor(ffs[:, tt_cols(tt)], sil[:, tt_cols(tt)], bank(tt, TW), ALU.mult).then_inc(evac_dve, 1)
                        for tt in range(NTT):
                            dve.wait_ge(ffhi_done, f * 3 + (nff + tt + 1))
                            sel = bass.ds(f, 1)
                            V.tensor_tensor(ff_lo[:, sel, tt_cols(tt)], ffs[:, tt_cols(tt)].unsqueeze(1), ff_hi[:, sel, tt_cols(tt)].bitcast(F32),
                                            ALU.subtract).then_inc(fflo_done, 1)
                        split_lo(f * 2 + (g0 + 3), (g0 + 1) % 2)
                    g0 = plan[f"down{layer}{n}"][0]
                    final = layer == 1 and n == len(FF_GROUPS) - 1

                    def down(j, par, split):
                        for tt in range(NTT):
                            dve.wait_ge(proj_done, j * 6 + (3 * g0 + 3 * par + tt + 1))
                            dst = y_ffn[:, bass.ds(j * 2 + par, 1) if not isinstance(j, int) else slice(2 * j + par, 2 * j + par + 1), tt_cols(tt)]
                            src = bank(tt, TW).unsqueeze(1)
                            if n == 0:
                                V.tensor_copy(dst, src).then_inc(evac_dve, 1)
                            else:
                                V.tensor_tensor(dst, dst, src, ALU.add).then_inc(evac_dve, 1)
                        if split:
                            split_lo(j * 2 + (g0 + par + 2), (g0 + par) % 2)

                    with dve.Fori(0, KD // 2 - final) as j:
                        for par in range(2):
                            down(j, par, True)
                    if final:
                        for par in range(2):
                            down(KD // 2 - 1, par, False)

            out_tiles(0)
            dve.wait_ge(x_loaded, 16)
            residual(1, y_mix, True)
            ffn(0)
            residual(3, y_ffn, True)
            g0 = plan["qkv"][0]
            for i in range(3):
                split_lo(g0 + i + 2, (g0 + i) % 2)
            dve.wait_ge(spilled, 32)

            def pair(hp, par, last):
                def fill(i):
                    f = i // 2
                    if i % 6 == 5 and i < 18:
                        split_lo(hp * 3 + (3 + g0 + f // 3 + 2), (g0 + 3 * (1 - par) + f // 3) % 2)
                attention("C", hp, False, None if last else fill)

            with dve.Fori(0, 3) as j:
                for par in range(2):
                    pair(j * 2 + par, par, False)
            pair(6, 0, False)
            pair(7, 1, True)
            out_tiles(1)
            dve.wait_ge(x_loaded, 32)
            residual(5, y_mix, True)
            ffn(1)
            residual(7, y_ffn, False)


_OUTS = [
    ("y_prompt", (1, TP, D)), ("y_sample", (1, TS, D)),
    ("pa_k", (1, 1, 128, 2, 64)), ("pa_v", (1, 1, 128, 2, 64)), ("pb_c", (1, 1, 4, 128, 128)), ("pb_n", (1, 1, 4, 128)),
    ("pb_m", (1, 1, 4)), ("pb_conv", (1, 1, 3, 1024)), ("pc_k", (1, 1, 512, 16, 64)), ("pc_v", (1, 1, 512, 16, 64)),
    ("sa_k", (1, 1, 32, 2, 64)), ("sa_v", (1, 1, 32, 2, 64)), ("sb_c", (1, 1, 4, 128, 128)), ("sb_n", (1, 1, 4, 128)),
    ("sb_m", (1, 1, 4)), ("sb_conv", (1, 1, 3, 1024)), ("sc_k", (1, 1, 32, 16, 64)), ("sc_v", (1, 1, 32, 16, 64)),
]


def constants():
    s, t = np.arange(128)[:, None], np.arange(128)[None, :]
    causal = np.where(s <= t, 0.0, -BIG).astype(np.float32)
    i, j = np.arange(128)[:, None], np.arange(256)[None, :]
    seen = np.where(i < 64, j < 192, j >= 64)
    slope = np.exp2(-8.0 * np.arange(1, HQ_A + 1) / HQ_A)[:, None, None]
    alibi = np.where(seen, slope * np.abs(128 + i - j), BIG).astype(np.float32)
    return dict(ident=np.eye(128, dtype=np.float32), causal=causal, alibi=alibi)


def kernel(**inputs):
    import concourse.bacc as bacc
    from concourse.bass_utils import run_bass_kernel_spmd

    nc = bacc.Bacc("TRN2", target_bir_lowering=False, num_devices=1, dynamic_dma_scratch_size=DMA_RING)
    arrays, ins, outs = {}, {}, {}
    for name, a in {**inputs, **constants()}.items():
        a = np.ascontiguousarray(a)
        arrays[f"in_{name}"] = a
        ins[name] = nc.dram_tensor(f"in_{name}", a.shape, mybir.dt.from_np(a.dtype), kind="ExternalInput").ap()
    for name, shape in _OUTS:
        outs[name] = nc.dram_tensor(f"out_{name}", shape, F32, kind="ExternalOutput").ap()
    build(nc, ins, outs)
    r = run_bass_kernel_spmd(nc, [arrays], core_ids=[0])
    return tuple(r.results[0][f"out_{name}"] for name, _ in _OUTS)
```

```python
import concourse.bass as bass
from concourse import mybir
from contextlib import ExitStack
import numpy as np

F32 = mybir.dt.float32
F32R = mybir.dt.float32r
ALU = mybir.AluOpType
ACT = mybir.ActivationFunctionType

D = 1024
TP, TS = 1024, 32
T = TP + TS
KD = D // 128
NTT = 3
TW = T // NTT
NBLK = TP // 128
HQ_A, HKV_A, HD = 8, 2, 64
H_B, DH_B = 4, 128
H_C = 16
W_A = HQ_A * HD
W_B = H_B * DH_B
COL_KA, COL_VA = W_A, W_A + 128
COL_QKB = W_A + 256
COL_VB = COL_QKB + 2 * W_B
COL_IG = COL_VB + W_B
COL_FG = COL_IG + H_B
COL_OG = COL_FG + H_B
D_FF = 2816
FF_GROUPS = [5, 5, 4, 4, 4]
PREV_C = 512
MAX_REL = 256
EPS = 1e-6
BIG = 1e30
QSCALE = -(HD ** -0.5)
KSCALE = DH_B ** -0.5
REV = 768
CONV_W = 4
DMA_RING = 2048
UW = 3 + TP + 3 + TS
CW = UW - 3

BW = {"A": 256, "C": 640}
CREDIT = 3


def tile_plan():
    plan, g, a, d = {}, 0, 0, 0

    def add(name, n, by):
        nonlocal g, a, d
        plan[name] = (g, n, a, d)
        g += n
        a += 3 * n if by == "act" else 3 * (n // 2) if by == "both" else 0
        d += 3 * n if by == "dve" else 3 * (n // 2) if by == "both" else 0

    for layer in range(2):
        if layer == 0:
            add("kv", 2, "act")
            add("qa", 4, "act")
            add("gates", 1, "act")
            add("heads", 4 * H_B, "act")
        else:
            add("qkv", 3 * KD, "act")
        add(f"out{layer}", KD, "act")
        for n, ff in enumerate(FF_GROUPS):
            add(f"gu{layer}{n}", 2 * ff, "both")
            add(f"down{layer}{n}", KD, "dve")
    return plan, g


def build(nc, ins, outs):
    I, O = ins, outs
    plan, TILES = tile_plan()
    ctx = ExitStack()
    with ctx:
        def at(name, shape, offset, dt=F32):
            return nc.alloc_sbuf_tensor_at(name, shape, dt, offset=offset)

        HB_ = KD * T * 4
        B0 = (nc.sbuf_base + 31) // 32 * 32
        h_hi = at("h_hi", [128, KD, T], B0, F32R)
        h_lo = at("h_lo", [128, KD, T], B0 + HB_, F32R)
        y_mix = at("y_mix", [128, KD, T], B0)
        R1 = B0 + 2 * HB_
        FFM = max(FF_GROUPS)
        ff_hi = at("ff_hi", [128, FFM, T], R1, F32R)
        ff_lo = at("ff_lo", [128, FFM, T], R1 + FFM * T * 4, F32R)
        norm_buf = at("norm_buf", [128, KD, T], B0 + HB_)
        o_hi = at("o_hi", [128, KD, T], R1, F32R)
        o_lo = at("o_lo", [128, KD, T], R1 + HB_, F32R)
        YF = R1 + 6 * T * 4 * 2
        y_ffn = at("y_ffn", [128, KD, T], YF)
        x = at("x", [128, KD, T], YF + HB_)
        XE = YF + 2 * HB_
        w_raw = at("w_raw", [128, 2, KD, 128], XE)
        w_hi = at("w_hi", [128, 2, KD, 128], XE + 8192, F32R)
        w_lo = at("w_lo", [128, 2, KD, 128], XE + 16384, F32R)
        SM = XE + 24576
        top = [SM]

        def small(name, shape, dt=F32):
            n = 4 * int(np.prod(shape[1:]))
            t = at(name, shape, top[0], dt)
            top[0] += (n + 31) // 32 * 32
            assert top[0] <= 229368, (name, top[0])
            return t

        ident = small("ident", [128, 128])
        ones = small("ones", [128, 128])
        prm = small("prm", [128, 128])
        prm2 = small("prm2", [128, 120])
        silu_c = small("silu_c", [128, KD, 2])
        mod = small("mod", [128, 12, KD, 2])
        pre_scale = small("pre_scale", [128, 4, KD, 2])
        post_gate = small("post_gate", [128, 4, KD, 2])
        mins = small("mins", [128, 6])
        sums = small("sums", [128, 6])
        rsum = small("rsum", [128, 6])
        neg_sink = small("neg_sink", [128, HQ_A])
        sink2 = small("sink2", [128, 2])
        sink_e = small("sink_e", [128, 6])
        F0 = top[0]
        sil = at("sil", [128, T], F0)
        ffs = at("ffs", [128, T], F0 + 4 * T)
        rstd = at("rstd", [128, NTT, TW], F0 + 8 * T)
        sq_sum = sil
        sq_ring = [at(f"sq_ring{i}", [128, TW], F0 + 4 * T + 4 * TW * i) for i in range(3)]
        conv_t = at("conv_t", [128, CW], F0)
        assert F0 + 12 * T <= 229368, F0
        ada_row = at("ada_row", [2, 4, 256], F0)

        MX = R1 + 2 * HB_
        mx = [MX]

        def scratch(name, shape, dt=F32):
            n = 4 * int(np.prod(shape[1:]))
            t = at(name, shape, mx[0], dt)
            mx[0] += (n + 31) // 32 * 32
            assert mx[0] <= XE, (name, mx[0] - XE)
            return t

        neg_bias = scratch("neg_bias", [128, 2, 640])
        probs_a = at("probs_a", [128, 3, 256], mx[0])
        probs = scratch("probs", [128, 2, 640])
        probs_t = scratch("probs_t", [128, 2, 5, 128])
        o_tok = scratch("o_tok", [128, NBLK + 1, 128])
        v_tok = scratch("v_tok", [128, NBLK + 2, 128])
        k_out = scratch("k_out", [128, 5, 128])
        mark = mx[0]
        q_c = [at("q_c0", [128, T], F0), scratch("q_c1", [128, T])]
        k_c = [at("k_c0", [128, T], F0 + 4 * T), scratch("k_c1", [128, T])]
        v_c = [at("v_c0", [128, T], F0 + 8 * T), scratch("v_c1", [128, T])]
        cache_kt = scratch("cache_kt", [128, 512])
        cache_k = [scratch(f"cache_k{p}", [128, 4, 128]) for p in range(2)]
        cache_v = [scratch(f"cache_v{p}", [128, 4, 128]) for p in range(2)]
        mx[0] = mark
        q_a = scratch("q_a", [128, T])
        k_a = scratch("k_a", [128, T])
        v_a = scratch("v_a", [128, T])
        cache_ak = scratch("cache_ak", [128, 128])
        cache_akt = scratch("cache_akt", [128, 128])
        mx[0] = MX
        u_in = [scratch("u_q", [128, UW]), scratch("u_k", [128, UW])]
        qk_b = [scratch("q_b", [128, T]), scratch("k_b", [128, T])]
        v_b = scratch("v_b", [128, T])
        og_b = scratch("og_b", [128, T])
        SELW = 2 * T + NBLK + 1
        brd = scratch("brd", [4, SELW])
        nm_h = at("nm_h", [4, T], R1 + HB_ + 7 * T * 4)
        a_h = at("a_h", [4, T], R1 + 7 * T * 4)
        h_tok = scratch("h_tok", [128, NBLK + 1, 128])
        qa_b = at("qa_b", [128, T], F0 + 8 * T)
        ot_f = conv_t
        FB = F0 + 4256
        wts = at("wts", [128, 2, 128], FB)
        decay = at("decay", [128, 2, 128], FB + 1024)
        k_w = at("k_w", [128, 2, 128], FB + 2048)
        v_x = at("v_x", [128, 2, 132], FB + 3072)
        assert FB + 3072 + 1056 <= F0 + 8 * T
        row = {n: at("row_" + n, [4, T], R1 + 4 * T * (4 + i)) for i, n in enumerate(["logi", "fg", "logf", "m"])}
        row |= {n: at("row_" + n, [4, T], R1 + HB_ + 4 * T * (4 + i)) for i, n in enumerate(["g", "b", "carry", "enegm"])}
        row["t"] = at("row_t", [4, T], F0 + 8 * T)
        row["wend"] = at("row_wend", [4, T], F0 + 4256)
        XT = R1
        x_in = at("x_in", [128, NBLK + 1, D], XT)
        prm_in = at("prm_in", [128, 128], XT + (NBLK + 1) * D * 4)
        prm2_in = at("prm2_in", [128, 128], XT + (NBLK + 1) * D * 4 + 512)
        ADB = KD * 256 * 4
        ada_s = [at(f"ada_s{u}", [128, KD, 256], YF + ADB * u) for u in range(4)]
        ada_m = [at(f"ada_m{u}", [128, KD, 256], (YF, R1 + HB_ // 2)[u // 2] + ADB * (u % 2)) for u in range(4)]
        y_out = [at(f"y_out{p}", [128, D], R1 + 4096 * p) for p in range(2)]

        MS = XE - 10240
        mS = [MS]

        def state(name, shape):
            n = 4 * int(np.prod(shape[1:]))
            t = at(name, shape, mS[0])
            mS[0] += (n + 31) // 32 * 32
            assert mS[0] <= XE
            return t

        mem = [state("mem_prompt", [128, 132]), state("mem_sample", [128, 132])]
        mem_in = state("mem_in", [128, H_B, 128])
        mem_out = state("mem_out", [128, 2, 132])
        cols = state("cols", [128, NBLK + 1, 3, H_B])
        cols_h = state("cols_h", [128, NBLK + 1, 3])
        conv_h = state("conv_h", [128, 5, 2])
        hnorm_h = state("hnorm_h", [128, 1])
        onehot = state("onehot", [4, 1])
        ae_h = state("ae_h", [4, NBLK + 1])
        rden = state("rden", [128, 2])
        junk = state("junk", [128, 2, 128])
        aend_h = state("aend_h", [128, NBLK + 1])
        ssq = state("ssq", [128, NBLK + 1])
        rs9 = state("rs9", [128, NBLK + 1])
        den = state("den", [128, 2])
        m_in = state("m_in", [4, 1])
        gate_b = state("gate_b", [36, 1])
        m_prev = state("m_prev", [4, NBLK + 1])
        nm_end = state("nm_end", [4, NBLK + 1])
        cmask = state("cmask", [128, 128])
        table = at("table", [16, 2 * MAX_REL + 1], XT + (NBLK + 1) * D * 4 + 1024)
        rtable = at("rtable", [16, REV], XT + (NBLK + 1) * D * 4 + 4096)
        assert mx[0] <= MS, (mx[0], MS)

        psum = ctx.enter_context(nc.psum_tensor("psum", [128, 8, 512], F32))
        def bank(b, w=512, rows=128):
            return psum[0:rows, b, 0:w]

        tps = psum[:, 5:7, :].rearrange("p b (s c) -> p (b s) c", c=128)
        oacc = psum[:, 7, :]

        x_spill = nc.dram_tensor("x_spill", [128, KD * T], F32, kind="Internal")
        rev_dram = nc.dram_tensor("rev_dram", [16, REV], F32, kind="Internal")

        bias_dram = nc.dram_tensor("bias_dram", [H_C, 128, 640], F32, kind="Internal")

        def sem(name):
            return ctx.enter_context(nc.semaphore(name))

        par_in, par2_in, misc_in, x_in_sem = sem("par_in"), sem("par2_in"), sem("misc_in"), sem("x_in_sem")
        const_done, rows_t, rows_got = sem("const_done"), sem("rows_t"), sem("rows_got")
        c_ready, ada_done, ada_got, derived = sem("c_ready"), sem("ada_done"), sem("ada_got"), sem("derived")
        ada_copied, ada_t = sem("ada_copied"), sem("ada_t")
        ada_loaded = [sem(f"ada_loaded{i}") for i in range(4)]
        xt_done, xt_act, xt_dve = sem("xt_done"), sem("xt_act"), sem("xt_dve")
        w_loaded = [sem("w_loaded0"), sem("w_loaded1")]
        hi_done, lo_done = sem("hi_done"), sem("lo_done")
        proj_done, evac_act, evac_dve = sem("proj_done"), sem("evac_act"), sem("evac_dve")
        ffhi_done, fflo_done = sem("ffhi_done"), sem("fflo_done")
        sq_done, ss_done, ms_done, rt_done = sem("sq_done"), sem("ss_done"), sem("ms_done"), sem("rt_done")
        x_new, xn_done, hh_done, hl_done = sem("x_new"), sem("xn_done"), sem("hh_done"), sem("hl_done")
        sqy_done, acc_done = sem("sqy_done"), sem("acc_done")
        spilled, x_loaded = sem("spilled"), sem("x_loaded")
        scores, scores_read, p_done = sem("scores"), sem("scores_read"), sem("p_done")
        t_done, t_read, o_done, o_read = sem("t_done"), sem("t_read"), sem("o_done"), sem("o_read")
        oh_done, ol_done = sem("oh_done"), sem("ol_done")
        bias_raw, bias_ok = [sem("bias_raw0"), sem("bias_raw1")], [sem("bias_ok0"), sem("bias_ok1")]
        ck_in, cv_in = [sem("ck_in0"), sem("ck_in1")], [sem("cv_in0"), sem("cv_in1")]
        kv_stored, stored, sink_ok, rev_ok, rev_st = sem("kv_stored"), sem("stored"), sem("sink_ok"), sem("rev_ok"), sem("rev_st")
        rev_built, sink_neg, toeplitz = sem("rev_built"), sem("sink_neg"), sem("toeplitz")
        gate_raw, gate_e, gate_rows = sem("gate_raw"), sem("gate_e"), sem("gate_rows")
        gate_dve, cols_t, cols_ok = sem("gate_dve"), sem("cols_t"), sem("cols_ok")
        conv_in, conv_done, conv_stored, head_set = sem("conv_in"), sem("conv_done"), sem("conv_stored"), sem("head_set")
        abc_done, qa_done = sem("abc_done"), sem("qa_done")
        st_done, arg_done, kv_done = sem("st_done"), sem("arg_done"), sem("kv_done")
        decay_done, kvx_done, w_done = sem("decay_done"), sem("kvx_done"), sem("w_done")
        num_done, den_done, num_read = sem("num_done"), sem("den_done"), sem("num_read")
        upd_done, mem_done = sem("upd_done"), sem("mem_done")
        ms9, rt9, hn_done, hT_done, og_done, oh9, ol9 = (sem(n) for n in (
            "ms9", "rt9", "hn_done", "hT_done", "og_done", "oh9", "ol9"))
        memT_done, memT_read, n_copied, state_st = sem("memT_done"), sem("memT_read"), sem("n_copied"), sem("state_st")
        mstate_ok, conv_free, state_free = sem("mstate_ok"), sem("conv_free"), sem("state_free")
        yt_done, yt_read, y_st = sem("yt_done"), sem("yt_read"), [sem("y_st0"), sem("y_st1")]

        ctx.enter_context(nc.allow_non_contiguous_dma(reason="three frames of conv state, one column of n"))
        block = ctx.enter_context(nc.Block())

        def apart(eng):
            eng.sem_inc(waited[eng], 1)

        waited = {nc.tensor: sem("waited_pe"), nc.vector: sem("waited_dve"), nc.gpsimd: sem("waited_pool")}

        def one(n):
            return n + 1

        PAIR = [(tt, par) for tt in range(NTT) for par in range(2)]

        def tt_cols(tt):
            return slice(tt * TW, (tt + 1) * TW)

        def groups(tt):
            if tt < NTT - 1:
                return [(0, TW, 0)]
            return [(0, TW - TS, 0), (TW - TS, TW, 1)]

        def qrows(p):
            return 128 if p < NBLK else TS

        def score_width(kind, p):
            if p == NBLK:
                return BW[kind] - 128 + TS, 0
            w = min(BW[kind], 128 * (p + 1))
            return w, BW[kind] - w

        def key_blocks(kind, p):
            if p == NBLK:
                return [(("cache", i), 128) for i in range(BW[kind] // 128 - 1)] + [(NBLK, TS)]
            n = score_width(kind, p)[0] // 128
            return [(b, 128) for b in range(p - n + 1, p + 1)]

        KINDS = {
            "A": dict(n0=0, r0=4, o0=0, pre=0, lag=2, score_bufs=3, fill0=0, probs=probs_a),
            "C": dict(n0=72, r0=4 + 72, o0=8, pre=4, lag=1, score_bufs=2, fill0=5, probs=probs),
        }

        def one_of(i, first=0):
            return slice(first + i, first + i + 1) if isinstance(i, int) else bass.ds(i + first, 1)

        def num_bank(c):
            return 0 if c % 2 else 7

        def score_bank(kind, n):
            return 1 + n % 3 if kind == "A" else 1 + 2 * (n % 2)

        @block.sync
        def _(sp):
            def rows_in(dst, r, src):
                n = src.shape[0]
                sp.dma_start(dst[r:r + n, :], src).then_inc(par_in if dst is prm_in else par2_in, 16)
                return r + n

            v128 = lambda a, pat: a.rearrange(pat, c=128)
            r = rows_in(prm_in, 0, v128(I["c_prompt"], "b (k c) -> (b k) c"))
            r = rows_in(prm_in, r, v128(I["c_sample"], "b (k c) -> (b k) c"))
            r = rows_in(prm_in, r, v128(I["norm_g"], "l n (k c) -> (l n k) c"))
            r = rows_in(prm_in, r, v128(I["conv_w_b"], "l j (k c) -> (l j k) c"))
            r = rows_in(prm_in, r, v128(I["conv_b_b"], "l (k c) -> (l k) c"))
            r = rows_in(prm_in, r, v128(I["hnorm_b"], "l (k c) -> (l k) c"))
            r = rows_in(prm_in, r, I["state_b_n"].rearrange("l b h c -> (l b h) c"))
            assert r == 128
            r = rows_in(prm2_in, 0, v128(I["b_ada"], "l (k c) -> (l k) c"))
            r = rows_in(prm2_in, r, v128(I["state_b_conv"], "l b j (k c) -> (l b j k) c"))
            assert r == 120
            sp.dma_start(ident[:, :], I["ident"]).then_inc(misc_in, 16)
            sp.dma_start(table[:, :], I["relbias_c"][0]).then_inc(rev_ok, 16)
            ada = I["w_ada"].rearrange("l (k p) n -> l p k n", p=128)
            xp = I["x_prompt"].rearrange("o (b p) d -> p (o b) d", p=128)
            for half in range(2):
                sp.dma_start(x_in[:, 4 * half:4 * half + 4, :], xp[:, 4 * half:4 * half + 4, :]).then_inc(x_in_sem, 16)
            sp.dma_start(x_in[0:TS, NBLK, :], I["x_sample"][0]).then_inc(x_in_sem, 16)
            def load(g, parts):
                if not (isinstance(g, int) and g < 2):
                    sp.wait_ge(lo_done, g - 1)
                for dst, src in parts:
                    sp.dma_start(dst, src).then_inc(w_loaded[parts_slot[0]], 16)

            parts_slot = [0]

            def plain(w, slot, cols, kt):
                parts_slot[0] = slot
                cut = {8: (0, 3, 6, 8), 5: (0, 2, 4, 5), 4: (0, 1, 2, 4)}[kt]
                return [(w_raw[:, slot, a:b, :], w[:, a:b, cols]) for a, b in zip(cut, cut[1:])]

            view = lambda a: a.rearrange("(k p) n -> p k n", p=128)
            w_ab = view(I["w_in_ab"][0])
            def ada_load(ring, layer, q, n):
                for u in range(4):
                    sp.wait_ge(ada_done, q * 4 + (n + u + 1))
                    c = bass.ds(q * 1024 + ((n + u) * 256 - layer * 6 * D), 256)
                    sp.dma_start(ring[u][:, :, :], ada[layer][:, :, c]).then_inc(ada_loaded[u], 16)

            ada_load(ada_s, 0, 0, 0)
            for i, c in enumerate((COL_KA, COL_VA)):
                load(i, plain(w_ab, i, slice(c, c + 128), KD))
            ada_load(ada_s, 0, 1, 0)
            sp.wait_ge(rev_built, 2)
            sp.dma_start(rev_dram.ap(), rtable[:, :]).then_inc(rev_st, 16)
            sp.wait_ge(rev_st, 16)
            sp.dma_start(bias_dram.ap(), bass.AP(rev_dram, 127, [[REV, H_C], [-1, 128], [1, 640]])).then_inc(toeplitz, 16)
            def q_tile(t):
                g = plan["qa"][0] + t
                slot = g % 2
                parts_slot[0] = slot
                c0, c1 = slice(t * HD, t * HD + HD), slice(t * HD + 256, t * HD + 256 + HD)
                load(g, [(w_raw[:, slot, :, 0:HD], w_ab[:, :, c0]),
                         (w_raw[:, slot, 0:4, HD:128], w_ab[:, 0:4, c1]),
                         (w_raw[:, slot, 4:8, HD:128], w_ab[:, 4:8, c1])])

            def gates_tile():
                g = plan["gates"][0]
                parts_slot[0] = g % 2
                load(g, [(w_raw[:, g % 2, :, 0:4], w_ab[:, :, COL_IG:COL_IG + 4]),
                         (w_raw[:, g % 2, :, 32:36], w_ab[:, :, COL_FG:COL_FG + 4]),
                         (w_raw[:, g % 2, :, 64:68], w_ab[:, :, COL_FG:COL_FG + 4])])

            def head_tile(h, i):
                g0 = plan["heads"][0]
                c = (COL_QKB, COL_QKB + W_B, COL_VB, COL_OG, COL_QKB + 128)[i]
                load(h * 4 + (g0 + i), plain(w_ab, (g0 + i) % 2, bass.ds(h * 128 + c, 128) if not isinstance(h, int)
                                             else slice(h * 128 + c, h * 128 + c + 128), KD))

            q_tile(0)
            q_tile(1)
            ada_load(ada_m, 0, 0, 8)
            q_tile(2)
            ada_load(ada_m, 0, 0, 12)
            q_tile(3)
            with sp.Fori(1, 3) as q:
                ada_load(ada_m, 0, q, 12)
            ada_load(ada_m, 1, 3, 12)
            gates_tile()
            with sp.Fori(4, 6) as q:
                ada_load(ada_m, 1, q, 12)
            head_tile(0, 0)
            with sp.Fori(6, 9) as q:
                ada_load(ada_m, 1, q, 12)
            with sp.Fori(0, H_B - 1) as hd:
                for i in range(1, 5):
                    head_tile(hd, i)
            for i in range(1, 4):
                head_tile(H_B - 1, i)

            def out_tiles(layer):
                g0 = plan[f"out{layer}"][0]
                w = view(I["w_out_c"][0]) if layer else None
                with sp.Fori(0, KD // 2) as j:
                    for par in range(2):
                        slot = (g0 + par) % 2
                        c = bass.ds(j * 256 + par * 128, 128)
                        if layer:
                            parts = plain(w, slot, c, KD)
                        else:
                            parts_slot[0] = slot
                            wo = I["w_out_ab"][0]
                            lo_h = wo[0:256, :].rearrange("(k p) n -> p k n", p=HD)
                            hi_h = wo[256:512, :].rearrange("(k p) n -> p k n", p=HD)
                            rest = wo[512:1024, :].rearrange("(k p) n -> p k n", p=128)
                            parts = [(w_raw[0:HD, slot, 0:4, :], lo_h[:, :, c]),
                                     (w_raw[HD:128, slot, 0:4, :], hi_h[:, :, c]),
                                     (w_raw[:, slot, 4:8, :], rest[:, :, c])]
                        load(j * 2 + (g0 + par), parts)

            def ffn_tiles(layer):
                wg, wu = view(I["w_ffn_gate"][layer]), view(I["w_ffn_up"][layer])
                f0 = 0
                for n, ff in enumerate(FF_GROUPS):
                    g0 = plan[f"gu{layer}{n}"][0]
                    with sp.Fori(0, ff) as f:
                        c = bass.ds(f * 128 + f0 * 128, 128)
                        load(f * 2 + g0, plain(wg, g0 % 2, c, KD))
                        load(f * 2 + (g0 + 1), plain(wu, (g0 + 1) % 2, c, KD))
                    wd = view(I["w_ffn_down"][layer][f0 * 128:(f0 + ff) * 128, :])
                    g0 = plan[f"down{layer}{n}"][0]
                    with sp.Fori(0, KD // 2) as j:
                        for par in range(2):
                            load(j * 2 + (g0 + par), plain(wd, (g0 + par) % 2, bass.ds(j * 256 + par * 128, 128), ff))
                    f0 += ff

            out_tiles(0)
            ffn_tiles(0)
            w_c = view(I["w_in_c"][0])
            g0 = plan["qkv"][0]
            with sp.Fori(0, KD // 2) as j:
                for i in range(6):
                    c = bass.ds(j * 256 + (i // 3) * 128 + (i % 3) * D, 128)
                    load(j * 6 + (g0 + i), plain(w_c, (g0 + i) % 2, c, KD))
            out_tiles(1)
            ffn_tiles(1)
            for b in range(NBLK + 1):
                sp.wait_ge(yt_read, b + 1)
                n = qrows(b)
                dst = O["y_prompt"][0, b * 128:(b + 1) * 128, :] if b < NBLK else O["y_sample"][0]
                sp.dma_start(dst, y_out[b % 2][0:n, :]).then_inc(y_st[b % 2], 16)
            sp.wait_ge(y_st[0], 16 * (NBLK // 2 + 1))
            sp.wait_ge(y_st[1], 16 * (NBLK // 2))

        @block.gpsimd
        def _(pool):
            nc.gpsimd.memset(ones[:, :], 1.0).then_inc(const_done, 1)
            pool.sem_inc(conv_free, 1)
            pool.sem_inc(state_free, 1)
            pool.dma_start(neg_sink[:, :], I["sink_a"][0].partition_broadcast(128)).then_inc(sink_ok, 16)
            pool.wait_ge(xt_act, 8)
            pool.wait_ge(xt_dve, 16)
            pool.dma_start(x_spill.ap(), x[:, :, :].rearrange("p k t -> p (k t)")).then_inc(spilled, 16)
            pool.wait_ge(spilled, 16)
            pool.wait_ge(hl_done, 3)
            pool.dma_start(cache_ak[:, :], I["cache_a_k"][0, 0].rearrange("t h d -> t (h d)")).then_inc(ck_in[0], 16)
            pool.dma_start(v_tok[:, NBLK + 1, :], I["cache_a_v"][0, 0].rearrange("t h d -> t (h d)")).then_inc(cv_in[0], 16)
            pool.wait_ge(t_read, 4)
            a_k = lambda a: a[0, 0].rearrange("t h d -> t (h d)")
            pool.dma_start(a_k(O["pa_k"]), k_out[:, 0, :]).then_inc(kv_stored, 16)
            pool.dma_start(a_k(O["sa_k"]), k_out[0:TS, 1, :]).then_inc(kv_stored, 16)
            pool.dma_start(a_k(O["pa_v"]), v_tok[:, NBLK - 1, :]).then_inc(kv_stored, 16)
            pool.dma_start(a_k(O["sa_v"]), v_tok[0:TS, NBLK, :]).then_inc(kv_stored, 16)
            with pool.Fori(0, 4) as t:
                for e in range(2):
                    pool.wait_ge(scores_read, t * 18 + CREDIT)
                    apart(pool)
                    pool.dma_start(neg_bias[:, e, 0:256].unsqueeze(1), I["alibi"].rearrange("h p c -> p h c")[:, bass.ds(t + e * 4, 1), :]
                                   ).then_inc(bias_raw[e], 16)
            pool.wait_ge(ol_done, one(8))
            pool.wait_ge(kv_stored, 64)
            pool.dma_start(m_in[:, :], I["state_b_m"][0].rearrange("b h -> h b")).then_inc(mstate_ok, 16)
            pool.dma_start(gate_b[0:4, :], I["b_gates_b"][0:1, 0:4].rearrange("b h -> h b")).then_inc(mstate_ok, 16)
            pool.dma_start(gate_b[32:36, :], I["b_gates_b"][0:1, 4:8].rearrange("b h -> h b")).then_inc(mstate_ok, 16)
            pool.dma_start(cmask[:, :], I["causal"]).then_inc(mstate_ok, 16)
            pool.dma_start(mem_in[:, :, :], I["state_b_c"][0, 0].rearrange("h v k -> v h k")).then_inc(mstate_ok, 16)
            pool.wait_ge(gate_rows, 2)
            pool.dma_start(O["pb_m"][0].rearrange("b h -> h b"), row["m"][:, TP - 1:TP]).then_inc(stored, 16)
            pool.dma_start(O["sb_m"][0].rearrange("b h -> h b"), row["m"][:, T - 1:T]).then_inc(stored, 16)
            with pool.Fori(0, H_B) as h:
                for i in range(2):
                    pool.wait_ge(evac_act, h * 12 + (CREDIT + plan["heads"][2] + 3 * (i + 1)))
                    apart(pool)
                    for name, c in (("pb_conv", TP), ("sb_conv", UW - 3)):
                        dst = O[name][0, 0].rearrange("j f -> f j")
                        pool.dma_start(dst[bass.ds(h * 128 + i * W_B, 128), :], u_in[i][:, c:c + 3]).then_inc(conv_stored, 16)
                pool.wait_ge(conv_stored, h * 64 + 64)
                pool.sem_inc(conv_free, 1)
                pool.wait_ge(memT_read, one(h + 1))
                apart(pool)
                for i, (nc_, nn) in enumerate((("pb_c", "pb_n"), ("sb_c", "sb_n"))):
                    dst = O[nc_][0, 0].rearrange("h v k -> v h k")
                    pool.dma_start(dst[:, bass.ds(h, 1), :], mem_out[:, i, 0:128]).then_inc(state_st, 16)
                    dst = O[nn][0, 0].rearrange("h k -> k h")
                    pool.dma_start(dst[:, bass.ds(h, 1)], mem_out[:, i, 128:129]).then_inc(state_st, 16)
                pool.wait_ge(state_st, h * 64 + 64)
                pool.sem_inc(state_free, 1)

            def reload_x(layer):
                pool.wait_ge(proj_done, 3 * plan[f"out{layer}"][0] + 1)
                pool.dma_start(x[:, :, :].rearrange("p k t -> p (k t)"), x_spill.ap()).then_inc(x_loaded, 16)

            reload_x(0)
            for tt in range(NTT):
                pool.wait_ge(x_new, 3 + tt + 1)
                pool.dma_start(x_spill.ap().rearrange("p (k t) -> p k t", k=KD)[:, :, tt_cols(tt)], x[:, :, tt_cols(tt)]).then_inc(spilled, 16)
            pool.wait_ge(spilled, 64)
            pool.wait_ge(hl_done, 9)

            def bias_c(hp, e, first=False):
                if not first:
                    pool.wait_ge(scores_read, hp * 18 + (CREDIT + 72 - 18 + 9 * (e + 1)))
                    apart(pool)
                pool.dma_start(neg_bias[:, e, :].unsqueeze(1), bias_dram.ap().rearrange("h p c -> p h c")[:, bass.ds(hp * 2 + e, 1), :]).then_inc(bias_raw[e], 16)
                pool.wait_ge(bias_raw[e], hp * 16 + (64 + 16))
                apart(pool)
                nc.gpsimd.memset(neg_bias[0:64, e, 576:640], BIG)
                nc.gpsimd.memset(neg_bias[64:128, e, 0:64], BIG).then_inc(bias_ok[e], 1)

            def caches_c(hp, par):
                for name, dst, s in (("cache_c_k", cache_k, ck_in), ("cache_c_v", cache_v, cv_in)):
                    src = I[name][0, 0].rearrange("(b p) h d -> p b (h d)", p=128)
                    pool.dma_start(dst[par][:, :, :], src[:, :, bass.ds(hp * 128, 128)]).then_inc(s[par], 16)

            def stores_c(hp):
                pool.wait_ge(t_read, hp * 22 + (76 + 4))
                apart(pool)
                for pn, sn, src in (("pc_k", "sc_k", k_out), ("pc_v", "sc_v", v_tok[:, 4:9, :])):
                    dst = O[pn][0, 0].rearrange("(b p) h d -> p b (h d)", p=128)
                    pool.dma_start(dst[:, :, bass.ds(hp * 128, 128)], src[:, 0:4, :]).then_inc(kv_stored, 16)
                    dst = O[sn][0, 0].rearrange("p h d -> p (h d)")
                    pool.dma_start(dst[:, bass.ds(hp * 128, 128)], src[0:TS, 4, :]).then_inc(kv_stored, 16)

            def pair_c(hp, par, last):
                if not last:
                    pool.wait_ge(ol_done, one(hp * 2 + 8))
                    apart(pool)
                    caches_c(hp + 1, 1 - par)
                stores_c(hp)
                if not last:
                    for e in range(2):
                        bias_c(hp + 1, e)

            pool.wait_ge(toeplitz, 16)
            caches_c(0, 0)
            for e in range(2):
                bias_c(0, e, first=True)
            with pool.Fori(0, 3) as j:
                for par in range(2):
                    pair_c(j * 2 + par, par, False)
            pair_c(6, 0, False)
            pair_c(7, 1, True)
            pool.wait_ge(kv_stored, 64 + 64 * 8)
            reload_x(1)

        @block.tensor
        def _(pe):
            tr = nc.tensor.transpose

            def project(g, slot, tt, hi, lo, kt, b, free, part=None):
                if part in (None, 0):
                    pe.wait_ge(free[0], free[1])
                    pe.wait_ge(lo_done, g + 1)
                out = psum[:, b, 0:TW]
                c = tt_cols(tt)
                for k in range(kt) if part is None else range(kt * part // 3, kt * (part + 1) // 3):
                    nc.tensor.matmul(out, w_hi[:, slot, k], hi[:, k, c], start=(k == 0), stop=False)
                    nc.tensor.matmul(out, w_hi[:, slot, k], lo[:, k, c], start=False, stop=False)
                    last = nc.tensor.matmul(out, w_lo[:, slot, k], hi[:, k, c], start=False, stop=(k == kt - 1))
                if part in (None, 2):
                    last.then_inc(proj_done, 1)

            def act_tile(name, i, slot, src, par=None):
                g0, _, a0, _ = plan[name]
                for tt in range(NTT):
                    project(i + g0, slot, tt, src[0], src[1], KD, tt, (evac_act, i * 3 + (a0 + tt + 1)))

            pe.sem_inc(hT_done, 1)
            pe.sem_inc(ada_done, 4)
            pe.wait_ge(misc_in, 16)
            pe.wait_ge(par_in, 112)
            tr(bank(0, 128), prm_in[:, :], ident[:, :]).then_inc(rows_t, 1)
            pe.wait_ge(par2_in, 32)
            tr(bank(1, 120), prm2_in[0:120, :], ident[0:120, 0:120]).then_inc(rows_t, 1)
            pe.wait_ge(rows_got, 2)
            pe.wait_ge(x_in_sem, 48)
            for k in range(KD):
                for part in range(3):
                    n = 3 * k + part
                    if n >= 3:
                        pe.wait_ge(xt_act, k) if part == 0 else pe.wait_ge(xt_dve, 2 * (k - 1) + part)
                    for b in range(4 * part, min(4 * part + 4, NBLK + 1)):
                        m = qrows(b)
                        last = tr(psum[:, part, 128 * (b % 4):128 * (b % 4) + m],
                                  x_in[0:m, b, 128 * k:128 * k + 128], ident[0:m, 0:m])
                    last.then_inc(xt_done, 1)
            def sum_x(n, tt, b0=4):
                pe.wait_ge(sq_done, 3 * (n // 2) + tt + 1)
                for k in range(KD):
                    last = nc.tensor.matmul(bank(b0 + tt, TW), ones[:, :], norm_buf[:, k, tt_cols(tt)], start=(k == 0), stop=(k == KD - 1))
                last.then_inc(ss_done, 1)

            def sum_y(n, tt):
                pe.wait_ge(acc_done, 24 * (n // 2) + 18 + 2 * tt + 2 + CREDIT)
                nc.tensor.matmul(bank(4 + tt, TW), ones[:, :], sq_sum[:, tt_cols(tt)], start=True, stop=True).then_inc(ss_done, 1)

            def last_pair(n, step):
                for s_, (tt, par) in enumerate(PAIR):
                    step(s_, tt, par)
                    if s_ in (3, 5):
                        sum_y(n, tt - 1)
                sum_y(n, 2)

            pe.wait_ge(const_done, 1)
            for tt in range(NTT):
                sum_x(0, tt, 0)

            def ada_products(ring, m, half, bank_, copied, loads):
                u = m % 4
                if half == 0:
                    pe.wait_ge(ada_copied, copied)
                    pe.wait_ge(ada_loaded[u], loads)
                for k in range(half * KD // 2, (half + 1) * KD // 2):
                    last = nc.tensor.matmul(psum[0:2, bank_, 0:256], silu_c[:, k], ring[u][:, k, :],
                                            start=(k == 0), stop=(k == KD - 1))
                if half == 1:
                    last.then_inc(ada_done, 1)

            def ada_transposes(q, bank_):
                pe.wait_ge(ada_copied, q * 4 + (4 + 2))
                pe.wait_ge(ada_got, one(q))
                apart(pe)
                for v in range(8):
                    last = tr(psum[:, bank_, 2 * v:2 * v + 2], ada_row[:, v // 2, 128 * (v % 2):128 * (v % 2) + 128], ident[0:2, 0:2])
                last.then_inc(ada_t, 1)

            pe.wait_ge(c_ready, 1)
            with pe.Fori(0, 2) as q:
                for v in range(8):
                    ada_products(ada_s, v // 2, v % 2, 3 + v // 2 % 2, q * 4 + (v // 2 + 1), q * 16 + 16)
                ada_transposes(q, 5)

            h = (h_hi, h_lo)
            def att_round(kind, it, r, items, after_out=False):
                c = KINDS[kind]
                for out_slot, src, m, n in items:
                    last = tr(tps[0:n, out_slot, 0:m], src, ident[0:m, 0:m])
                last.then_inc(t_done, 1)

            def attention(kind, it, q, k, kct, vt, vc, par, fill, pre):
                c = KINDS[kind]
                N = lambda n: it * 18 + (c["n0"] + n)
                R = lambda n: it * (18 + c["pre"]) + (c["r0"] + c["pre"] + n)
                lag, sb, f0 = c["lag"], c["score_bufs"], c["fill0"]
                pre()
                for i in range(19 + lag):
                    if i < 18:
                        n, e, p = i, i // 9, i % 9
                        m, (w, _) = qrows(p), score_width(kind, p)
                        rows = slice(64 * e, 64 * e + 64)
                        pe.wait_ge(scores_read, N(n) + (CREDIT + 1 - sb))
                        apart(pe)
                        lhs = q[rows, 128 * p:128 * p + m]
                        col = 0
                        for blk, kn in cut_scores(kind, p):
                            last = nc.tensor.matmul(psum[0:m, score_bank(kind, n) + col // 512, col % 512:col % 512 + kn],
                                                    lhs, keys(blk, kn, rows, k, kct), start=True, stop=True)
                            col += kn
                        last.then_inc(scores, 1)
                    if fill:
                        fill(i + f0)
                    if lag <= i < 18 + lag:
                        n = i - lag
                        e, p = n // 9, n % 9
                        m = qrows(p)
                        pe.wait_ge(p_done, N(n) + 1)
                        pe.wait_ge(t_read, R(n))
                        apart(pe)
                        for s, (_, kn) in enumerate(key_blocks(kind, p)):
                            last = tr(tps[0:kn, s, 0:m], c["probs"][0:m, n % sb, 128 * s:128 * s + kn], ident[0:m, 0:m])
                        last.then_inc(t_done, 1)
                    if i > lag:
                        n = i - lag - 1
                        e, p = n // 9, n % 9
                        m = qrows(p)
                        pe.wait_ge(t_read, R(n) + 1)
                        pe.wait_ge(o_read, one(N(n)))
                        apart(pe)
                        kb = key_blocks(kind, p)
                        for s, (blk, kn) in enumerate(kb):
                            v = vc[0:kn, blk[1], 64 * e:64 * e + 64] if isinstance(blk, tuple) else vt[0:kn, blk, 64 * e:64 * e + 64]
                            last = nc.tensor.matmul(oacc[0:m, 0:64], probs_t[0:kn, n % 2, s, 0:m], v,
                                                    start=(s == 0), stop=(s == len(kb) - 1))
                        last.then_inc(o_done, 1)
                for r, blocks in enumerate((range(0, 5), range(5, 9))):
                    if fill:
                        fill(19 + lag + f0 + r)
                    if r == 0:
                        pe.wait_ge(o_read, one(N(18)))
                    pe.wait_ge(t_read, R(18))
                    if r == 1:
                        pe.wait_ge(ol_done, one(it * 2 + (c["o0"] + 1)))
                    for s, b in enumerate(blocks):
                        m = qrows(b)
                        last = tr(tps[:, s, 0:m], o_tok[0:m, b, :], ident[0:m, 0:m])
                    last.then_inc(t_done, 1)

            def cut_scores(kind, p):
                if p == NBLK:
                    return [(("cache", 0), BW[kind] - 128), (TP, TS)]
                w = score_width(kind, p)[0]
                k0 = 128 * (p + 1) - w
                return [(k0, min(w, 512))] + ([(k0 + 512, w - 512)] if w > 512 else [])

            def keys(blk, kn, rows, k, kct):
                return kct[rows, 0:kn] if isinstance(blk, tuple) else k[rows, blk:blk + kn]

            def ada_fill(j, par, i):
                v = 20 * par + i
                if i <= 20 and v in (8, 16, 24, 32) or v == 40:
                    ada_transposes(j * 5 + (2 + v // 8 - 1), 4)
                if i < 20:
                    m = v // 2
                    ada_products(ada_m, m, v % 2, 0, j * 20 + (8 + m + 2), j * 80 + 16 * (2 + m // 4 + 1))

            for s_, (tt, i) in enumerate(PAIR):
                pe.wait_ge(hl_done, tt + 1)
                project(i, i, tt, h_hi, h_lo, KD, s_ % 3, (evac_act, CREDIT - 2 + s_))
            pe.wait_ge(ck_in[0], 16)
            att_round("A", 0, 0, [(0, cache_ak[:, :], 128, 128)])
            pe.wait_ge(evac_act, CREDIT + 6)
            pe.wait_ge(t_read, 1)
            att_round("A", 0, 1, [(s, v_a[:, 128 * b:128 * b + 128], 128, 128) for s, b in enumerate(range(5))])
            pe.wait_ge(t_read, 2)
            att_round("A", 0, 2, [(s, v_a[:, 128 * b:128 * b + qrows(b)], 128, qrows(b)) for s, b in enumerate(range(5, 9))])
            pe.wait_ge(t_read, 3)
            att_round("A", 0, 3, [(s, k_a[:, 128 * b:128 * b + qrows(b)], 128, qrows(b)) for s, b in enumerate((7, 8))])
            pe.wait_ge(cv_in[0], 16)
            with pe.Fori(0, 2) as j:
                for par in range(2):
                    t = j * 2 + par
                    act_tile("qa", t, (plan["qa"][0] + par) % 2, h)
                    pe.wait_ge(evac_act, t * 3 + (CREDIT + plan["qa"][2] + 3))
                    pe.wait_ge(ol_done, one(t * 2))
                    attention("A", t, q_a, k_a, cache_akt, v_tok, v_tok[:, NBLK + 1:NBLK + 2, :], par,
                              lambda i: ada_fill(j, par, i), lambda: None)
            pe.wait_ge(ol_done, one(8))
            act_tile("gates", 0, plan["gates"][0] % 2, h)

            def head_products(hd):
                for i in range(4):
                    act_tile("heads", hd * 4 + i, (plan["heads"][0] + i) % 2, h)

            head_products(0)
            pe.wait_ge(gate_rows, 2)
            for b in range(NBLK + 1):
                m = qrows(b)
                for i, name in enumerate(("g", "wend", "enegm")):
                    last = tr(psum[0:m, 5, 12 * b + 4 * i:12 * b + 4 * i + 4], row[name][:, 128 * b:128 * b + m], ident[0:4, 0:4])
            last.then_inc(cols_t, 1)
            pe.wait_ge(mstate_ok, 80)
            for i in range(H_B):
                last = tr(psum[:, 6, 128 * i:128 * i + 128], mem_in[:, i, :], ident[:, :])
            last.then_inc(cols_t, 1)
            pe.wait_ge(cols_ok, 2)
            def head(hd):
                pe.wait_ge(head_set, hd + 1)
                pe.wait_ge(evac_act, hd * 12 + (CREDIT + plan["heads"][2] + 12))
                pe.wait_ge(og_done, one(hd))
                for tt in range(NTT):
                    nc.tensor.matmul(bank(tt, TW), ones[0:4, :], a_h[:, tt_cols(tt)], start=True, stop=True
                                     ).then_inc(abc_done, 1)
                nc.tensor.matmul(bank(3, NBLK + 1), ones[0:4, :], ae_h[:, :], start=True, stop=True
                                 ).then_inc(abc_done, 1)
                pe.wait_ge(conv_in, one(hd * 2 + 2))
                pe.wait_ge(qa_done, hd * 4 + 4)
                pe.wait_ge(ol9, one(hd))
                pe.wait_ge(memT_read, one(hd))

                def front(c):
                    m = qrows(c)
                    cs = slice(128 * c, 128 * c + m)
                    pe.wait_ge(w_done, one(hd * 9 + c))
                    nc.tensor.matmul(psum[0:m, 4, 0:m], qk_b[1][:, cs], qk_b[0][:, cs], start=True, stop=True).then_inc(st_done, 1)
                    pe.wait_ge(decay_done, one(hd * 9 + c))
                    apart(pe)
                    nc.tensor.matmul(psum[0:m, 5, 0:m], ones[0:4, 0:m], nm_h[:, cs], start=True, stop=False)
                    nc.tensor.matmul(psum[0:m, 5, 0:m], ident[0:m, 0:m], cmask[0:m, 0:m], start=False, stop=True).then_inc(arg_done, 1)
                    pe.wait_ge(kvx_done, one(hd * 9 + c))
                    tr(psum[0:m, 6, 0:128], qk_b[1][:, cs], ident[:, :])
                    tr(psum[0:m, 6, 128:256], v_b[:, cs], ident[:, :]).then_inc(kv_done, 1)

                def back(c):
                    m = qrows(c)
                    cs = slice(128 * c, 128 * c + m)
                    mm = mem[c // NBLK]
                    nb = num_bank(c)
                    pe.wait_ge(mem_done, hd * 11 + (c + 2))
                    pe.wait_ge(num_read, one(hd * 9 + max(c - 1, 0)))
                    pe.wait_ge(w_done, one(hd * 9 + (c + 1)))
                    pe.wait_ge(kvx_done, one(hd * 9 + (c + 1)))
                    nc.tensor.matmul(psum[0:m, nb, 0:129], qa_b[:, cs], mm[:, 0:129], start=True, stop=False)
                    nc.tensor.matmul(psum[0:m, nb, 0:129], wts[0:m, c % 2, 0:m], v_x[0:m, c % 2, 0:129], start=False, stop=True
                                     ).then_inc(num_done, 1)
                    nc.tensor.matmul(psum[:, 3, 0:129], k_w[0:m, c % 2, :], v_x[0:m, c % 2, 0:129], start=True, stop=True
                                     ).then_inc(upd_done, 1)

                front(0)
                for c in range(NBLK + 1):
                    if c < NBLK:
                        front(c + 1)
                    back(c)
                pe.wait_ge(mem_done, hd * 11 + 11)
                pe.wait_ge(kvx_done, one(hd * 9 + 9))
                for i in range(2):
                    last = tr(psum[:, 6, 128 * i:128 * i + 128], mem[i][:, 0:128], ident[:, :])
                last.then_inc(memT_done, 1)
                pe.wait_ge(hn_done, hd + 1)
                for r, blocks in enumerate((range(0, 4), range(4, 8), range(8, 9))):
                    b_ = (4, 5, 3)[r]
                    for s, b in enumerate(blocks):
                        m = qrows(b)
                        last = tr(psum[:, b_, 128 * s:128 * s + m], h_tok[0:m, b, :], ident[0:m, 0:m])
                    last.then_inc(hT_done, 1)

            head(0)
            with pe.Fori(1, H_B) as hd:
                head_products(hd)
                head(hd)

            def out_tiles(layer):
                g0, _, a0, _ = plan[f"out{layer}"]
                with pe.Fori(0, KD // 2 - 1) as j:
                    for par in range(2):
                        act_tile(f"out{layer}", j * 2 + par, (g0 + par) % 2, (o_hi, o_lo))
                last_pair(1 + 4 * layer, lambda s_, tt, par: project(
                    g0 + KD - 2 + par, (g0 + par) % 2, tt, o_hi, o_lo, KD, s_ % 3, (evac_act, a0 + 3 * (KD - 2) + CREDIT - 2 + s_)))

            def ffn(layer):
                for n, ff in enumerate(FF_GROUPS):
                    g0, _, a0, d0 = plan[f"gu{layer}{n}"]
                    if n == 0:
                        for tt in range(NTT):
                            pe.wait_ge(hl_done, 3 + 6 * layer + tt + 1)
                            project(g0, g0 % 2, tt, h_hi, h_lo, KD, tt, (evac_act, a0 + CREDIT))
                            project(g0 + 1, (g0 + 1) % 2, tt, h_hi, h_lo, KD, 3 + tt, (ms_done, 9 + 12 * layer))
                    with pe.Fori(1 if n == 0 else 0, ff) as f:
                        for tt in range(NTT):
                            project(f * 2 + g0, g0 % 2, tt, h_hi, h_lo, KD, tt, (evac_dve, f * 3 + (d0 + CREDIT - 2 + tt)))
                        for tt in range(NTT):
                            project(f * 2 + (g0 + 1), (g0 + 1) % 2, tt, h_hi, h_lo, KD, tt, (evac_act, f * 3 + (a0 + CREDIT + 1 + tt)))
                    nff = 3 * (sum(FF_GROUPS) * layer + sum(FF_GROUPS[:n + 1]))
                    g0, _, _, d0 = plan[f"down{layer}{n}"]
                    final = n == len(FF_GROUPS) - 1
                    with pe.Fori(0, KD // 2 - final) as j:
                        for par in range(2):
                            for tt in range(NTT):
                                pe.wait_ge(fflo_done, nff - 2 + tt)
                                project(j * 2 + (g0 + par), (g0 + par) % 2, tt, ff_hi, ff_lo, ff, tt,
                                        (evac_dve, j * 6 + (3 * par + d0 + tt + CREDIT - 2)))
                    if final:
                        last_pair(3 + 4 * layer, lambda s_, tt, par: project(
                            g0 + KD - 2 + par, (g0 + par) % 2, tt, ff_hi, ff_lo, ff, s_ % 3, (evac_dve, d0 + 3 * (KD - 2) + CREDIT - 2 + s_)))

            pe.wait_ge(ol9, one(H_B))
            out_tiles(0)
            for tt in range(NTT):
                sum_x(2, tt)
            ffn(0)
            for tt in range(NTT):
                sum_x(4, tt)
            g0, _, a0, _ = plan["qkv"]

            def qkv_step(hp, par, f, b, ahead, part=None):
                i, tt = f // 3, f % 3
                slot = (g0 + 3 * par + i) % 2
                project(hp * 3 + (g0 + i), slot, tt, h_hi, h_lo, KD, b, (evac_act, hp * 9 + (a0 + f + CREDIT - ahead)), part)

            for s_, (tt, i) in enumerate(PAIR):
                pe.wait_ge(hl_done, 6 + tt + 1)
                project(g0 + i, (g0 + i) % 2, tt, h_hi, h_lo, KD, s_ % 3, (evac_act, a0 + CREDIT - 2 + s_))
            for f in range(6, 9):
                qkv_step(0, 0, f, f % 3, 2)

            def pair(hp, par, last):
                c = KINDS["C"]
                R = lambda n: hp * 22 + (c["r0"] + n)

                def pre():
                    step(0)
                    pe.wait_ge(ol_done, one(hp * 2 + c["o0"]))
                    pe.wait_ge(ck_in[par], ck_count(hp, par))
                    att_round("C", hp, 0, [(s, cache_k[par][:, s, :], 128, 128) for s in range(4)])
                    step(1)
                    pe.wait_ge(evac_act, hp * 9 + (a0 + 9 + CREDIT))
                    pe.wait_ge(t_read, R(1))
                    att_round("C", hp, 1, [(s, v_c[par][:, 128 * b:128 * b + 128], 128, 128) for s, b in enumerate(range(5))])
                    step(2)
                    pe.wait_ge(t_read, R(2))
                    att_round("C", hp, 2, [(s, v_c[par][:, 128 * b:128 * b + qrows(b)], 128, qrows(b)) for s, b in enumerate(range(5, 9))])
                    step(3)
                    pe.wait_ge(t_read, R(3))
                    att_round("C", hp, 3, [(s, k_c[par][:, 128 * b:128 * b + qrows(b)], 128, qrows(b)) for s, b in enumerate(range(4, 9))])
                    step(4)
                    pe.wait_ge(cv_in[par], ck_count(hp, par))
                    pe.wait_ge(t_read, R(4))

                fill = None if last else (lambda i: qkv_step(hp + 1, 1 - par, i // 3, 0, 0, i % 3))
                step = fill or (lambda i: None)
                attention("C", hp, q_c[par], k_c[par], cache_kt, v_tok, cache_v[par], par, fill, pre)

            def ck_count(hp, par):
                return (hp - par) * 8 + (16 + (16 if par == 0 else 0))

            with pe.Fori(0, 3) as j:
                for par in range(2):
                    pair(j * 2 + par, par, False)
            pair(6, 0, False)
            pair(7, 1, True)
            pe.wait_ge(ol_done, one(24))
            out_tiles(1)
            for tt in range(NTT):
                sum_x(6, tt)
            ffn(1)
            for b in range(NBLK + 1):
                m = qrows(b)
                pe.wait_ge(x_new, 9 + (128 * b + m - 1) // TW + 1)
                if b >= 2:
                    pe.wait_ge(yt_read, b - 1)
                for k in range(KD):
                    last = tr(psum[0:m, 2 * (b % 2) + k // 4, 128 * (k % 4):128 * (k % 4) + 128], x[:, k, 128 * b:128 * b + m], ident[:, :])
                last.then_inc(yt_done, 1)

        @block.scalar
        def _(act):
            A = nc.scalar.activation
            for s in (decay_done, kvx_done, num_read, memT_read, conv_in):
                act.sem_inc(s, 1)
            act.sem_inc(evac_act, CREDIT)

            def split_hi(g, slot):
                if not (isinstance(g, int) and g < 2):
                    act.wait_ge(proj_done, g * 3 - 3)
                act.wait_ge(w_loaded[slot], loads(g, slot))
                A(w_hi[:, slot], w_raw[:, slot], ACT.Copy).then_inc(hi_done, 1)

            def loads(g, slot):
                return (g - slot) * 24 + 48

            def split_next(g, slot):
                if isinstance(g, int) and g + 2 >= TILES:
                    return
                split_hi(g + 2, slot)

            act.wait_ge(rows_t, 1)
            A(prm[:, :], bank(0, 128), ACT.Copy).then_inc(rows_got, 1)
            act.drain()
            A(silu_c[:, :, :].rearrange("p k r -> p r k"), prm[:, 0:16].rearrange("p (r k) -> p r k", r=2), ACT.Silu).then_inc(c_ready, 1)
            act.wait_ge(rows_t, 2)
            A(prm2[:, :], bank(1, 120), ACT.Copy).then_inc(rows_got, 1)
            for k in range(KD):
                act.wait_ge(xt_done, 3 * k + 1)
                A(x[:, k, 0:512], bank(0), ACT.Copy).then_inc(xt_act, 1)
            def square(n, tt):
                if n:
                    act.wait_ge(x_new, 3 * (n // 2 - 1) + tt + 1)
                A(norm_buf[:, :, tt_cols(tt)], x[:, :, tt_cols(tt)], ACT.Square).then_inc(sq_done, 1)

            def root(n, tt):
                act.wait_ge(ms_done, 3 * n + tt + 1)
                A(rstd[:, tt], rstd[:, tt], ACT.Sqrt).then_inc(rt_done, 1)

            def h_out(n, tt):
                act.wait_ge(xn_done, 3 * n + tt + 1)
                for k in range(KD):
                    for a, b, r in groups(tt):
                        c = slice(tt * TW + a, tt * TW + b)
                        A(norm_buf[:, k, c], norm_buf[:, k, c], ACT.Identity, scale=pre_scale[:, n, k, r:r + 1], bias=mod[:, 3 * n, k, r:r + 1])
                act.drain()
                A(h_hi[:, :, tt_cols(tt)], norm_buf[:, :, tt_cols(tt)], ACT.Copy).then_inc(hh_done, 1)

            act.wait_ge(xt_dve, 16)
            act.wait_ge(xt_act, 8)
            for tt in range(NTT):
                square(0, tt)
            for tt in range(NTT):
                root(0, tt)
            for g in range(2):
                split_hi(g, g)
            act.wait_ge(derived, 1)
            for tt in range(NTT):
                h_out(0, tt)

            def copies(name, i, slot, dst, func=ACT.Copy, scale=1.0, wait=None, g=None):
                g0, _, a0, _ = plan[name]
                for tt in range(NTT):
                    act.wait_ge(proj_done, i * 3 + (3 * g0 + tt + 1))
                    A(dst(tt), bank(tt, TW), func, scale=scale).then_inc(evac_act, 1)
                split_next(i + g0, slot)

            def attention(kind, it, sinks, fill, pre):
                c = KINDS[kind]
                N = lambda n: it * 18 + (c["n0"] + n)
                TD = lambda n: it * (20 + c["pre"]) + ((0 if kind == "A" else 4 + 80) + (4 if kind == "A" else 0) + c["pre"] + n)
                lag, sb, probs, f0 = c["lag"], c["score_bufs"], c["probs"], c["fill0"]
                pre()
                def exps(n):
                    p = n % 9
                    m, (w, _) = qrows(p), score_width(kind, p)
                    act.wait_ge(scores_read, N(n) + (CREDIT + 1))
                    if sinks:
                        e = n // 9
                        A(sink_e[0:m, n % 6:n % 6 + 1], sink2[0:m, e:e + 1], ACT.Exp, scale=-1.0, bias=mins[0:m, n % 6:n % 6 + 1])
                    A(probs[0:m, n % sb, 0:w], probs[0:m, n % sb, 0:w], ACT.Exp, scale=-1.0,
                      bias=mins[0:m, n % 6:n % 6 + 1], accum_out=sums[0:m, n % 6:n % 6 + 1]).then_inc(p_done, 1)

                def copy(n):
                    p = n % 9
                    m, kb = qrows(p), key_blocks(kind, p)
                    act.wait_ge(t_done, TD(n) + 1)
                    full = sum(kn == 128 for _, kn in kb)
                    if full == len(kb):
                        A(probs_t[:, n % 2, 0:full, 0:m], tps[:, 0:full, 0:m], ACT.Copy).then_inc(t_read, 1)
                    else:
                        A(probs_t[:, n % 2, 0:full, 0:m], tps[:, 0:full, 0:m], ACT.Copy)
                        A(probs_t[0:TS, n % 2, full, 0:m], tps[0:TS, full, 0:m], ACT.Copy).then_inc(t_read, 1)

                for i in range(19 + lag):
                    if lag == 1 and i < 18:
                        exps(i)
                    if lag <= i < 18 + lag:
                        copy(i - lag)
                    if lag > 1 and i < 18:
                        exps(i)
                    if fill:
                        fill(i + f0)
                for r in range(2):
                    if fill:
                        fill(19 + lag + f0 + r)
                    act.wait_ge(t_done, TD(18 + r) + 1)
                    nb, c0 = (5, 0) if r == 0 else (4, 640)
                    dst = o_hi[:, bass.ds(it, 1) if not isinstance(it, int) else slice(it, it + 1), :]
                    w = 640 if r == 0 else T - 640
                    A(dst[:, :, c0:c0 + w], psum_cols(w), ACT.Copy).then_inc(oh_done, 1)

            def psum_cols(w):
                return psum[:, 5:7, :].rearrange("p b c -> p (b c)")[:, 0:w].unsqueeze(1)

            act.wait_ge(spilled, 16)
            act.wait_ge(rev_st, 16)

            def num_out(hd, c):
                m = qrows(c)
                act.wait_ge(den_done, hd * 9 + (c + 1))
                A(h_tok[0:m, c, :], psum[0:m, num_bank(c), 0:128], ACT.Copy, scale=rden[0:m, c % 2:c % 2 + 1])
                A(junk[0:m, c % 2, :], psum[0:m, num_bank(c), 0:128], ACT.Square, scale=rden[0:m, c % 2:c % 2 + 1],
                  accum_out=ssq[0:m, c:c + 1]).then_inc(num_read, 1)

            for s_, (tt, i) in enumerate(PAIR):
                act.wait_ge(proj_done, s_ + 1)
                A((k_a, v_a)[i][:, tt_cols(tt)], bank(s_ % 3, TW), ACT.Copy).then_inc(evac_act, 1)
            for i in range(2):
                split_next(i, i)
            act.wait_ge(t_done, 1)
            A(cache_akt[:, :], tps[:, 0, :], ACT.Copy).then_inc(t_read, 1)
            act.wait_ge(t_done, 2)
            A(v_tok[:, 0:5, :], tps[:, 0:5, :], ACT.Copy).then_inc(t_read, 1)
            act.wait_ge(t_done, 3)
            A(v_tok[:, 5:8, :], tps[:, 0:3, :], ACT.Copy)
            A(v_tok[0:TS, 8, :], tps[0:TS, 3, :], ACT.Copy).then_inc(t_read, 1)
            act.wait_ge(t_done, 4)
            A(k_out[:, 0, :], tps[:, 0, :], ACT.Copy)
            A(k_out[0:TS, 1, :], tps[0:TS, 1, :], ACT.Copy).then_inc(t_read, 1)
            act.wait_ge(sink_neg, 1)
            with act.Fori(0, 2) as j:
                for par in range(2):
                    t = j * 2 + par
                    copies("qa", t, (plan["qa"][0] + par) % 2, lambda tt: q_a[:, tt_cols(tt)], scale=QSCALE)
                    attention("A", t, True, None, lambda: None)
            act.wait_ge(mstate_ok, 80)
            g0, _, a0, _ = plan["gates"]
            for tt in range(NTT):
                act.wait_ge(proj_done, 3 * g0 + tt + 1)
                A(row["logi"][:, tt_cols(tt)], psum[0:4, tt, 0:TW], ACT.Identity, bias=gate_b[0:4, :])
                A(row["fg"][:, tt_cols(tt)], psum[32:36, tt, 0:TW], ACT.Identity, bias=gate_b[32:36, :]).then_inc(evac_act, 1)
            split_next(g0, g0 % 2)
            act.drain()
            A(row["t"][:, :], row["fg"][:, :], ACT.Abs)
            act.drain()
            A(row["t"][:, :], row["t"][:, :], ACT.Exp, scale=-1.0)
            act.drain()
            A(row["t"][:, :], row["t"][:, :], ACT.Ln, bias=1.0).then_inc(gate_e, 1)
            def head_products(hd):
                g0, _, a0, _ = plan["heads"]
                for i in range(4):
                    slot = (g0 + i) % 2
                    for tt in range(NTT):
                        act.wait_ge(proj_done, hd * 12 + (3 * g0 + 3 * i + tt + 1))
                        if i < 2:
                            if tt == 0:
                                act.wait_ge(conv_free, hd + 1)
                                act.wait_ge(conv_done, one(hd * 2))
                            a = tt * TW
                            n = TW if tt < 2 else TW - TS
                            if tt < 2:
                                A(u_in[i][:, 3 + a:3 + a + n], psum[:, tt, 0:n], ACT.Copy).then_inc(evac_act, 1)
                            else:
                                A(u_in[i][:, 3 + a:3 + a + n], psum[:, tt, 0:n], ACT.Copy)
                                A(u_in[i][:, UW - TS:UW], psum[:, tt, n:TW], ACT.Copy).then_inc(evac_act, 1)
                        elif i == 2:
                            A(v_b[:, tt_cols(tt)], bank(tt, TW), ACT.Copy).then_inc(evac_act, 1)
                        else:
                            A(og_b[:, tt_cols(tt)], bank(tt, TW), ACT.Sigmoid).then_inc(evac_act, 1)
                    if i in (1, 2):
                        n = i - 1
                        act.wait_ge(conv_done, one(hd * 2 + (n + 1)))
                        A(qk_b[n][:, 0:TP], conv_t[:, 0:TP], ACT.Silu, bias=conv_h[:, 4, n:n + 1])
                        A(qk_b[n][:, TP:T], conv_t[:, TP + 3:CW], ACT.Silu, bias=conv_h[:, 4, n:n + 1]).then_inc(conv_in, 1)
                    split_next(hd * 4 + (g0 + i), slot)

            head_products(0)
            act.wait_ge(gate_rows, 1)
            A(brd[:, T:2 * T], brd[:, T:2 * T], ACT.Exp)
            A(brd[:, 2 * T:SELW], brd[:, 2 * T:SELW], ACT.Exp)
            A(row["enegm"][:, :], row["m"][:, :], ACT.Exp, scale=-1.0)
            A(row["wend"][:, :], row["wend"][:, :], ACT.Exp).then_inc(gate_rows, 1)
            act.wait_ge(stored, 32)
            act.wait_ge(cols_ok, 2)

            def head(hd):
                for c in range(NBLK + 1):
                    m = qrows(c)
                    act.wait_ge(arg_done, hd * 9 + (c + 1))
                    A(decay[0:m, c % 2, 0:m], psum[0:m, 5, 0:m], ACT.Exp, bias=cols_h[0:m, c, 0:1]).then_inc(decay_done, 1)
                    act.wait_ge(kv_done, hd * 9 + (c + 1))
                    A(k_w[0:m, c % 2, :], psum[0:m, 6, 0:128], ACT.Copy, scale=cols_h[0:m, c, 1:2])
                    A(v_x[0:m, c % 2, 0:128], psum[0:m, 6, 128:256], ACT.Copy).then_inc(kvx_done, 1)
                    if c >= 1:
                        num_out(hd, c - 1)
                num_out(hd, NBLK)
                act.wait_ge(ms9, hd + 1)
                A(rs9[:, :], rs9[:, :], ACT.Sqrt).then_inc(rt9, 1)
                act.wait_ge(memT_done, hd + 1)
                act.wait_ge(n_copied, hd + 1)
                A(mem_out[:, :, 0:128], psum[:, 6, 0:256].rearrange("p (i k) -> p i k", i=2), ACT.Copy).then_inc(memT_read, 1)
                act.wait_ge(og_done, one(hd + 1))
                A(o_hi[:, one_of(hd, 4), :], ot_f[:, 0:T].unsqueeze(1), ACT.Copy).then_inc(oh9, 1)

            head(0)
            with act.Fori(1, H_B) as hd:
                head_products(hd)
                head(hd)

            def out_tiles(layer):
                g0, _, a0, _ = plan[f"out{layer}"]

                def step(tile, tt, b_, u):
                    act.wait_ge(proj_done, u + (3 * g0 + 1))
                    dst = y_mix[:, bass.ds(tile, 1) if not isinstance(tile, int) else slice(tile, tile + 1), tt_cols(tt)]
                    A(dst.rearrange("p o c -> p (o c)"), bank(b_, TW), ACT.Copy)
                    act.wait_ge(acc_done, u + (48 * layer + 1))
                    A(sq_ring[b_][:, :], bank(b_, TW), ACT.Square).then_inc(evac_act, 1)

                with act.Fori(0, KD // 2 - 1) as j:
                    for par in range(2):
                        for tt in range(NTT):
                            step(j * 2 + par, tt, tt, j * 6 + (3 * par + tt))
                        split_hi(j * 2 + (g0 + par + 2), (g0 + par) % 2)
                for s_, (tt, par) in enumerate(PAIR):
                    step(KD - 2 + par, tt, s_ % 3, 3 * (KD - 2) + s_)
                for par in range(2):
                    split_hi(g0 + KD + par, (g0 + par) % 2)

            def ffn(layer):
                for n, ff in enumerate(FF_GROUPS):
                    g0, _, a0, d0 = plan[f"gu{layer}{n}"]
                    nff = 3 * (sum(FF_GROUPS) * layer + sum(FF_GROUPS[:n]))
                    if n == 0:
                        for tt in range(NTT):
                            act.wait_ge(proj_done, 3 * g0 + 2 * tt + 1)
                            A(sil[:, tt_cols(tt)], bank(tt, TW), ACT.Silu).then_inc(evac_act, 1)
                        for tt in range(NTT):
                            act.wait_ge(evac_dve, d0 + CREDIT + tt + 1)
                            A(ff_hi[:, 0, tt_cols(tt)], ffs[:, tt_cols(tt)], ACT.Copy).then_inc(ffhi_done, 1)
                        for i in range(2):
                            split_hi(g0 + 2 + i, (g0 + i) % 2)
                    with act.Fori(1 if n == 0 else 0, ff) as f:
                        for tt in range(NTT):
                            act.wait_ge(proj_done, f * 6 + (3 * g0 + tt + 1))
                            act.wait_ge(evac_dve, f * 3 + (d0 + CREDIT))
                            A(sil[:, tt_cols(tt)], bank(tt, TW), ACT.Silu).then_inc(evac_act, 1)
                        split_hi(f * 2 + (g0 + 2), g0 % 2)
                        for tt in range(NTT):
                            act.wait_ge(evac_dve, f * 3 + (d0 + CREDIT + tt + 1))
                            A(ff_hi[:, bass.ds(f, 1), tt_cols(tt)].rearrange("p o c -> p (o c)"), ffs[:, tt_cols(tt)], ACT.Copy
                              ).then_inc(ffhi_done, 1)
                        split_hi(f * 2 + (g0 + 3), (g0 + 1) % 2)
                    g0 = plan[f"down{layer}{n}"][0]
                    final = n == len(FF_GROUPS) - 1

                    def step(tile, tt, i, u):
                        act.wait_ge(evac_dve, u + (d0_ + CREDIT + 1))
                        act.wait_ge(acc_done, u + (24 + 48 * layer + 1))
                        src = y_ffn[:, bass.ds(tile, 1) if not isinstance(tile, int) else slice(tile, tile + 1), tt_cols(tt)]
                        A(sq_ring[i][:, :], src.rearrange("p o c -> p (o c)"), ACT.Square).then_inc(sqy_done, 1)

                    d0_ = plan[f"down{layer}{n}"][3]
                    with act.Fori(0, KD // 2 - final) as j:
                        for par in range(2):
                            if final:
                                for tt in range(NTT):
                                    step(j * 2 + par, tt, tt, j * 6 + (3 * par + tt))
                            split_hi(j * 2 + (g0 + par + 2), (g0 + par) % 2)
                    if final:
                        for s_, (tt, par) in enumerate(PAIR):
                            step(KD - 2 + par, tt, s_ % 3, 3 * (KD - 2) + s_)
                        if layer == 0:
                            for par in range(2):
                                split_hi(g0 + KD + par, (g0 + par) % 2)

            def residual(n, h_next):
                if h_next is None:
                    for tt in range(NTT):
                        root(n, tt)
                    return
                for tt in range(2):
                    root(n, tt)
                    square(n + 1, tt)
                root(n + 1, 0)
                root(n, 2)
                if n == 1:
                    act.wait_ge(derived, 2)
                h_out(h_next, 0)
                square(n + 1, 2)
                root(n + 1, 1)
                h_out(h_next, 1)
                root(n + 1, 2)
                h_out(h_next, 2)

            out_tiles(0)
            residual(1, 1)
            ffn(0)
            residual(3, 2)
            g0, _, a0, _ = plan["qkv"]

            def qkv_step(hp, par, f, b):
                i, tt = f // 3, f % 3
                act.wait_ge(proj_done, hp * 9 + (3 * g0 + f + 1))
                A((q_c, k_c, v_c)[i][par][:, tt_cols(tt)], bank(b, TW), ACT.Copy, scale=QSCALE if i == 0 else 1.0).then_inc(evac_act, 1)
                if tt == NTT - 1:
                    split_hi(hp * 3 + (g0 + i + 2), (g0 + 3 * par + i) % 2)

            for s_, (tt, i) in enumerate(PAIR):
                act.wait_ge(proj_done, 3 * g0 + s_ + 1)
                A((q_c, k_c)[i][0][:, tt_cols(tt)], bank(s_ % 3, TW), ACT.Copy, scale=QSCALE if i == 0 else 1.0).then_inc(evac_act, 1)
            for i in range(2):
                split_hi(g0 + i + 2, (g0 + i) % 2)
            for f in range(6, 9):
                qkv_step(0, 0, f, f % 3)
            act.wait_ge(spilled, 64)

            def pair(hp, par, last):
                TD = lambda n: hp * 24 + (84 + n)

                def pre():
                    act.wait_ge(t_done, TD(1))
                    A(cache_kt[:, :], tps[:, 0:4, :].rearrange("p s c -> p (s c)"), ACT.Copy).then_inc(t_read, 1)
                    act.wait_ge(t_done, TD(2))
                    act.wait_ge(kv_stored, hp * 64 + 64)
                    A(v_tok[:, 0:5, :], tps[:, 0:5, :], ACT.Copy).then_inc(t_read, 1)
                    act.wait_ge(t_done, TD(3))
                    A(v_tok[:, 5:8, :], tps[:, 0:3, :], ACT.Copy)
                    A(v_tok[0:TS, 8, :], tps[0:TS, 3, :], ACT.Copy).then_inc(t_read, 1)
                    step(2)
                    act.wait_ge(t_done, TD(4))
                    A(k_out[:, 0:4, :], tps[:, 0:4, :], ACT.Copy)
                    A(k_out[0:TS, 4, :], tps[0:TS, 4, :], ACT.Copy).then_inc(t_read, 1)

                def fill(i):
                    if i % 3 == 2:
                        qkv_step(hp + 1, 1 - par, i // 3, 0)

                fill, step = (None, lambda i: None) if last else (fill, fill)
                attention("C", hp, False, fill, pre)

            with act.Fori(0, 3) as j:
                for par in range(2):
                    pair(j * 2 + par, par, False)
            pair(6, 0, False)
            pair(7, 1, True)
            out_tiles(1)
            residual(5, 3)
            ffn(1)
            residual(7, None)
            for b in range(NBLK + 1):
                m = qrows(b)
                act.wait_ge(yt_done, b + 1)
                if b >= 2:
                    act.wait_ge(y_st[b % 2], 16 * (b // 2))
                A(y_out[b % 2][0:m, :], psum[0:m, 2 * (b % 2):2 * (b % 2) + 2, :].rearrange("p b c -> p (b c)"), ACT.Copy).then_inc(yt_read, 1)

        @block.vector
        def _(dve):
            V = nc.vector
            for s in (ada_got, ol_done, w_done, og_done, ol9, conv_done, o_read):
                dve.sem_inc(s, 1)
            dve.sem_inc(ada_copied, 2)
            dve.sem_inc(acc_done, CREDIT)
            dve.sem_inc(evac_dve, CREDIT)
            dve.sem_inc(scores_read, CREDIT)

            def split_lo(g, slot):
                dve.wait_ge(hi_done, g + 1)
                V.tensor_tensor(w_lo[:, slot], w_raw[:, slot], w_hi[:, slot].bitcast(F32), ALU.subtract).then_inc(lo_done, 1)

            def split_next(g, slot):
                if isinstance(g, int) and g + 2 >= TILES:
                    return
                split_lo(g + 2, slot)

            dve.wait_ge(sink_ok, 16)
            V.tensor_scalar(neg_sink[:, :], neg_sink[:, :], -1.0, None, ALU.mult).then_inc(sink_neg, 1)
            dve.wait_ge(rev_ok, 16)
            pad = BW["C"] - 1 - MAX_REL
            V.tensor_scalar(rtable[:, 0:pad], table[:, 2 * MAX_REL:2 * MAX_REL + 1].to_broadcast([16, pad]), -1.0, None,
                            ALU.mult).then_inc(rev_built, 1)
            V.tensor_scalar(rtable[:, pad:REV], table[:, 2 * MAX_REL:2 * MAX_REL - (REV - pad):-1], -1.0, None,
                            ALU.mult).then_inc(rev_built, 1)
            for k in range(KD):
                for part in (1, 2):
                    dve.wait_ge(xt_done, 3 * k + part + 1)
                    n = 512 if part == 1 else TS
                    V.tensor_copy(x[:, k, 512 * part:512 * part + n], bank(part, n)).then_inc(xt_dve, 1)
            def ada_copy(q, m, b_):
                dve.wait_ge(ada_done, q * 4 + (4 + m + 1))
                V.tensor_copy(ada_row[:, m % 4, :], psum[0:2, b_, 0:256]).then_inc(ada_copied, 1)

            def ada_group(q, b_):
                dve.wait_ge(ada_t, q + 1)
                V.tensor_tensor(mod[:, one_of(q)].rearrange("p o k r -> p (o k) r"),
                                psum[:, b_, 0:16].rearrange("p (k r) -> p k r", r=2),
                                prm2[:, slice(8 * q, 8 * q + 8) if isinstance(q, int) else bass.ds(q * 8, 8)].unsqueeze(2).to_broadcast([128, KD, 2]),
                                ALU.add).then_inc(ada_got, 1)

            def derive(s):
                gb = lambda n: prm[:, 16 + 8 * n:24 + 8 * n].unsqueeze(2).to_broadcast([128, KD, 2])
                return (lambda: V.scalar_tensor_tensor(pre_scale[:, s], mod[:, 3 * s + 1], 1.0, gb(2 * s), ALU.add, ALU.mult),
                        lambda: V.tensor_tensor(post_gate[:, s], mod[:, 3 * s + 2], gb(2 * s + 1), ALU.mult))

            def mean_square(n, tt, b0=4):
                dve.wait_ge(ss_done, 3 * n + tt + 1)
                V.tensor_scalar(rstd[:, tt], bank(b0 + tt, TW), 1.0 / D, EPS, ALU.mult, ALU.add).then_inc(ms_done, 1)

            def rms(n, tt, src):
                dve.wait_ge(rt_done, 3 * n + tt + 1)
                V.reciprocal(rstd[:, tt], rstd[:, tt])
                dve.drain()
                return V.tensor_tensor(norm_buf[:, :, tt_cols(tt)], src[:, :, tt_cols(tt)],
                                       rstd[:, tt].unsqueeze(1).to_broadcast([128, KD, TW]), ALU.mult)

            def h_low(i, tt):
                dve.wait_ge(hh_done, 3 * i + tt + 1)
                V.tensor_tensor(h_lo[:, :, tt_cols(tt)], norm_buf[:, :, tt_cols(tt)], h_hi[:, :, tt_cols(tt)].bitcast(F32),
                                ALU.subtract).then_inc(hl_done, 1)

            for tt in range(NTT):
                mean_square(0, tt, 0)
            for m in range(4):
                ada_copy(0, m, 3 + m % 2)
            ada_group(0, 5)
            for tt in range(2):
                rms(0, tt, x).then_inc(xn_done, 1)
                for m in range(4 + 2 * tt, 6 + 2 * tt):
                    ada_copy(0, m, 3 + m % 2)
            ada_group(1, 5)
            dve.drain()
            derive(0)[0]().then_inc(derived, 1)
            rms(0, 2, x).then_inc(xn_done, 1)
            for g in range(2):
                split_lo(g, g)
            for tt in range(NTT):
                h_low(0, tt)

            def add_square(u, wait, i, tt):
                dve.wait_ge(*wait)
                V.tensor_tensor(sq_sum[:, tt_cols(tt)], sq_sum[:, tt_cols(tt)], sq_ring[i][:, :], ALU.add).then_inc(acc_done, 1)

            def residual(n, src, more):
                def add(tt, first=True):
                    if first:
                        mean_square(n, tt)
                    rms(n, tt, src)
                    dve.drain()
                    for k in range(KD):
                        for a, b, r in groups(tt):
                            c = slice(tt * TW + a, tt * TW + b)
                            last = V.scalar_tensor_tensor(x[:, k, c], norm_buf[:, k, c], post_gate[:, n // 2, k, r:r + 1],
                                                          x[:, k, c], ALU.mult, ALU.add)
                    last.then_inc(x_new, 1)

                i = (n + 1) // 2
                add(0)
                add(1)
                if not more:
                    add(2)
                    return
                mean_square(n + 1, 0)
                mean_square(n, 2)
                rms(n + 1, 0, x).then_inc(xn_done, 1)
                add(2, False)
                mean_square(n + 1, 1)
                h_low(i, 0)
                rms(n + 1, 1, x).then_inc(xn_done, 1)
                mean_square(n + 1, 2)
                h_low(i, 1)
                rms(n + 1, 2, x).then_inc(xn_done, 1)
                h_low(i, 2)

            def attention(kind, it, sinks, fill):
                c = KINDS[kind]
                N = lambda n: it * 18 + (c["n0"] + n)
                lag, sb, probs = c["lag"], c["score_bufs"], c["probs"]
                f0 = c["fill0"]
                for i in range(20 + lag):
                    if i >= lag + 2:
                        n = i - lag - 2
                        e, p = n // 9, n % 9
                        m = qrows(p)
                        s6 = slice(n % 6, n % 6 + 1)
                        dve.wait_ge(o_done, N(n) + 1)
                        src = sums
                        if sinks:
                            V.tensor_tensor(rsum[0:m, s6], sums[0:m, s6], sink_e[0:m, s6], ALU.add)
                            dve.drain()
                            src = rsum
                        V.reciprocal(rsum[0:m, s6], src[0:m, s6])
                        dve.drain()
                        V.tensor_scalar(o_tok[0:m, p, 64 * e:64 * e + 64], oacc[0:m, 0:64], rsum[0:m, s6], None,
                                        ALU.mult).then_inc(o_read, 1)
                    if i < 18:
                        n, e, p = i, i // 9, i % 9
                        m, (w, c0) = qrows(p), score_width(kind, p)
                        if p == 0:
                            if kind == "A":
                                dve.wait_ge(bias_raw[e], it * 16 + 16)
                            else:
                                dve.wait_ge(bias_ok[e], it + 1)
                        dve.wait_ge(scores, N(n) + 1)
                        b_ = score_bank(kind, n)
                        sc = psum[0:m, b_:b_ + 2, :].rearrange("p b c -> p (b c)")[:, 0:w]
                        mn = mins[0:m, n % 6:n % 6 + 1]
                        apart(dve)
                        op = V.tensor_tensor_reduce(out=probs[0:m, n % sb, 0:w], in0=sc, in1=neg_bias[0:m, e, c0:c0 + w],
                                                    scale=1.0, scalar=3.0e38, op0=ALU.add, op1=ALU.min, accum_out=mn)
                        if sinks:
                            dve.drain()
                            op = V.tensor_tensor(mn, mn, sink2[0:m, e:e + 1], ALU.min)
                        op.then_inc(scores_read, 1)
                    if fill and i < 19 + lag:
                        fill(i + f0)
                for r in range(2):
                    dve.wait_ge(oh_done, it * 2 + (c["o0"] + r + 1))
                    c0, w = (0, 640) if r == 0 else (640, T - 640)
                    sel = bass.ds(it, 1) if not isinstance(it, int) else slice(it, it + 1)
                    src = psum[:, 5:7, :].rearrange("p b c -> p (b c)")[:, 0:w].unsqueeze(1)
                    V.tensor_tensor(o_lo[:, sel, c0:c0 + w], src, o_hi[:, sel, c0:c0 + w].bitcast(F32), ALU.subtract
                                    ).then_inc(ol_done, 1)
                    if fill:
                        fill(19 + lag + f0 + r)

            for i in range(2):
                split_next(i, i)
            dve.wait_ge(spilled, 16)
            with dve.Fori(0, 2) as j:
                for par in range(2):
                    t = j * 2 + par
                    V.tensor_copy(sink2[:, :].unsqueeze(2), neg_sink[:, :].rearrange("p (e t) -> p e t", e=2)[:, :, bass.ds(t, 1)])
                    split_lo(t + (plan["qa"][0] + 2), (plan["qa"][0] + par) % 2)
                    dve.drain()

                    def fill(i):
                        v = 20 * par + i
                        if i < 20 and v % 2 == 1:
                            ada_copy(j * 5, 8 + v // 2, 0)
                        if i <= 20 and v in (8, 16, 24, 32) or v == 40:
                            ada_group(j * 5 + (2 + v // 8 - 1), 4)

                    attention("A", t, True, fill)
            dve.drain()
            for s in range(4):
                if s:
                    derive(s)[0]()
                last = derive(s)[1]()
            last.then_inc(derived, 1)
            V.memset(h_tok[:, :, :], 0.0)
            V.memset(ssq[:, :], 0.0)
            for i in range(2):
                V.memset(u_in[i][:, 0:3], 0.0)
            dve.drain()
            split_next(plan["gates"][0], plan["gates"][0] % 2)
            V.memset(row["carry"][:, :], 1.0)
            dve.drain()
            V.memset(row["carry"][:, 0:T:128], 0.0)
            dve.wait_ge(gate_e, 1)
            V.scalar_tensor_tensor(row["logf"][:, :], row["fg"][:, :], 0.0, row["t"][:, :], ALU.min, ALU.subtract)
            dve.drain()
            V.tensor_tensor_scan(row["b"][:, :], row["carry"][:, :], row["logf"][:, :], 0.0, ALU.mult, ALU.add)
            V.tensor_tensor_scan(row["m"][:, 0:TP], row["logf"][:, 0:TP], row["logi"][:, 0:TP], 0.0, ALU.add, ALU.max)
            V.tensor_tensor_scan(row["m"][:, TP:T], row["logf"][:, TP:T], row["logi"][:, TP:T], m_in[:, :], ALU.add, ALU.max)
            V.memset(m_prev[:, 0:1], 0.0)
            dve.drain()
            V.tensor_copy(m_prev[:, 1:NBLK], row["m"][:, 127:TP - 1:128])
            V.tensor_copy(m_prev[:, NBLK:NBLK + 1], m_in[:, :])
            V.tensor_tensor(row["g"][:, :], row["logi"][:, :], row["b"][:, :], ALU.subtract)
            V.tensor_tensor(brd[:, 0:T], row["b"][:, :], row["m"][:, :], ALU.subtract)
            dve.drain()
            V.tensor_copy(nm_end[:, 0:NBLK], brd[:, 127:TP:128])
            V.tensor_copy(nm_end[:, NBLK:NBLK + 1], brd[:, T - 1:T])
            dve.drain()
            V.tensor_tensor(brd[:, 2 * T:SELW], m_prev[:, :], nm_end[:, :], ALU.add)
            for dst, src, per in ((brd[:, T:2 * T], brd[:, 0:T], m_prev), (row["wend"][:, :], row["g"][:, :], nm_end)):
                V.tensor_tensor(dst[:, 0:TP].rearrange("p (b c) -> p b c", c=128), src[:, 0:TP].rearrange("p (b c) -> p b c", c=128),
                                per[:, 0:NBLK].unsqueeze(2).to_broadcast([4, NBLK, 128]), ALU.add)
                last = V.tensor_scalar(dst[:, TP:T], src[:, TP:T], per[:, NBLK:NBLK + 1], None, ALU.add)
            last.then_inc(gate_rows, 1)
            def head_constants(hd):
                hs = one_of(hd)
                dve.wait_ge(hT_done, one(hd * 3))
                dve.wait_ge(state_free, hd + 1)
                V.tensor_copy(onehot[:, :], ident[0:4, hs])
                cw = prm[:, 80:120].rearrange("p (j i h) -> p j i h", i=2, h=H_B)
                V.tensor_copy(conv_h[:, :, :].unsqueeze(3), cw[:, :, :, hs])
                V.tensor_copy(hnorm_h[:, :], prm[:, one_of(hd, 120)])
                cs_in = prm2[:, 96:120].rearrange("p (j i h) -> p i j h", i=2, h=H_B)
                for i in range(2):
                    V.tensor_copy(u_in[i][:, TP + 3:TP + 6].unsqueeze(2), cs_in[:, i, :, hs])
                dve.drain()

            def head_state(hd):
                hs = one_of(hd)
                V.tensor_copy(cols_h[:, :, :].unsqueeze(3), cols[:, :, :, hs])
                V.memset(mem[0][:, 0:129], 0.0).then_inc(mem_done, 1)
                V.tensor_copy(mem[1][:, 0:128].unsqueeze(1), mem_in[:, hs, :])
                V.tensor_copy(mem[1][:, 128:129], prm[:, one_of(hd, 124)]).then_inc(mem_done, 1)
                dve.drain()
                V.tensor_scalar(nm_h[:, :], brd[:, 0:T], onehot[:, :], None, ALU.mult)
                V.tensor_scalar(a_h[:, :], brd[:, T:2 * T], onehot[:, :], None, ALU.mult)
                V.tensor_scalar(ae_h[:, :], brd[:, 2 * T:SELW], onehot[:, :], None, ALU.mult).then_inc(head_set, 1)

            def head_conv(hd):
                g0, _, a0, _ = plan["heads"]
                for i in range(4):
                    if i < 2:
                        dve.wait_ge(evac_act, hd * 12 + (CREDIT + a0 + 3 * (i + 1)))
                        dve.wait_ge(conv_in, one(hd * 2 + i))
                        V.tensor_scalar(conv_t[:, :], u_in[i][:, 0:CW], conv_h[:, 0, i:i + 1], None, ALU.mult)
                        for jj in range(1, CONV_W):
                            dve.drain()
                            last = V.scalar_tensor_tensor(conv_t[:, :], u_in[i][:, jj:jj + CW], conv_h[:, jj, i:i + 1], conv_t[:, :],
                                                          ALU.mult, ALU.add)
                        last.then_inc(conv_done, 1)
                    split_lo(hd * 4 + (g0 + i + 2), (g0 + i) % 2)

            def head(hd):
                dve.wait_ge(conv_in, one(hd * 2 + 1))
                for tt in range(NTT):
                    dve.wait_ge(abc_done, hd * 4 + (tt + 1))
                    V.tensor_tensor(qa_b[:, tt_cols(tt)], qk_b[0][:, tt_cols(tt)], bank(tt, TW), ALU.mult).then_inc(qa_done, 1)
                dve.wait_ge(abc_done, hd * 4 + 4)
                V.tensor_copy(aend_h[:, :], bank(3, NBLK + 1)).then_inc(qa_done, 1)
                dve.drain()

                def weights(c):
                    m = qrows(c)
                    dve.wait_ge(st_done, hd * 9 + (c + 1))
                    dve.wait_ge(decay_done, one(hd * 9 + (c + 1)))
                    V.scalar_tensor_tensor(wts[0:m, c % 2, 0:m], psum[0:m, 4, 0:m], KSCALE, decay[0:m, c % 2, 0:m],
                                           ALU.mult, ALU.mult).then_inc(w_done, 1)

                def finish(c):
                    m = qrows(c)
                    dve.wait_ge(num_done, hd * 9 + (c + 1))
                    mm = mem[c // NBLK]
                    dve.wait_ge(upd_done, hd * 9 + (c + 1))
                    V.scalar_tensor_tensor(mm[:, 0:129], mm[:, 0:129], aend_h[:, c:c + 1], psum[:, 3, 0:129],
                                           ALU.mult, ALU.add).then_inc(mem_done, 1)
                    d_, nb = den[0:m, c % 2:c % 2 + 1], num_bank(c)
                    V.tensor_scalar(d_, psum[0:m, nb, 128:129], cols_h[0:m, c, 2:3], None, ALU.max)
                    dve.drain()
                    V.scalar_tensor_tensor(d_, psum[0:m, nb, 128:129], -1.0, d_, ALU.mult, ALU.max)
                    dve.drain()
                    V.reciprocal(rden[0:m, c % 2:c % 2 + 1], d_).then_inc(den_done, 1)

                weights(0)
                for c in range(NBLK + 1):
                    if c < NBLK:
                        weights(c + 1)
                    finish(c)
                dve.drain()
                for i in range(2):
                    last = V.tensor_copy(mem_out[:, i, 128:129], mem[i][:, 128:129])
                last.then_inc(n_copied, 1)
                dve.wait_ge(num_read, one(hd * 9 + 9))
                V.tensor_scalar(rs9[:, :], ssq[:, :], 1.0 / DH_B, EPS, ALU.mult, ALU.add).then_inc(ms9, 1)
                dve.wait_ge(rt9, hd + 1)
                V.reciprocal(rs9[:, :], rs9[:, :])
                dve.drain()
                V.tensor_tensor(h_tok[:, :, :], h_tok[:, :, :], rs9[:, :].unsqueeze(2).to_broadcast([128, NBLK + 1, 128]),
                                ALU.mult).then_inc(hn_done, 1)
                for r, (c0, w, b_) in enumerate(((0, 512, 4), (512, 512, 5), (TP, TS, 3))):
                    dve.wait_ge(hT_done, one(hd * 3 + (r + 1)))
                    last = V.scalar_tensor_tensor(ot_f[:, c0:c0 + w], psum[:, b_, 0:w], hnorm_h[:, :], og_b[:, c0:c0 + w],
                                                  ALU.mult, ALU.mult)
                last.then_inc(og_done, 1)
                dve.wait_ge(oh9, hd + 1)
                V.tensor_tensor(o_lo[:, one_of(hd, 4), :], ot_f[:, 0:T].unsqueeze(1), o_hi[:, one_of(hd, 4), :].bitcast(F32),
                                ALU.subtract).then_inc(ol9, 1)

            head_constants(0)
            head_conv(0)
            V.memset(cols[:, :, :, :], 0.0)
            dve.drain()
            dve.wait_ge(cols_t, 1)
            for b0, b1, m in ((0, NBLK, 128), (NBLK, NBLK + 1, TS)):
                src = psum[0:m, 5, 12 * b0:12 * b1].rearrange("p (b i h) -> p b i h", i=3, h=H_B)
                for i in range(3):
                    last = V.tensor_scalar(cols[0:m, b0:b1, i, :], src[:, :, i, :], KSCALE if i == 1 else 1.0, None, ALU.mult)
            last.then_inc(cols_ok, 1)
            dve.wait_ge(cols_t, 2)
            V.tensor_copy(mem_in[:, :, :].rearrange("p h k -> p (h k)"), bank(6)).then_inc(cols_ok, 1)
            dve.wait_ge(stored, 32)
            dve.wait_ge(gate_rows, 2)
            V.memset(v_x[:, :, 128:129], 1.0)
            dve.drain()
            head_state(0)
            head(0)
            with dve.Fori(1, H_B) as hd:
                head_constants(hd)
                head_state(hd)
                head_conv(hd)
                head(hd)

            def out_tiles(layer):
                g0, _, a0, _ = plan[f"out{layer}"]
                dve.drain()
                V.memset(sq_sum[:, :], 0.0)
                dve.drain()
                add = lambda u, i, tt: add_square(u, (evac_act, u + (a0 + CREDIT + 1)), i, tt)
                with dve.Fori(0, KD // 2 - 1) as j:
                    for par in range(2):
                        for tt in range(NTT):
                            add(j * 6 + (3 * par + tt), tt, tt)
                        split_lo(j * 2 + (g0 + par + 2), (g0 + par) % 2)
                for s_, (tt, par) in enumerate(PAIR):
                    add(3 * (KD - 2) + s_, s_ % 3, tt)
                    dve.drain()

            def ffn(layer):
                for n, ff in enumerate(FF_GROUPS):
                    g0, _, a0, d0 = plan[f"gu{layer}{n}"]
                    nff = 3 * (sum(FF_GROUPS) * layer + sum(FF_GROUPS[:n]))
                    if n == 0:
                        for tt in range(NTT):
                            dve.wait_ge(proj_done, 3 * g0 + 2 * tt + 2)
                            dve.wait_ge(evac_act, a0 + CREDIT + tt + 1)
                            V.tensor_tensor(ffs[:, tt_cols(tt)], sil[:, tt_cols(tt)], bank(3 + tt, TW), ALU.mult).then_inc(evac_dve, 1)
                        for tt in range(NTT):
                            dve.wait_ge(ffhi_done, nff + tt + 1)
                            V.tensor_tensor(ff_lo[:, 0, tt_cols(tt)], ffs[:, tt_cols(tt)], ff_hi[:, 0, tt_cols(tt)].bitcast(F32),
                                            ALU.subtract).then_inc(fflo_done, 1)
                        for i in range(2):
                            split_lo(g0 + 2 + i, (g0 + i) % 2)
                    with dve.Fori(1 if n == 0 else 0, ff) as f:
                        split_lo(f * 2 + (g0 + 2), g0 % 2)
                        for i in range(NTT + 1):
                            if i < NTT:
                                dve.wait_ge(proj_done, f * 6 + (3 * g0 + 3 + i + 1))
                                dve.wait_ge(evac_act, f * 3 + (a0 + CREDIT + i + 1))
                                V.tensor_tensor(ffs[:, tt_cols(i)], sil[:, tt_cols(i)], bank(i, TW), ALU.mult).then_inc(evac_dve, 1)
                            if i == 0:
                                continue
                            tt = i - 1
                            dve.wait_ge(ffhi_done, f * 3 + (nff + tt + 1))
                            sel = bass.ds(f, 1)
                            V.tensor_tensor(ff_lo[:, sel, tt_cols(tt)], ffs[:, tt_cols(tt)].unsqueeze(1), ff_hi[:, sel, tt_cols(tt)].bitcast(F32),
                                            ALU.subtract).then_inc(fflo_done, 1)
                        split_lo(f * 2 + (g0 + 3), (g0 + 1) % 2)
                    g0 = plan[f"down{layer}{n}"][0]
                    final = n == len(FF_GROUPS) - 1

                    def down(tile, tt, b_, u):
                        dve.wait_ge(proj_done, u + (3 * g0 + 1))
                        dst = y_ffn[:, bass.ds(tile, 1) if not isinstance(tile, int) else slice(tile, tile + 1), tt_cols(tt)]
                        src = bank(b_, TW).unsqueeze(1)
                        if n == 0:
                            V.tensor_copy(dst, src).then_inc(evac_dve, 1)
                        else:
                            V.tensor_tensor(dst, dst, src, ALU.add).then_inc(evac_dve, 1)

                    add = lambda u, i, tt: add_square(u, (sqy_done, u + (24 * layer + 1)), i, tt)
                    if final:
                        dve.drain()
                        V.memset(sq_sum[:, :], 0.0)
                        dve.drain()
                    with dve.Fori(0, KD // 2 - final) as j:
                        for par in range(2):
                            for tt in range(NTT):
                                down(j * 2 + par, tt, tt, j * 6 + (3 * par + tt))
                            if final:
                                for tt in range(NTT):
                                    add(j * 6 + (3 * par + tt), tt, tt)
                            split_lo(j * 2 + (g0 + par + 2), (g0 + par) % 2)
                    if final:
                        for s_, (tt, par) in enumerate(PAIR):
                            u = 3 * (KD - 2) + s_
                            down(KD - 2 + par, tt, s_ % 3, u)
                            if par == 1:
                                add(u - 1, (s_ - 1) % 3, tt)
                                dve.drain()
                                add(u, s_ % 3, tt)

            def split_two(g0):
                for i in range(2):
                    split_lo(g0 + i, (g0 + i) % 2)

            out_tiles(0)
            split_two(plan["gu00"][0])
            dve.wait_ge(x_loaded, 16)
            residual(1, y_mix, True)
            ffn(0)
            split_two(plan["qkv"][0])
            residual(3, y_ffn, True)
            g0 = plan["qkv"][0]
            for i in range(3):
                split_lo(g0 + i + 2, (g0 + i) % 2)
            dve.wait_ge(spilled, 64)

            def pair(hp, par, last):
                def fill(i):
                    f = i // 3
                    if i % 9 == 8:
                        split_lo(hp * 3 + (3 + g0 + f // 3 + 2), (g0 + 3 * (1 - par) + f // 3) % 2)
                attention("C", hp, False, None if last else fill)

            with dve.Fori(0, 3) as j:
                for par in range(2):
                    pair(j * 2 + par, par, False)
            pair(6, 0, False)
            pair(7, 1, True)
            out_tiles(1)
            split_two(plan["gu10"][0])
            dve.wait_ge(x_loaded, 32)
            residual(5, y_mix, True)
            ffn(1)
            residual(7, y_ffn, False)


_OUTS = [
    ("y_prompt", (1, TP, D)), ("y_sample", (1, TS, D)),
    ("pa_k", (1, 1, 128, 2, 64)), ("pa_v", (1, 1, 128, 2, 64)), ("pb_c", (1, 1, 4, 128, 128)), ("pb_n", (1, 1, 4, 128)),
    ("pb_m", (1, 1, 4)), ("pb_conv", (1, 1, 3, 1024)), ("pc_k", (1, 1, 512, 16, 64)), ("pc_v", (1, 1, 512, 16, 64)),
    ("sa_k", (1, 1, 32, 2, 64)), ("sa_v", (1, 1, 32, 2, 64)), ("sb_c", (1, 1, 4, 128, 128)), ("sb_n", (1, 1, 4, 128)),
    ("sb_m", (1, 1, 4)), ("sb_conv", (1, 1, 3, 1024)), ("sc_k", (1, 1, 32, 16, 64)), ("sc_v", (1, 1, 32, 16, 64)),
]


def constants():
    s, t = np.arange(128)[:, None], np.arange(128)[None, :]
    causal = np.where(s <= t, 0.0, -BIG).astype(np.float32)
    i, j = np.arange(128)[:, None], np.arange(256)[None, :]
    seen = np.where(i < 64, j < 192, j >= 64)
    slope = np.exp2(-8.0 * np.arange(1, HQ_A + 1) / HQ_A)[:, None, None]
    alibi = np.where(seen, slope * np.abs(128 + i - j), BIG).astype(np.float32)
    return dict(ident=np.eye(128, dtype=np.float32), causal=causal, alibi=alibi)


def kernel(**inputs):
    import concourse.bacc as bacc
    from concourse.bass_utils import run_bass_kernel_spmd

    nc = bacc.Bacc("TRN2", target_bir_lowering=False, num_devices=1, dynamic_dma_scratch_size=DMA_RING)
    arrays, ins, outs = {}, {}, {}
    for name, a in {**inputs, **constants()}.items():
        a = np.ascontiguousarray(a)
        arrays[f"in_{name}"] = a
        ins[name] = nc.dram_tensor(f"in_{name}", a.shape, mybir.dt.from_np(a.dtype), kind="ExternalInput").ap()
    for name, shape in _OUTS:
        outs[name] = nc.dram_tensor(f"out_{name}", shape, F32, kind="ExternalOutput").ap()
    build(nc, ins, outs)
    r = run_bass_kernel_spmd(nc, [arrays], core_ids=[0])
    return tuple(r.results[0][f"out_{name}"] for name, _ in _OUTS)
```
